# Optimizing a Trainium2 kernel written in Bass

```python
import math
import jax, jax.numpy as jnp
from jax import lax
import numpy as np

D_MODEL = 1024
BATCH = 1
SEQ = 128
DEPTH = 2
DEC_BATCH = 1
DEC_SEQ = 256
PAST_LEN = 128

GRID_W = 64
HEAD_DIM = 64
D_RWKV = 384
H_RWKV = D_RWKV // HEAD_DIM
D_DIFF = 384
H_DIFF = D_DIFF // HEAD_DIM
D_QK = HEAD_DIM // 2
D_FNET = D_MODEL - D_RWKV - D_DIFF
FNET_GROUPS = 4
FNET_GROUP_DIM = D_FNET // FNET_GROUPS
LORA_W = 32
LORA_A = 32
LORA_G = 64
N_RWKV_IN = 3 * D_RWKV + 2 * LORA_W + 2 * LORA_A + LORA_G
N_DIFF_IN = 3 * D_DIFF
D_IN = N_RWKV_IN + N_DIFF_IN + D_FNET
RWKV_SPLITS = (D_RWKV, 2 * D_RWKV, 3 * D_RWKV, 3 * D_RWKV + 2 * LORA_W, 3 * D_RWKV + 2 * LORA_W + 2 * LORA_A)
D_FF = ((8 * D_MODEL + 3 * 256 - 1) // (3 * 256)) * 256
ROPE_PAIRS = D_QK // 4
ROPE_BASE = 10000.0
Q_BLOCK = 128
RMS_EPS = 1e-6
GN_EPS = 64e-5
SUBLN_EPS = 1e-5
DECAY_SCALE = math.exp(-0.5)

kernel_name = 'hybrid_rwkv7_diffattn_fnet_dit_step'

F32 = jnp.float32

def rmsnorm(x, g, eps=RMS_EPS):
    xf = x.astype(F32)
    y = xf * lax.rsqrt(jnp.mean(xf * xf, axis=-1, keepdims=True) + eps)
    return (y * g.astype(F32)).astype(x.dtype)

def modulation(cond, w_mod, b_mod):
    m = jax.nn.silu(cond) @ w_mod + b_mod
    return jnp.split(m[:, None, :], 6, axis=-1)

def token_shift(x, mu):
    prev = jnp.pad(x[:, :-1], ((0, 0), (1, 0), (0, 0)))
    nxt = jnp.pad(x[:, 1:], ((0, 0), (0, 1), (0, 0)))
    return x + mu[0] * (prev - x) + mu[1] * (nxt - x)

def wkv_scan(s0, r, w, k, v, kk, a, reverse):
    def step(S, inp):
        r_t, w_t, k_t, v_t, kk_t, a_t = inp
        sa = jnp.einsum('bhvk,bhk->bhv', S, -kk_t)
        S = S * w_t[:, :, None, :] + sa[..., None] * (kk_t * a_t)[:, :, None, :] + v_t[..., None] * k_t[:, :, None, :]
        return S, jnp.einsum('bhvk,bhk->bhv', S, r_t)
    xs = tuple(jnp.moveaxis(t, 1, 0) for t in (r, w, k, v, kk, a))
    S, ys = lax.scan(step, s0, xs, reverse=reverse)
    return S, jnp.moveaxis(ys, 0, 1)

def rwkv_time_mix(u, s0, p, l):
    B, T, _ = u.shape
    u = token_shift(u.astype(F32), p['shift_mu'][l])
    r, k, v, wd, ad, gd = jnp.split(u, RWKV_SPLITS, axis=-1)
    wd = wd.reshape(B, T, 2, LORA_W)
    ad = ad.reshape(B, T, 2, LORA_A)
    w = jnp.exp(-DECAY_SCALE * jax.nn.sigmoid(p['decay_w0'][l] + jnp.einsum('btdr,drc->btdc', jnp.tanh(wd), p['decay_up'][l])))
    a = jax.nn.sigmoid(p['iclr_a0'][l] + jnp.einsum('btdr,drc->btdc', ad, p['iclr_up'][l]))
    g = jax.nn.sigmoid(gd) @ p['gate_up'][l]
    heads = lambda t: t.reshape(B, T, H_RWKV, HEAD_DIM)
    kk = heads(k * p['k_k'][l])
    kk = kk / jnp.maximum(jnp.sqrt(jnp.sum(kk * kk, axis=-1, keepdims=True)), 1e-12)
    k_dir = k[:, :, None, :] * (1.0 + (a - 1.0) * p['k_a'][l])
    rh, vh = heads(r), heads(v)
    k_f, k_b = heads(k_dir[:, :, 0]), heads(k_dir[:, :, 1])
    S_f, y_f = wkv_scan(s0[:, 0], rh, heads(w[:, :, 0]), k_f, vh, kk, heads(a[:, :, 0]), False)
    S_b, y_b = wkv_scan(s0[:, 1], rh, heads(w[:, :, 1]), k_b, vh, kk, heads(a[:, :, 1]), True)
    y = y_f + y_b
    mu = jnp.mean(y, axis=-1, keepdims=True)
    var = jnp.mean(jnp.square(y - mu), axis=-1, keepdims=True)
    y = ((y - mu) * lax.rsqrt(var + GN_EPS)).reshape(B, T, D_RWKV) * p['lnx_g'][l] + p['lnx_b'][l]
    bonus = jnp.sum(rh * (k_f + k_b) * p['r_k'][l], axis=-1, keepdims=True) * vh
    out = (y + bonus.reshape(B, T, D_RWKV)) * g
    return out, jnp.stack([S_f, S_b], axis=1)

def axial_rope(T):
    rows = T // GRID_W
    row = jnp.repeat(jnp.arange(rows), GRID_W).astype(F32)
    col = jnp.tile(jnp.arange(GRID_W), rows).astype(F32)
    inv = 1.0 / (ROPE_BASE ** (jnp.arange(ROPE_PAIRS, dtype=F32) / ROPE_PAIRS))
    ang = jnp.stack([row[:, None] * inv, col[:, None] * inv], axis=1)
    return jnp.cos(ang), jnp.sin(ang)

def apply_rope(x, cos, sin):
    xs = x.astype(F32).reshape(*x.shape[:-1], 2, 2, ROPE_PAIRS)
    x1, x2 = xs[..., 0, :], xs[..., 1, :]
    c, s = cos[:, None, None], sin[:, None, None]
    out = jnp.stack([x1 * c - x2 * s, x2 * c + x1 * s], axis=-2)
    return out.reshape(x.shape).astype(x.dtype)

def diff_attention(q, k, v, lam_params, lam_init, subln_g):
    B, Tq, H = q.shape[:3]
    lp = lam_params.astype(F32)
    lam = jnp.exp(jnp.sum(lp[0] * lp[1])) - jnp.exp(jnp.sum(lp[2] * lp[3])) + lam_init
    kf, vf = k.astype(F32), v.astype(F32)
    qb = jnp.moveaxis((q.astype(F32) * D_QK ** -0.5).reshape(B, Tq // Q_BLOCK, Q_BLOCK, H, 2, D_QK), 1, 0)

    def block(q_blk):
        pr = jax.nn.softmax(jnp.einsum('bqhmd,bkhmd->bhmqk', q_blk, kf), axis=-1)
        return jnp.einsum('bhqk,bkhd->bqhd', pr[:, :, 0] - lam * pr[:, :, 1], vf)

    o = jnp.moveaxis(lax.map(block, qb), 0, 1).reshape(B, Tq, H, HEAD_DIM)
    o = o * lax.rsqrt(jnp.mean(o * o, axis=-1, keepdims=True) + SUBLN_EPS) * subln_g * (1.0 - lam_init)
    return o.reshape(B, Tq, H * HEAD_DIM)

def fourier_mix(u):
    B, T, _ = u.shape
    f = jnp.fft.fft2(u.astype(F32).reshape(B, T, FNET_GROUPS, FNET_GROUP_DIM), axes=(1, 3), norm='ortho').real
    return f.reshape(B, T, D_FNET)

def mixer_sublayer(h, p, l, s0, ctx_k, ctx_v, rope):
    B, T, _ = h.shape
    u_rwkv, u_diff, u_fnet = jnp.split(h @ p['w_in'][l], [N_RWKV_IN, N_RWKV_IN + N_DIFF_IN], axis=-1)
    y_rwkv, s_new = rwkv_time_mix(u_rwkv, s0, p, l)
    q, k, v = jnp.split(u_diff, 3, axis=-1)
    q = q.reshape(B, T, H_DIFF, 2, D_QK)
    k = k.reshape(B, T, H_DIFF, 2, D_QK)
    v = v.reshape(B, T, H_DIFF, HEAD_DIM)
    if rope is None:
        keys, vals = k, v
    else:
        q = apply_rope(q, *rope)
        k = apply_rope(k, *rope)
        keys = jnp.concatenate([ctx_k.astype(k.dtype), k], axis=1)
        vals = jnp.concatenate([ctx_v.astype(v.dtype), v], axis=1)
    lam_init = 0.8 - 0.6 * math.exp(-0.3 * l)
    y_diff = diff_attention(q, keys, vals, p['diff_lambda'][l], lam_init, p['subln_g'][l])
    y_fnet = fourier_mix(u_fnet)
    y = jnp.concatenate([y_rwkv, y_diff, y_fnet], axis=-1).astype(h.dtype) @ p['w_out'][l]
    return y, s_new, k, v

def swiglu(h, w_in, w_out):
    gt, up = jnp.split(h @ w_in, 2, axis=-1)
    return (jax.nn.silu(gt) * up) @ w_out

def trunk_layer(x, cond, p, l, s0, ctx_k, ctx_v, rope):
    sh1, sc1, g1, sh2, sc2, g2 = modulation(cond, p['w_mod'][l], p['b_mod'][l])
    h = rmsnorm(x, p['norm1_g'][l]) * (1 + sc1) + sh1
    y, s_new, k, v = mixer_sublayer(h, p, l, s0, ctx_k, ctx_v, rope)
    x = x + g1 * y
    h = rmsnorm(x, p['norm2_g'][l]) * (1 + sc2) + sh2
    x = x + g2 * swiglu(h, p['w_ffn_in'][l], p['w_ffn_out'][l])
    return x, s_new, k, v

def setup_inputs(seed: int = 0) -> dict:
    key = jax.random.key(seed)
    ks = iter(jax.random.split(key, 40))
    nrm = lambda shape, s: jax.random.normal(next(ks), shape, F32) * s
    L = DEPTH
    return {
        'x_prompt': nrm((BATCH, SEQ, D_MODEL), 1.0),
        'x_sample': nrm((DEC_BATCH, DEC_SEQ, D_MODEL), 1.0),
        'c': nrm((DEC_BATCH, D_MODEL), 1.0),
        'state_rwkv': nrm((DEC_BATCH, L, 2, H_RWKV, HEAD_DIM, HEAD_DIM), 0.5),
        'cache_diff_k': nrm((DEC_BATCH, L, PAST_LEN, H_DIFF, 2, D_QK), 1.0),
        'cache_diff_v': nrm((DEC_BATCH, L, PAST_LEN, H_DIFF, HEAD_DIM), 1.0),
        'c_ctx': nrm((D_MODEL,), 1.0),
        'norm1_g': 1.0 + nrm((L, D_MODEL), 0.02),
        'norm2_g': 1.0 + nrm((L, D_MODEL), 0.02),
        'final_norm_g': 1.0 + nrm((D_MODEL,), 0.02),
        'w_mod': nrm((L, D_MODEL, 6 * D_MODEL), 0.5 * D_MODEL ** -0.5),
        'b_mod': nrm((L, 6 * D_MODEL), 0.02),
        'w_in': nrm((L, D_MODEL, D_IN), D_MODEL ** -0.5),
        'w_out': nrm((L, D_MODEL, D_MODEL), D_MODEL ** -0.5),
        'shift_mu': jax.random.uniform(next(ks), (L, 2, N_RWKV_IN), F32, 0.0, 0.4),
        'decay_w0': nrm((L, 2, D_RWKV), 1.0),
        'decay_up': nrm((L, 2, LORA_W, D_RWKV), 0.1 * LORA_W ** -0.5),
        'iclr_a0': nrm((L, 2, D_RWKV), 0.5),
        'iclr_up': nrm((L, 2, LORA_A, D_RWKV), 0.1 * LORA_A ** -0.5),
        'gate_up': nrm((L, LORA_G, D_RWKV), LORA_G ** -0.5),
        'k_k': 1.0 + nrm((L, D_RWKV), 0.1),
        'k_a': 1.0 + nrm((L, D_RWKV), 0.1),
        'r_k': nrm((L, H_RWKV, HEAD_DIM), 0.1),
        'lnx_g': 1.0 + nrm((L, D_RWKV), 0.02),
        'lnx_b': nrm((L, D_RWKV), 0.02),
        'diff_lambda': nrm((L, 4, D_QK), 0.1),
        'subln_g': 1.0 + nrm((L, HEAD_DIM), 0.02),
        'w_ffn_in': nrm((L, D_MODEL, 2 * D_FF), D_MODEL ** -0.5),
        'w_ffn_out': nrm((L, D_FF, D_MODEL), D_FF ** -0.5),
    }

def reference(x_prompt, x_sample, c, state_rwkv, cache_diff_k, cache_diff_v, c_ctx, norm1_g, norm2_g, final_norm_g,
              w_mod, b_mod, w_in, w_out, shift_mu, decay_w0, decay_up, iclr_a0, iclr_up, gate_up, k_k, k_a, r_k,
              lnx_g, lnx_b, diff_lambda, subln_g, w_ffn_in, w_ffn_out):
    p = dict(norm1_g=norm1_g, norm2_g=norm2_g, w_mod=w_mod, b_mod=b_mod, w_in=w_in, w_out=w_out,
             shift_mu=shift_mu, decay_w0=decay_w0, decay_up=decay_up, iclr_a0=iclr_a0, iclr_up=iclr_up,
             gate_up=gate_up, k_k=k_k, k_a=k_a, r_k=r_k, lnx_g=lnx_g, lnx_b=lnx_b, diff_lambda=diff_lambda,
             subln_g=subln_g, w_ffn_in=w_ffn_in, w_ffn_out=w_ffn_out)

    xp = x_prompt
    s_zero = jnp.zeros((x_prompt.shape[0], 2, H_RWKV, HEAD_DIM, HEAD_DIM), F32)
    states, ks, vs = [], [], []
    for l in range(DEPTH):
        xp, s_new, k, v = trunk_layer(xp, c_ctx[None, :], p, l, s_zero, None, None, None)
        states.append(s_new)
        ks.append(k)
        vs.append(v)
    y_prompt = rmsnorm(xp, final_norm_g)
    new_state_rwkv = jnp.stack(states, axis=1)
    new_cache_diff_k = jnp.stack(ks, axis=1)
    new_cache_diff_v = jnp.stack(vs, axis=1)

    rope = axial_rope(x_sample.shape[1])
    xs = x_sample
    for l in range(DEPTH):
        xs, _, _, _ = trunk_layer(xs, c, p, l, state_rwkv[:, l].astype(F32), cache_diff_k[:, l], cache_diff_v[:, l], rope)
    y_sample = rmsnorm(xs, final_norm_g)
    return (y_prompt, y_sample, new_state_rwkv, new_cache_diff_k, new_cache_diff_v)


_drawn_inputs = setup_inputs


def setup_inputs(seed=0):
    import zlib

    import numpy as np

    out = dict(_drawn_inputs(seed))
    spreads = {}
    factors = {'state_rwkv': 4.852,
     'norm2_g': 7.013,
     'final_norm_g': 2.844,
     'decay_up': 3.982,
     'lnx_g': 8.0,
     'lnx_b': 8.0,
     'diff_lambda': 4.907,
     'subln_g': 8.0}
    for name, (base, spread) in spreads.items():
        noise = np.random.default_rng([zlib.crc32(name.encode()), seed]).standard_normal(out[name].shape)
        drawn = base * np.exp(spread * noise) if base else spread * noise
        out[name] = __import__('jax').numpy.asarray(drawn.astype(out[name].dtype))
    for name, factor in factors.items():
        out[name] = (out[name] * factor).astype(out[name].dtype)
    return out
```

```python
import math
from contextlib import ExitStack

import numpy as np

import concourse.bass as bass
from concourse import mybir

F32 = mybir.dt.float32
ALU = mybir.AluOpType
ACT = mybir.ActivationFunctionType
AX = mybir.AxisListType

P = 128
D = 1024
KC = D // P
DEPTH = 2
SEQ, DEC = 128, 256
TOK = SEQ + DEC
TILES = TOK // P
HD = 64
DR = 384
HC = DR // P
HEADS = DR // HD
DQK = 32
NR = 1344
FNET0 = 1152
NTOK = 1408
DIN = NR + NTOK
DFF = 2816
FC = DFF // P
GRID_W = 64
RMS_EPS, GN_EPS, SUBLN_EPS = 1e-6, 64e-5, 1e-5
DECAY = math.exp(-0.5)
QSCALE = DQK ** -0.5
GROUPS = ((0, SEQ), (SEQ, TOK))
RING = 4
LEVELS = 7

VEC = {}
_row = 0
for _name, _n in (("norm1_g", 8), ("norm2_g", 8), ("b_mod", 48), ("decay_w0", 6), ("iclr_a0", 6), ("k_k", 3),
                  ("k_a", 3), ("r_k", 3), ("lnx_g", 3), ("lnx_b", 3), ("subln_g", 1), ("mu0", 11), ("mu1", 11)):
    VEC[_name] = _row
    _row += _n
SH1, SC1, G1, SH2, SC2, G2 = range(0, 48, 8)

S_MOD, S_R, S_GD, S_T, S_OUT, S_FI, S_FO, SLOTS = 0, 24, 29, 30, 35, 39, 61, 72

STAGES = {
    "vector_setup": "vec dvec lam_dots mods gmod lam",
    "vector_norm1": "n1_rstd n1_scaled",
    "vector_norm2": "n2_rstd n2_scaled",
    "vector_shift": "u_prev shifted",
    "vector_layouts": "gd_sig vtok S0T kT",
    "vector_attention": "max neg_max rinv rlam p1 pdiff o",
    "vector_subnorm": "o_sq o_ms o_rinv o_n",
    "vector_keys": "kk_raw kk_sq kk_den kk",
    "vector_decay": "LW sum nh EI EX kap r k_scaled b_scaled",
    "vector_bonus": "bonus_k bonus_r bonus",
    "vector_solve": "Z Sfin stmp SH",
    "vector_groupnorm": "gn_d gn_sq gn y_rwkv",
    "vector_ffn": "ff_silu ff",
    "vector_prologue": "xT cond_cols final_g cond_half cond",
    "scalar_inputs": "u_copy u_own wd_tanh gd_tanh",
    "scalar_sqrt": "o_sqrt kk_sqrt",
    "scalar_outputs": "y_attn fz y_fnet gate",
    "scalar_decay": "w_tanh a_tanh e_kap e_r e_3 e_tot",
    "scalar_keys": "ktok btok",
    "scalar_merge": "X XT",
    "scalar_solve": "U y_raw state_rows",
    "pool_rope": "rope_cos rope_sin rope",
    "pool_keys": "a b ka kd",
    "pool_merge": "A1 XT0",
    "tensor_norm": "vec_tr n1_ss n2_ss",
    "tensor_layouts": "v_tr s0_tr q_tr k_tr",
    "tensor_attention": "scores p_tr pv",
    "tensor_mixed": "gate_mm kk_ss o_tr fz_mm fnet_mm",
    "tensor_decay": "lora_mm kt_tr bonus_mm",
    "tensor_merge": "V_mm X_mm XT_mm",
    "tensor_solve": "Z_mm U_mm S_mm Y_mm st_tr",
    "tensor_groupnorm": "gn_mean_mm gn_var_mm",
    "tensor_ffn_out": "ffo_mm ffo_half",
}
STAGE_OF = {step: stage for stage, steps in STAGES.items() for step in steps.split()}

STEP_TILE = ((0, 0), (1, 2), (2, 1))


def tables():
    i = np.arange(P)
    eye = np.eye(P)
    t = {"ident": eye, "ones": np.ones((P, P)), "bones": (i[:, None] // HD == i[None] // HD) * 1.0}
    s, q = i[:, None], i[None]
    t["amask"] = np.concatenate([s < q, s > q, s <= q, s >= q], 1) * 1.0
    lm = []
    for j in range(LEVELS):
        b = 1 << j
        low = (s // (2 * b) == q // (2 * b)) & (s // b % 2 == 1) & (q // b % 2 == 0)
        lm += [eye - low, eye - low.T]
    t["lmask"] = np.concatenate(lm, 1)
    t["smask"] = np.tile((np.arange(TOK) % P != 0) * 1.0, (P, 1))
    f = np.float32
    pos = np.arange(DEC)
    row, col = (pos // GRID_W).astype(f), (pos % GRID_W).astype(f)
    inv = (1.0 / (f(10000.0) ** (np.arange(8, dtype=f) / f(8)))).astype(f)
    ang = np.stack([row[:, None] * inv, col[:, None] * inv], 1)
    cs, sn = np.cos(ang), np.sin(ang)
    cos = np.stack([cs, cs], 2).reshape(2, P, 32)
    sin = np.stack([-sn, sn], 2).reshape(2, P, 32)
    t["cos"] = cos.transpose(1, 0, 2).reshape(P, 64)
    t["sin"] = sin.transpose(1, 0, 2).reshape(P, 64)

    def dft(n):
        a = 2 * np.pi * (np.outer(np.arange(n), np.arange(n)) % n) / n
        return np.cos(a) / np.sqrt(n), np.sin(a) / np.sqrt(n)

    c, s_ = dft(SEQ)
    t["dft_prompt"] = np.concatenate([c, s_], 1)
    c, s_ = dft(DEC)
    t["dft_sample"] = np.concatenate([c, s_], 1).reshape(2, P, 512).transpose(1, 0, 2).reshape(P, 1024)
    c, s_ = dft(HD)
    z = np.zeros((HD, HD))
    t["dft_dim"] = np.concatenate([np.block([[c, z], [z, c]]), -np.block([[s_, z], [z, s_]])], 1)
    return t


TABLES = tables()
TABLE_AT = {}
_at = 0
for _k, _v in TABLES.items():
    TABLE_AT[_k] = (_at, _v.shape[1])
    _at += _v.shape[1]
NTABLE = _at


def packed_tables():
    return np.concatenate(list(TABLES.values()), 1).astype(np.float32)


def lam_table():
    li = np.array([0.8 - 0.6 * math.exp(-0.3 * l) for l in range(DEPTH)])
    return np.repeat(np.stack([li, 1 - li], 1)[:, None], P, 1).astype(np.float32)


def build(nc, a, counts):
    ctx = ExitStack()
    with ctx:
        def sb(name, shape, dt=F32):
            return ctx.enter_context(nc.sbuf_tensor(name, shape, dt))

        sems = {}
        seen = {}
        counted = bool(counts)

        def sem(name):
            if name not in sems:
                sems[name] = ctx.enter_context(nc.semaphore(name))
            return sems[name]

        def made(name, key=0, by=1):
            stage = STAGE_OF.get(name, name)
            seen[stage] = seen.get(stage, 0) + by
            counts[name, key] = seen[stage]
            return sem(stage), by

        def loaded(name, key=0):
            return made(name, key, 16)

        def after(name, key=0):
            return sem(STAGE_OF.get(name, name)), counts[name, key] if counted else 1

        tab = sb("tab", [P, NTABLE])

        def table(name):
            at, n = TABLE_AT[name]
            return tab[:, at:at + n]

        ident, ones, bones = table("ident"), table("ones"), table("bones")
        amask = table("amask").rearrange("p (m t) -> p m t", m=4)
        lmask = table("lmask").rearrange("p (j d t) -> p j d t", j=LEVELS, d=2)
        smask = table("smask")
        cos = table("cos").rearrange("p (t n) -> p t n", t=2)
        sin = table("sin").rearrange("p (t x h n) -> p t x h n", t=2, x=2, h=2)
        dft_prompt = table("dft_prompt")
        dft_sample = table("dft_sample").rearrange("p (t n) -> p t n", t=2)
        dft_dim = table("dft_dim").rearrange("p (m n) -> p m n", m=2)

        xT = sb("xT", [P, KC, TOK])
        hT = sb("hT", [P, KC, TOK])
        yT = sb("yT", [P, KC, TOK])
        ring = sb("ring", [P, RING, 2048])
        big = sb("big", [P, FC * TOK])
        ffT = big[:, :].rearrange("p (f t) -> p f t", f=FC)
        tok = big[:, 0:TILES * NTOK].rearrange("p (t n) -> p t n", t=TILES)
        uT = big[:, TILES * NTOK:].rearrange("p (c t) -> p c t", c=11)
        xsq = big[:, 0:KC * TOK].rearrange("p (k t) -> p k t", k=KC)
        xin = big[:, 0:TILES * D].rearrange("p (t n) -> p t n", t=TILES)

        share = sb("share", [P, 10752])
        cut = [0]

        def part(n):
            cut[0] += n
            return share[:, cut[0] - n:cut[0]]

        rot = part(1536).rearrange("p (t n) -> p t n", t=2)
        rot2 = part(1536).rearrange("p (t n) -> p t n", t=2)
        qT = part(HC * TOK).rearrange("p (c t) -> p c t", c=HC)
        kT = part(HC * 512).rearrange("p (c t) -> p c t", c=HC)
        prob = part(1536).rearrange("p (b m t) -> p b m t", b=2, m=2)
        pdiff = part(768).rearrange("p (b t) -> p b t", b=2)
        pdT = part(768).rearrange("p (b t) -> p b t", b=2)
        osb = part(TILES * DR).rearrange("p (t n) -> p t n", t=TILES)
        ctxk = part(DR)
        ctxv = part(DR)
        cut[0] = 0
        AKB, AKV, ARB, ARV = (part(1536).rearrange("p (g u t) -> p g u t", g=3, u=4) for _ in range(4))
        X, XT, VB = (part(1536).rearrange("p (g u t) -> p g u t", g=3, u=4) for _ in range(3))

        kk = yT[:, 0:HC, :]
        vtok = sb("vtok", [P, TILES, DR])
        bonus = hT[:, 0:HC, :]
        gate = hT[:, HC:2 * HC, :]
        late = sb("late", [P, 2, 2, TOK])
        KAP, RT = late[:, 0], late[:, 1]
        fz = late[:, :, :, :].rearrange("p a d t -> p a (d t)")
        BT, KT, KD = (sb(n, [P, 2, TOK]) for n in ("BT", "KT", "KD"))
        LW, EI, EX, E3, AA = (sb(n, [P, TOK]) for n in ("LW", "EI", "EX", "E3", "AA"))
        ktok = sb("ktok", [P, 2, 2, P])
        btok = sb("btok", [P, 2, 2, P])
        upad = late[:, :, :, :].rearrange("p a d t -> p (a d t)")[:, 0:2 * (TOK + 3)].rearrange("p (b t) -> p b t", b=2)
        tanh2 = sb("tanh2", [P, 2, TOK])
        gsum = rstd = sb("gsum", [P, TOK])

        vrow = LW[:, 0:P]
        vec = sb("vec", [P, P])
        mods = sb("mods", [P, 48, 2])
        gmod = sb("gmod", [P, 2, KC, 2])
        scond = sb("scond", [P, KC, 2])
        fing = sb("fing", [P, KC])
        dvec = sb("dvec", [P, 64])
        muc, w0h, a0h, omka, subs = (dvec[:, 0:11], dvec[:, 11:17], dvec[:, 17:23], dvec[:, 23:26], dvec[:, 26:27])
        eps = sb("eps", [P, 4])
        lora = sb("lora", [P, DR])
        gup = sb("gup", [HD, DR])
        lrow = E3[:, 0:P]
        lprod = sb("lprod", [P, 2, DQK])
        lsum = sb("lsum", [P, 8])
        lamc = sb("lamc", [P, 2])
        lam = sb("lam", [P, 1])
        amax = sb("amax", [P, 2, 2])
        nmax = sb("nmax", [P, 2, 2])
        rsum = sb("rsum", [P, 2, 2])
        rinv = sb("rinv", [P, 2, 2])
        onorm = sb("onorm", [P, 18])
        zs = AA[:, 0:256]
        usb = hT[:, 6:8, :].rearrange("p k t -> p (k t)").rearrange("p (g n) -> p g n", g=3)
        nh = sb("nh", [P, 2, 3])
        et = sb("et", [P, 2, 3])
        sin_rows = BT[0:HD, :, :]
        S0T = sb("S0T", [P, 2, HC, HD])
        SH = sb("SH", [P, 3, 2, HD])
        stmp = sb("stmp", [P, 2, HD])
        Sfin = sb("Sfin", [P, HC, 2, HD])
        sout = KD[0:HD, :, :]
        PS = ctx.enter_context(nc.psum_tensor("PS", [P, 8, 512], F32))

        def layer(x, l):
            s = x[bass.ds(l, 1)]
            n = len(x.shape)
            names = " ".join("bcdefg"[:n - 1])
            first = names.split()[0]
            rest = " ".join(names.split()[1:])
            return s.rearrange(f"o {names} -> (o {first}) {rest}")

        def reset(all_sems):
            with nc.Block() as block:
                @block.sync
                def _(sp):
                    for x in all_sems:
                        sp.sem_clear(x)

        with nc.Block() as block:
            @block.sync
            def _(sp):
                sp.dma_start(tab[:, :], a["tables"]).then_inc(*loaded("tables"))
                sp.dma_start(xin[:, 0, :], a["x_prompt"][0]).then_inc(*loaded("x_loaded"))
                sp.dma_start(xin[:, 1:3, :], a["x_sample"][0].rearrange("(t p) n -> p t n", p=P)).then_inc(*loaded("x_loaded", 1))

            @block.scalar
            def _(act):
                act.wait_ge(*after("vrow_zero"))
                for i, n in enumerate(("c_ctx", "c", "final_norm_g")):
                    src = a[n][0] if n == "c" else a[n]
                    act.dma_start(vrow[8 * i:8 * i + 8, :], src.rearrange("(k p) -> k p", p=P)).then_inc(*loaded("cond_loaded", i))
                act.wait_ge(*after("cond_cols"))
                nc.scalar.activation(scond[:, :, :].rearrange("p k c -> p c k"),
                                     vec[:, 0:16].rearrange("p (c k) -> p c k", c=2), ACT.Tanh,
                                     scale=0.5).then_inc(*made("cond_tanh"))

            @block.gpsimd
            def _(pool):
                nc.gpsimd.memset(vrow[:, :], 0.0).then_inc(*made("vrow_zero"))
                nc.gpsimd.memset(eps[:, 0:1], RMS_EPS).then_inc(*made("pads", 1))
                nc.gpsimd.memset(eps[:, 1:2], GN_EPS).then_inc(*made("pads", 2))
                nc.gpsimd.memset(eps[:, 2:3], SUBLN_EPS).then_inc(*made("pads", 3))
                nc.gpsimd.memset(eps[:, 3:4], 0.0).then_inc(*made("pads", 4))

            @block.tensor
            def _(pe):
                pe.wait_ge(*after("tables"))
                pe.wait_ge(*after("x_loaded", 1))
                for k in range(KC):
                    if k >= 4:
                        pe.wait_ge(*after("xT", k - 4))
                    for t in range(TILES):
                        mm = nc.tensor.transpose(PS[:, k % 4, t * P:(t + 1) * P], xin[:, t, k * P:(k + 1) * P], ident)
                    mm.then_inc(*made("xT_mm", k))
                pe.wait_ge(*after("cond_loaded", 2))
                nc.tensor.transpose(PS[:, 4, 0:P], vrow[:, :], ident).then_inc(*made("cond_mm"))

            @block.vector
            def _(dve):
                for k in range(KC):
                    dve.wait_ge(*after("xT_mm", k))
                    nc.vector.tensor_copy(xT[:, k, :], PS[:, k % 4, 0:TOK]).then_inc(*made("xT", k))
                dve.wait_ge(*after("cond_mm"))
                nc.vector.tensor_copy(vec[:, :], PS[:, 4, 0:P]).then_inc(*made("cond_cols"))
                dve.wait_ge(*after("cond_cols"))
                nc.vector.tensor_copy(fing[:, :], vec[:, 16:24]).then_inc(*made("final_g"))
                dve.wait_ge(*after("cond_tanh"))
                for i in range(2):
                    nc.vector.tensor_scalar(lprod[:, i, 0:8], scond[:, :, i], 1.0, 0.5, ALU.add, ALU.mult).then_inc(*made("cond_half", i))
                dve.wait_ge(*after("cond_half", 1))
                for i in range(2):
                    nc.vector.tensor_tensor(scond[:, :, i], lprod[:, i, 0:8], vec[:, 8 * i:8 * i + 8], ALU.mult).then_inc(*made("cond", i))

        reset(list(sems.values()))
        prologue_names = set(sems)

        def norm_act(act, n, eps_col=0):
            for k in range(KC):
                nc.scalar.activation(xsq[:, k, :], xT[:, k, :], ACT.Square).then_inc(*made(f"{n}_sq", k))
            act.wait_ge(*after(f"{n}_ss"))
            nc.scalar.activation(rstd[:, :], PS[:, 6, 0:TOK], ACT.Sqrt, bias=eps[:, eps_col:eps_col + 1],
                                 scale=1.0 / D).then_inc(*made(f"{n}_sqrt"))

        def norm_pe(pe, n):
            for k in range(KC):
                pe.wait_ge(*after(f"{n}_sq", k))
                mm = nc.tensor.matmul(PS[:, 6, 0:TOK], ones, xsq[:, k, :], start=(k == 0), stop=(k == KC - 1))
            mm.then_inc(*made(f"{n}_ss"))

        with nc.Fori(0, DEPTH) as l:
            first_sems = set(sems)
            with nc.Block() as block:
                def layer2(x, l, p=P):
                    return x[bass.ds(l, 1)].rearrange("o (k p) -> (o k) p", p=p)

                def flat(x):
                    return x.rearrange("p u t -> p (u t)")

                def tok_job(n):
                    if n < 3:
                        return NTOK - P, P, n
                    s, t = divmod(n - 3, 3)
                    return 256 * s, 256, t

                def xbank(j, g):
                    return 2 if (3 * j + g) % 2 else 4

                def vbank(j, g):
                    return (3 * j + g) % 2

                def copy_pdT(act, i):
                    nk = 128 if i < HEADS else 384
                    act.wait_ge(*after("p_tr", i))
                    if i >= 2:
                        act.wait_ge(*after("pv", i - 2))
                    nc.scalar.activation(pdT[:, i % 2, 0:nk], PS[:, 4 + i % 2, 0:nk], ACT.Copy).then_inc(*made("pdT", i))

                prob_flat = prob.rearrange("p b m t -> p (b m t)")

                def abank(n, h):
                    return ((0, 1), (5, 6))[n % 2][h]

                def diff(dve, i):
                    V = nc.vector
                    t, h = divmod(i, HEADS)
                    nk = 128 if t == 0 else 384
                    dve.wait_ge(*after("exp", (i, 1)))
                    V.reciprocal(rinv[:, i % 2, :], rsum[:, i % 2, :]).then_inc(*made("rinv", i))
                    dve.wait_ge(*after("rinv", i))
                    V.tensor_scalar(rinv[:, i % 2, 1:2], rinv[:, i % 2, 1:2], lam[:, 0:1], None, ALU.mult).then_inc(*made("rlam", i))
                    dve.wait_ge(*after("rlam", i))
                    V.tensor_scalar(prob[:, i % 2, 1, 0:nk], prob[:, i % 2, 1, 0:nk], rinv[:, i % 2, 1:2], None, ALU.mult).then_inc(*made("p1", i))
                    dve.wait_ge(*after("p1", i))
                    if i >= 2:
                        dve.wait_ge(*after("p_tr", i - 2))
                    V.scalar_tensor_tensor(pdiff[:, i % 2, 0:nk], prob[:, i % 2, 0, 0:nk], rinv[:, i % 2, 0:1],
                                           prob[:, i % 2, 1, 0:nk], ALU.mult, ALU.subtract).then_inc(*made("pdiff", i))
                    if h == 2 and t >= 1:
                        copy_o(dve, t - 1)
                    if i == 17:
                        copy_o(dve, 2)

                def copy_o(dve, t):
                    dve.wait_ge(*after("pv", HEADS * t + HEADS - 1))
                    nc.vector.tensor_copy(osb[:, t, :], PS[:, 6 + t % 2, 0:DR]).then_inc(*made("o", t))

                def last_use(s):
                    if s < S_R:
                        return "mod_mm", s
                    if s < S_GD:
                        return "in_mm", 2 * (s - S_R) + 1
                    if s < S_OUT:
                        return "in_mm", 13 + 3 * (s - S_GD)
                    if s < S_FI:
                        return "out_mm", 2 * (s - S_OUT) + 1
                    if s < S_FO:
                        return "ff_mm", s - S_FI
                    return "ffo_mm", s - S_FO

                def slot_loads(s):
                    dst = ring[:, s % RING, :]
                    d8 = dst.rearrange("p (k n) -> p k n", k=KC)
                    if s < S_R:
                        w = layer(a["w_mod"], l).rearrange("(k p) n -> p k n", p=P)
                        return [(d8, w[:, :, 256 * s:256 * s + 256])]
                    if s < S_OUT:
                        w = layer(a["w_in"], l).rearrange("(k p) n -> p k n", p=P)
                        if s < S_GD:
                            at = 256 * (s - S_R)
                            return [(d8, w[:, :, at:at + 256])]
                        if s == S_GD:
                            return [(d8[:, :, 0:64], w[:, :, 1280:NR]), (d8[:, :, 64:192], w[:, :, DIN - P:DIN])]
                        at = NR + 256 * (s - S_T)
                        return [(d8, w[:, :, at:at + 256])]
                    if s < S_FI:
                        w = layer(a["w_out"], l).rearrange("(k p) n -> p k n", p=P)
                        at = 256 * (s - S_OUT)
                        return [(d8, w[:, :, at:at + 256])]
                    if s < S_FO:
                        w = layer(a["w_ffn_in"], l).rearrange("(k p) n -> p k n", p=P)
                        f = s - S_FI
                        return [(d8[:, :, 0:P], w[:, :, f * P:f * P + P]),
                                (d8[:, :, P:2 * P], w[:, :, DFF + f * P:DFF + f * P + P])]
                    w = layer(a["w_ffn_out"], l).rearrange("(k p) n -> p k n", p=P)
                    d4 = dst.rearrange("p (k n) -> p k n", k=4)
                    units = [divmod(4 * (s - S_FO) + j, FC) for j in range(4)]
                    out = []
                    j = 0
                    while j < 4:
                        half, k0 = units[j]
                        m = 1
                        while j + m < 4 and units[j + m][0] == half:
                            m += 1
                        out.append((d4[:, j:j + m, :], w[:, k0:k0 + m, half * 512:half * 512 + 512]))
                        j += m
                    return out

                @block.sync
                def _(sp):
                    for s in range(SLOTS):
                        if s >= RING:
                            sp.wait_ge(*after(*last_use(s - RING)))
                        for dst, src in slot_loads(s):
                            sp.dma_start(dst, src).then_inc(*loaded(f"slot{s % RING}", s))
                    sp.wait_ge(*after("state_stored", 1))

                @block.gpsimd
                def _(pool):
                    for i, at in enumerate((0, SEQ + 1, TOK + 2)):
                        nc.gpsimd.memset(upad[:, :, at:at + 1], 0.0).then_inc(*made("pad_cols", i))
                    for t in range(2):
                        src = tok[:, t + 1, 0:768]
                        pool.wait_ge(*after("tok_dve", 14))
                        pool.wait_ge(*after("tok_act", 14))
                        nc.gpsimd.tensor_tensor(rot[:, t, :].rearrange("p (h n) -> p h n", n=32),
                                                src.rearrange("p (h n) -> p h n", n=32),
                                                cos[:, t, :].unsqueeze(1).to_broadcast([P, 24, 32]),
                                                ALU.mult).then_inc(*made("rope_cos", t))
                        for h in range(2):
                            o = rot2[:, t, :].rearrange("p (g x h n) -> p g x h n", g=24, x=2, h=2)[:, :, :, h, :]
                            i = src.rearrange("p (g x h n) -> p g x h n", g=24, x=2, h=2)[:, :, :, 1 - h, :]
                            nc.gpsimd.tensor_tensor(o, i, sin[:, t, :, h, :].unsqueeze(1).to_broadcast([P, 24, 2, 8]),
                                                    ALU.mult).then_inc(*made("rope_sin", (t, h)))
                        pool.wait_ge(*after("rope_cos", t))
                        pool.wait_ge(*after("rope_sin", (t, 1)))
                        nc.gpsimd.tensor_tensor(rot[:, t, :], rot[:, t, :], rot2[:, t, :], ALU.add).then_inc(*made("rope", t))
                    for c in range(HC):
                        for d in range(2):
                            pool.wait_ge(*after("a_tanh", (c, d)))
                            if (c, d) == (0, 0):
                                pool.wait_ge(*after("kk", HC - 1))
                            if c >= 1:
                                pool.wait_ge(*after("A_mm", (c - 1, 2, 1)))
                                pool.wait_ge(*after("kt_tr", c - 1))
                                pool.wait_ge(*after("bonus_k", c - 1))
                            nc.gpsimd.tensor_scalar(AA[:, :], AA[:, :], 0.5, 0.5, ALU.mult, ALU.add).then_inc(*made("a", (c, d)))
                            pool.wait_ge(*after("a", (c, d)))
                            nc.gpsimd.tensor_tensor(BT[:, d, :], AA[:, :], kk[:, c, :], ALU.mult).then_inc(*made("b", (c, d)))
                            nc.gpsimd.tensor_scalar(KD[:, d, :], AA[:, :], vec[:, VEC["k_a"] + c:VEC["k_a"] + c + 1],
                                                    omka[:, c:c + 1], ALU.mult, ALU.add).then_inc(*made("ka", (c, d)))
                            pool.wait_ge(*after("ka", (c, d)))
                            nc.gpsimd.tensor_tensor(KD[:, d, :], KD[:, d, :], uT[:, 3 + c, :], ALU.mult).then_inc(*made("kd", (c, d)))
                        for g in range(3):
                            pool.wait_ge(*after("A", (c, g, 0)))
                            nc.gpsimd.tensor_tensor(AKB[:, g, :, :], AKB[:, g, :, :],
                                                    ident.unsqueeze(1).to_broadcast([P, 4, P]), ALU.add).then_inc(*made("A1", (c, g)))
                            pool.wait_ge(*after("A1", (c, g)))
                            for d in range(2):
                                nc.gpsimd.tensor_tensor(XT[:, g, 2 * d:2 * d + 2, :], AKB[:, g, 2 * d:2 * d + 2, :],
                                                        lmask[:, 0, 1 - d, :].unsqueeze(1).to_broadcast([P, 2, P]),
                                                        ALU.mult).then_inc(*made("XT0", (c, g, d)))

                @block.scalar
                def _(act):
                    def vload(name, rows, src):
                        at = VEC[name]
                        act.dma_start(vrow[at:at + rows, 0:src.shape[-1]], src).then_inc(*loaded("vec_loaded", name))

                    k_p = "(k p) -> k p"
                    vload("norm1_g", 8, layer2(a["norm1_g"], l))
                    vload("norm2_g", 8, layer2(a["norm2_g"], l))
                    vload("b_mod", 48, layer2(a["b_mod"], l))
                    for n in ("decay_w0", "iclr_a0"):
                        vload(n, 6, layer(a[n], l).rearrange("d (k p) -> (d k) p", p=P))
                    for n in ("k_k", "k_a", "lnx_g", "lnx_b"):
                        vload(n, 3, layer2(a[n], l))
                    vload("r_k", 3, layer(a["r_k"], l).rearrange("(k h) n -> k (h n)", h=2))
                    sg = layer2(a["subln_g"], l, 64)
                    r0 = VEC["subln_g"]
                    for h in range(2):
                        act.dma_start(vrow[r0:r0 + 1, 64 * h:64 * h + 64], sg).then_inc(*loaded("vec_loaded", ("subln", h)))
                    for i in range(2):
                        mu = layer(a["shift_mu"], l)[i:i + 1, :]
                        r0 = VEC[f"mu{i}"]
                        act.dma_start(vrow[r0:r0 + 10, :], mu[:, 0:1280].rearrange("o (k p) -> (o k) p", p=P)).then_inc(*loaded("vec_loaded", ("mu", i)))
                        act.dma_start(vrow[r0 + 10:r0 + 11, 0:64], mu[:, 1280:NR]).then_inc(*loaded("vec_loaded", ("mue", i)))
                    act.dma_start(lora[0:64, :], layer(a["decay_up"], l).rearrange("d r n -> (d r) n")).then_inc(*loaded("lora_loaded"))
                    act.dma_start(lora[64:128, :], layer(a["iclr_up"], l).rearrange("d r n -> (d r) n")).then_inc(*loaded("lora_loaded", 1))
                    act.dma_start(gup[:, :], layer(a["gate_up"], l)).then_inc(*loaded("lora_loaded", 2))
                    dl = layer(a["diff_lambda"], l).rearrange("a b -> (a b)").unsqueeze(0).to_broadcast([P, P])
                    act.dma_start(lrow[:, :], dl).then_inc(*loaded("lam_loaded"))
                    act.dma_start(lamc[:, :], layer(a["lam_init"], l)).then_inc(*loaded("lam_loaded", 1))
                    act.dma_start(ctxk, layer(a["cache_k"], l)).then_inc(*loaded("ctx_loaded"))
                    act.dma_start(ctxv, layer(a["cache_v"], l)).then_inc(*loaded("ctx_loaded", 1))
                    for d in range(2):
                        act.dma_start(sin_rows[:, d, :].rearrange("v (h k) -> v h k", h=HEADS),
                                      layer(a["state"], l)[d].rearrange("h v k -> v h k")).then_inc(*loaded("state_loaded", d))

                    norm_act(act, "n1")
                    def add_shift(n, base):
                        for k in range(KC):
                            for gi, (t0, t1) in enumerate(GROUPS):
                                act.wait_ge(*after(f"{n}_scaled", (k, gi)))
                                nc.scalar.activation(hT[:, k, t0:t1], hT[:, k, t0:t1], ACT.Identity,
                                                     bias=mods[:, base + k, gi:gi + 1]).then_inc(*made(f"{n}_h", (k, gi)))

                    add_shift("n1", SH1)
                    act.wait_ge(*after("lam_dots", 1))
                    nc.scalar.activation(lsum[:, 2:4], lsum[:, 0:2], ACT.Exp).then_inc(*made("lam_exp"))

                    for j in range(11):
                        m = HD if j == 10 else P
                        act.wait_ge(*after("in_mm", j))
                        if j >= 2:
                            act.wait_ge(*after("shifted", j - 2))
                        u = PS[0:m, j % 4, 0:TOK]
                        nc.scalar.activation(upad[0:m, j % 2, 1:1 + SEQ], u[:, 0:SEQ], ACT.Copy).then_inc(*made("u_copy", (j, 0)))
                        nc.scalar.activation(upad[0:m, j % 2, 2 + SEQ:2 + TOK], u[:, SEQ:TOK], ACT.Copy).then_inc(*made("u_copy", (j, 1)))
                        nc.scalar.activation(uT[0:m, j, :], u, ACT.Copy, scale=muc[0:m, j:j + 1]).then_inc(*made("u_own", j))
                    for n in range(18):
                        if n % 2 == 0:
                            at, w, t = tok_job(n)
                            act.wait_ge(*after("in_mm", 11 + n))
                            nc.scalar.activation(tok[:, t, at:at + w], PS[:, (11 + n) % 4, 0:w], ACT.Copy).then_inc(*made("tok_act", n if n < 14 else 14))
                    act.wait_ge(*after("tok_dve", 14))
                    act.wait_ge(*after("tok_act", 14))
                    act.dma_start(layer(a["out_k"], l), tok[:, 0, 384:768]).then_inc(*loaded("cache_stored"))
                    act.dma_start(layer(a["out_v"], l), tok[:, 0, 768:1152]).then_inc(*loaded("cache_stored", 1))
                    act.wait_ge(*after("shifted", 10))
                    nc.scalar.activation(tanh2[0:64, 0, :], uT[0:64, 9, :], ACT.Tanh).then_inc(*made("wd_tanh"))
                    nc.scalar.activation(tanh2[0:64, 1, :], uT[0:64, 10, :], ACT.Tanh, scale=0.5).then_inc(*made("gd_tanh"))
                    for c in range(HC):
                        act.wait_ge(*after("q_tr", c))
                        nc.scalar.activation(qT[:, c, :], PS[:, (2 * c) % 8, 0:TOK], ACT.Copy).then_inc(*made("qT", c))
                    for i in range(18):
                        t, h = divmod(i, HEADS)
                        nk = 128 if t == 0 else 384
                        act.wait_ge(*after("neg_max", i))
                        if i >= 2:
                            act.wait_ge(*after("pdiff", i - 2))
                        for m in range(2):
                            nc.scalar.activation(prob[:, i % 2, m, 0:nk], PS[:, 2 * (i % 2) + m, 0:nk], ACT.Exp,
                                                 bias=nmax[:, i % 2, m:m + 1], scale=QSCALE,
                                                 accum_out=rsum[:, i % 2, m:m + 1]).then_inc(*made("exp", (i, m)))
                        if i >= 1:
                            copy_pdT(act, i - 1)
                    copy_pdT(act, 17)
                    for c in range(HC):
                        act.wait_ge(*after("gate_mm", c))
                        nc.scalar.activation(gate[:, c, :], PS[:, c, 0:TOK], ACT.Copy).then_inc(*made("gate", c))
                    act.wait_ge(*after("o_ms"))
                    nc.scalar.activation(onorm[:, :], onorm[:, :], ACT.Sqrt, bias=eps[:, 2:3], scale=1.0 / HD).then_inc(*made("o_sqrt"))
                    for c in range(HC):
                        act.wait_ge(*after("kk_ss", c))
                        nc.scalar.activation(KD[:, 0, :] if c == 0 else KD[:, 1, :] if c == 1 else E3[:, :],
                                             PS[:, 3 + c, 0:TOK], ACT.Sqrt, bias=eps[:, 3:4]).then_inc(*made("kk_sqrt", c))
                    for t in range(TILES):
                        act.wait_ge(*after("o_tr", t))
                        nc.scalar.activation(yT[:, 3:6, t * P:(t + 1) * P],
                                             PS[:, t, 0:DR].rearrange("p (c n) -> p c n", c=3), ACT.Copy,
                                             scale=subs).then_inc(*made("y_attn", t))
                    for dc in range(2):
                        act.wait_ge(*after("fz_mm", dc))
                        nc.scalar.activation(fz[:, dc, 0:256], PS[:, 4 + 2 * dc, 0:256], ACT.Copy).then_inc(*made("fz", (dc, 0)))
                        nc.scalar.activation(fz[:, dc, 256:768], PS[:, 5 + 2 * dc, :], ACT.Copy).then_inc(*made("fz", (dc, 1)))
                    for dc in range(2):
                        act.wait_ge(*after("fnet_mm", dc))
                        nc.scalar.activation(yT[:, 6 + dc, :], PS[:, dc, 0:TOK], ACT.Copy).then_inc(*made("y_fnet", dc))
                    for c in range(HC):
                        for d in range(2):
                            act.wait_ge(*after("lora_mm", (c, d)))
                            if (c, d) != (0, 0):
                                pc, pd = (c, 0) if d else (c - 1, 1)
                                act.wait_ge(*after("ka", (pc, pd)))
                                act.wait_ge(*after("b", (pc, pd)))
                                act.wait_ge(*after("EX", (pc, pd)))
                            nc.scalar.activation(LW[:, :], PS[:, 0, 0:TOK], ACT.Tanh, scale=0.5,
                                                 bias=w0h[:, 3 * d + c:3 * d + c + 1]).then_inc(*made("w_tanh", (c, d)))
                            nc.scalar.activation(AA[:, :], PS[:, 1, 0:TOK], ACT.Tanh, scale=0.5,
                                                 bias=a0h[:, 3 * d + c:3 * d + c + 1]).then_inc(*made("a_tanh", (c, d)))
                            act.wait_ge(*after("EX", (c, d)))
                            if c >= 1:
                                act.wait_ge(*after("Y_mm", c - 1))
                            if (c, d) != (0, 0):
                                act.wait_ge(*after("b_scaled", (pc, pd)))
                            kap, r, e3 = (((EX, 1.0), (EI, 1.0), (EI, -1.0)), ((EI, -1.0), (EX, -1.0), (EX, 1.0)))[d]
                            nc.scalar.activation(KAP[:, d, :], kap[0][:, :], ACT.Exp, scale=kap[1]).then_inc(*made("e_kap", (c, d)))
                            nc.scalar.activation(RT[:, d, :], r[0][:, :], ACT.Exp, scale=r[1]).then_inc(*made("e_r", (c, d)))
                            nc.scalar.activation(E3[:, :], e3[0][:, :], ACT.Exp, scale=e3[1]).then_inc(*made("e_3", (c, d)))
                            nc.scalar.activation(et[:, d, :], nh[:, d, :], ACT.Exp, scale=-1.0).then_inc(*made("e_tot", (c, d)))
                        act.wait_ge(*after("kt_tr", c))
                        if c >= 1:
                            act.wait_ge(*after("S_mm", (c - 1, 1)))
                        nc.scalar.activation(ktok[:, :, :, :].rearrange("p d t n -> p (d t n)"), PS[:, 2, :], ACT.Copy).then_inc(*made("ktok", c))
                        nc.scalar.activation(btok[:, :, :, :].rearrange("p d t n -> p (d t n)"), PS[:, 3, :], ACT.Copy).then_inc(*made("btok", c))
                        for j in range(1, LEVELS):
                            for g in range(3):
                                if j < LEVELS - 1:
                                    act.wait_ge(*after("X_mm", (c, j, g)))
                                    nc.scalar.activation(flat(X[:, g]), PS[:, xbank(j, g), :], ACT.Copy).then_inc(*made("X", (c, j, g)))
                                act.wait_ge(*after("XT_mm", (c, j, g)))
                                nc.scalar.activation(flat(XT[:, g]), PS[:, xbank(j, g) + 1, :], ACT.Copy).then_inc(*made("XT", (c, j, g)))
                        for g in range(3):
                            act.wait_ge(*after("U_mm", (c, g)))
                            if c >= 1 and g == 0:
                                act.wait_ge(*after("Y_mm", c - 1))
                            nc.scalar.activation(usb[:, g, :], PS[:, 7, 0:256], ACT.Copy, scale=-1.0).then_inc(*made("U", (c, g)))
                        act.wait_ge(*after("Y_mm", c))
                        for h in range(2):
                            hs = slice(h * HD, (h + 1) * HD)
                            nc.scalar.activation(yT[hs, c, :], PS[hs, 5 + h, 0:TOK], ACT.Copy).then_inc(*made("y_raw", c if h else (c, 0)))
                    for d in range(2):
                        act.wait_ge(*after("st_tr", d))
                        nc.scalar.activation(sout[:, d, :], PS[0:HD, 6 + d, 0:DR], ACT.Copy).then_inc(*made("state_rows", d))
                    act.wait_ge(*after("state_rows", 1))
                    for d in range(2):
                        act.dma_start(layer(a["out_s"], l)[d].rearrange("h v k -> v h k"),
                                      sout[:, d, :].rearrange("v (h k) -> v h k", h=HEADS)).then_inc(*loaded("state_stored", d))
                    for c in range(HC):
                        act.wait_ge(*after("gn_var_mm", c))
                        nc.scalar.activation(KT[:, 0, :] if c == 0 else KT[:, 1, :] if c == 1 else BT[:, 0, :],
                                             PS[:, 3 + c, 0:TOK], ACT.Sqrt, bias=eps[:, 1:2], scale=1.0 / HD).then_inc(*made("gn_sqrt", c))

                    act.wait_ge(*after("x1", (KC - 1, 1)))
                    act.wait_ge(*after("cache_stored", 1))
                    norm_act(act, "n2")
                    add_shift("n2", SH2)
                    for f in range(FC):
                        act.wait_ge(*after("ff_mm", f))
                        if f >= 2:
                            act.wait_ge(*after("ff", f - 2))
                        nc.scalar.activation(tanh2[:, f % 2, :], PS[:, 2 * (f % 2), 0:TOK], ACT.Tanh, scale=0.5).then_inc(*made("ff_tanh", f))

                @block.vector
                def _(dve):
                    V = nc.vector
                    dve.wait_ge(*after("vec_tr"))
                    V.tensor_copy(vec[:, :], PS[:, 5, 0:P]).then_inc(*made("vec"))
                    dve.wait_ge(*after("vec"))
                    col = lambda n, k: vec[:, VEC[n]:VEC[n] + k]
                    dve.wait_ge(*after("lam_loaded", 1))
                    V.tensor_tensor(muc, col("mu0", 11), col("mu1", 11), ALU.add).then_inc(*made("dvec", 0))
                    V.tensor_scalar(w0h, col("decay_w0", 6), 0.5, None, ALU.mult).then_inc(*made("dvec", 1))
                    V.tensor_scalar(a0h, col("iclr_a0", 6), 0.5, None, ALU.mult).then_inc(*made("dvec", 2))
                    V.tensor_scalar(omka, col("k_a", 3), -1.0, 1.0, ALU.mult, ALU.add).then_inc(*made("dvec", 3))
                    V.tensor_tensor(subs, col("subln_g", 1), lamc[:, 1:2], ALU.mult).then_inc(*made("dvec", 4))
                    dve.wait_ge(*after("dvec", 0))
                    V.tensor_scalar(muc, muc, -1.0, 1.0, ALU.mult, ALU.add).then_inc(*made("dvec", 5))
                    lr = lrow[:, :].rearrange("p (a n) -> p a n", a=4)
                    V.tensor_tensor(lprod[:, :, :], lr[:, 0:4:2, :], lr[:, 1:4:2, :], ALU.mult).then_inc(*made("lam_dots", 0))
                    dve.wait_ge(*after("lam_dots", 0))
                    V.tensor_reduce(lsum[:, 0:2], lprod[:, :, :], AX.X, ALU.add).then_inc(*made("lam_dots", 1))

                    def norm_apply(n, g, base):
                        dve.wait_ge(*after(f"{n}_sqrt"))
                        V.reciprocal(rstd[:, :], rstd[:, :]).then_inc(*made(f"{n}_rstd"))
                        dve.wait_ge(*after(f"{n}_rstd"))
                        for k in range(KC):
                            for gi, (t0, t1) in enumerate(GROUPS):
                                V.scalar_tensor_tensor(hT[:, k, t0:t1], xT[:, k, t0:t1], gmod[:, g, k, gi:gi + 1],
                                                       rstd[:, t0:t1], ALU.mult, ALU.mult).then_inc(*made(f"{n}_scaled", (k, gi)))

                    dve.wait_ge(*after("mod_mm", S_R - 1))
                    V.tensor_tensor(mods[:, :, :], PS[:, 7, 0:96].rearrange("p (n c) -> p n c", c=2),
                                    col("b_mod", 48).unsqueeze(2).to_broadcast([P, 48, 2]), ALU.add).then_inc(*made("mods"))
                    dve.wait_ge(*after("mods"))
                    for g, (n, sc) in enumerate((("norm1_g", SC1), ("norm2_g", SC2))):
                        V.tensor_scalar(gmod[:, g, :, :], mods[:, sc:sc + 8, :], 1.0, None, ALU.add).then_inc(*made("gmod", (g, 0)))
                    dve.wait_ge(*after("gmod", (1, 0)))
                    for g, (n, sc) in enumerate((("norm1_g", SC1), ("norm2_g", SC2))):
                        V.tensor_tensor(gmod[:, g, :, :], gmod[:, g, :, :], col(n, 8).unsqueeze(2).to_broadcast([P, KC, 2]),
                                        ALU.mult).then_inc(*made("gmod", (g, 1)))
                    dve.wait_ge(*after("gmod", (1, 1)))
                    norm_apply("n1", 0, SH1)
                    dve.wait_ge(*after("lam_exp"))
                    V.tensor_tensor(lsum[:, 4:5], lsum[:, 2:3], lsum[:, 3:4], ALU.subtract).then_inc(*made("lam", 0))
                    dve.wait_ge(*after("lam", 0))
                    V.tensor_tensor(lam[:, :], lsum[:, 4:5], lamc[:, 0:1], ALU.add).then_inc(*made("lam", 1))

                    for j in range(11):
                        m = HD if j == 10 else P
                        dve.wait_ge(*after("u_copy", (j, 1)))
                        dve.wait_ge(*after("u_own", j))
                        dve.wait_ge(*after("pad_cols", 2))
                        for side in range(2):
                            mu = vec[0:m, VEC[f"mu{side}"] + j:VEC[f"mu{side}"] + j + 1]
                            if side:
                                dve.wait_ge(*after("u_prev", (j, 1)))
                            for gi, (t0, t1) in enumerate(GROUPS):
                                at = t0 + gi + 2 * side
                                last = V.scalar_tensor_tensor(uT[0:m, j, t0:t1], upad[0:m, j % 2, at:at + t1 - t0], mu,
                                                              uT[0:m, j, t0:t1], ALU.mult, ALU.add)
                                last.then_inc(*(made("u_prev", (j, gi)) if side == 0 else made("shifted", j if gi else (j, 0))))
                    for n in range(18):
                        if n % 2 == 1:
                            at, w, t = tok_job(n)
                            dve.wait_ge(*after("in_mm", 11 + n))
                            V.tensor_copy(tok[:, t, at:at + w], PS[:, (11 + n) % 4, 0:w]).then_inc(*made("tok_dve", n if n < 14 else 14))
                    dve.wait_ge(*after("gd_tanh"))
                    V.tensor_scalar(tanh2[0:64, 1, :], tanh2[0:64, 1, :], 0.5, 0.5, ALU.mult, ALU.add).then_inc(*made("gd_sig"))
                    for c in range(HC):
                        dve.wait_ge(*after("v_tr", c))
                        V.tensor_copy(vtok[:, :, c * P:(c + 1) * P],
                                      PS[:, 4 + c, 0:TOK].rearrange("p (t n) -> p t n", t=3)).then_inc(*made("vtok", c))
                    dve.wait_ge(*after("s0_tr"))
                    V.tensor_copy(S0T[:, :, :, :].rearrange("p d c n -> p (d c n)"), PS[:, 7, 0:DR]).then_inc(*made("S0T"))
                    for c in range(HC):
                        dve.wait_ge(*after("k_tr", c))
                        V.tensor_copy(kT[:, c, :], PS[:, 2 * c + 1, :]).then_inc(*made("kT", c))
                    for i in range(18):
                        t, h = divmod(i, HEADS)
                        nk = 128 if t == 0 else 384
                        dve.wait_ge(*after("scores", i))
                        if i >= 2:
                            dve.wait_ge(*after("exp", (i - 2, 1)))
                        V.tensor_reduce(amax[:, i % 2, :], PS[:, 2 * (i % 2):2 * (i % 2) + 2, 0:nk], AX.X, ALU.max).then_inc(*made("max", i))
                        dve.wait_ge(*after("max", i))
                        V.tensor_scalar(nmax[:, i % 2, :], amax[:, i % 2, :], -QSCALE, None, ALU.mult).then_inc(*made("neg_max", i))
                        if i >= 1:
                            diff(dve, i - 1)
                    diff(dve, 17)
                    for t in range(TILES):
                        if t == 0:
                            dve.wait_ge(*after("o", 2))
                            dve.wait_ge(*after("pdT", 17))
                        V.tensor_tensor(prob_flat[:, t * DR:(t + 1) * DR], osb[:, t, :], osb[:, t, :], ALU.mult).then_inc(*made("o_sq", t))
                    dve.wait_ge(*after("o_sq", 2))
                    V.tensor_reduce(onorm[:, :], prob_flat[:, 0:3 * DR].rearrange("p (h n) -> p h n", n=HD), AX.X, ALU.add).then_inc(*made("o_ms"))
                    for c in range(HC):
                        V.tensor_scalar(kk[:, c, :], uT[:, 3 + c, :], vec[:, VEC["k_k"] + c:VEC["k_k"] + c + 1], None, ALU.mult).then_inc(*made("kk_raw", c))
                    dve.wait_ge(*after("kk_raw", 2))
                    for c in range(HC):
                        V.tensor_tensor((LW, EI, EX)[c][:, :], kk[:, c, :], kk[:, c, :], ALU.mult).then_inc(*made("kk_sq", c))
                    dve.wait_ge(*after("o_sqrt"))
                    V.reciprocal(onorm[:, :], onorm[:, :]).then_inc(*made("o_rinv"))
                    dve.wait_ge(*after("o_rinv"))
                    for t in range(TILES):
                        V.tensor_tensor(osb[:, t, :].rearrange("p (h n) -> p h n", n=HD), osb[:, t, :].rearrange("p (h n) -> p h n", n=HD),
                                        onorm[:, 6 * t:6 * t + 6].unsqueeze(2).to_broadcast([P, 6, HD]), ALU.mult).then_inc(*made("o_n", t))
                    for c in range(HC):
                        b = (KD[:, 0, :], KD[:, 1, :], E3[:, :])[c]
                        dve.wait_ge(*after("kk_sqrt", c))
                        V.tensor_scalar(b, b, 1e-12, None, ALU.max).then_inc(*made("kk_den", (c, 0)))
                        dve.wait_ge(*after("kk_den", (c, 0)))
                        V.reciprocal(b, b).then_inc(*made("kk_den", (c, 1)))
                        dve.wait_ge(*after("kk_den", (c, 1)))
                        V.tensor_tensor(kk[:, c, :], kk[:, c, :], b, ALU.mult).then_inc(*made("kk", c))

                    for c in range(HC):
                        for d in range(2):
                            dve.wait_ge(*after("w_tanh", (c, d)))
                            if (c, d) == (0, 0):
                                dve.wait_ge(*after("kk", 2))
                            V.tensor_scalar(LW[:, :], LW[:, :], -0.5 * DECAY, -0.5 * DECAY, ALU.mult, ALU.add).then_inc(*made("LW", (c, d)))
                            dve.wait_ge(*after("LW", (c, d)))
                            if (c, d) != (0, 0):
                                pc, pd = (c, 0) if d else (c - 1, 1)
                                dve.wait_ge(*after("e_tot", (pc, pd)))
                            V.tensor_tensor_scan(EI[:, :], smask, LW[:, :], 0.0, ALU.mult, ALU.add).then_inc(*made("sum", (c, d)))
                            dve.wait_ge(*after("sum", (c, d)))
                            V.tensor_scalar(nh[:, d, :], EI[:, P - 1:TOK:P], -0.5, None, ALU.mult).then_inc(*made("nh", (c, d)))
                            dve.wait_ge(*after("nh", (c, d)))
                            V.tensor_tensor(EI[:, :].rearrange("p (t n) -> p t n", t=3), EI[:, :].rearrange("p (t n) -> p t n", t=3),
                                            nh[:, d, :].unsqueeze(2).to_broadcast([P, 3, P]), ALU.add).then_inc(*made("EI", (c, d)))
                            dve.wait_ge(*after("EI", (c, d)))
                            V.tensor_tensor(EX[:, :], EI[:, :], LW[:, :], ALU.subtract).then_inc(*made("EX", (c, d)))
                            dve.wait_ge(*after("e_kap", (c, d)))
                            V.tensor_tensor(KAP[:, d, :], KAP[:, d, :], kk[:, c, :], ALU.mult).then_inc(*made("kap", (c, d)))
                            dve.wait_ge(*after("e_r", (c, d)))
                            V.tensor_tensor(RT[:, d, :], RT[:, d, :], uT[:, c, :], ALU.mult).then_inc(*made("r", (c, d)))
                            dve.wait_ge(*after("e_3", (c, d)))
                            dve.wait_ge(*after("kd", (c, d)))
                            V.tensor_tensor(KT[:, d, :], KD[:, d, :], E3[:, :], ALU.mult).then_inc(*made("k_scaled", (c, d)))
                            V.tensor_tensor(BT[:, d, :], BT[:, d, :], E3[:, :], ALU.mult).then_inc(*made("b_scaled", (c, d)))
                        V.tensor_tensor(gsum[:, :], KD[:, 0, :], KD[:, 1, :], ALU.add).then_inc(*made("bonus_k", c))
                        dve.wait_ge(*after("bonus_k", c))
                        V.scalar_tensor_tensor(gsum[:, :], gsum[:, :], vec[:, VEC["r_k"] + c:VEC["r_k"] + c + 1], uT[:, c, :],
                                               ALU.mult, ALU.mult).then_inc(*made("bonus_r", c))
                        dve.wait_ge(*after("bonus_mm", c))
                        V.tensor_tensor(bonus[:, c, :], PS[:, 4, 0:TOK], uT[:, 6 + c, :], ALU.mult).then_inc(*made("bonus", c))
                        dve.wait_ge(*after("e_tot", (c, 1)))
                        if c >= 1:
                            dve.wait_ge(*after("Y_mm", c - 1))
                        for d in range(2):
                            t = STEP_TILE[1][d]
                            V.tensor_scalar(SH[:, 1, d, :], S0T[:, d, c, :], et[:, d, t:t + 1], None, ALU.mult).then_inc(*made("SH", (c, 1, d)))
                        for g in range(3):
                            for n in range(2):
                                dve.wait_ge(*after("A_mm", (c, g, n)))
                                if c >= 1 and g == 0 and n == 0:
                                    dve.wait_ge(*after("Y_mm", c - 1))
                                for i, dst in enumerate(((AKB, AKV), (ARB, ARV))[n]):
                                    for h in range(2):
                                        V.tensor_tensor(dst[:, g, h:4:2, :],
                                                        PS[:, abank(2 * g + n, h), 256 * i:256 * i + 256].rearrange("p (d t) -> p d t", d=2),
                                                        amask[:, 2 * n:2 * n + 2, :], ALU.mult).then_inc(*made("A", (c, g, n) if (i, h) == (1, 1) else (c, g, n, i, h)))
                        for j in range(LEVELS):
                            for g in range(3):
                                dve.wait_ge(*after("V_mm", (c, j, g)))
                                dst = X if j == 0 else VB
                                if j >= 2:
                                    dve.wait_ge(*after("XT_mm", (c, j - 1, g)))
                                for d in range(2):
                                    V.tensor_tensor(dst[:, g, 2 * d:2 * d + 2, :],
                                                    PS[:, vbank(j, g), 256 * d:256 * d + 256].rearrange("p (u t) -> p u t", u=2),
                                                    lmask[:, j, d, :].unsqueeze(1).to_broadcast([P, 2, P]),
                                                    ALU.mult).then_inc(*made("V", (c, j, g) if d else (c, j, g, 0)))
                        for g in range(3):
                            dve.wait_ge(*after("Z_mm", (c, g)))
                            if g >= 1:
                                dve.wait_ge(*after("U_mm", (c, g - 1)))
                            for h in range(2):
                                V.tensor_copy(zs.rearrange("p (d h n) -> p d h n", d=2, h=2)[:, :, h, :],
                                              PS[:, (6, 4)[h], 0:P].rearrange("p (d n) -> p d n", d=2)).then_inc(*made("Z", (c, g) if h else (c, g, 0)))
                            if g < 2:
                                dve.wait_ge(*after("S_mm", (c, g)))
                                for d in range(2):
                                    t, tn = STEP_TILE[g][d], STEP_TILE[2][d]
                                    s = PS[:, 3, d * HD:(d + 1) * HD]
                                    if g == 0:
                                        V.tensor_scalar(Sfin[:, c, d, :], s, et[:, d, t:t + 1], None, ALU.mult).then_inc(*made("Sfin", (c, d)))
                                    else:
                                        V.tensor_tensor(stmp[:, d, :], s, SH[:, 1, d, :], ALU.add).then_inc(*made("stmp", (c, d)))
                                if g == 1:
                                    dve.wait_ge(*after("stmp", (c, 1)))
                                    for d in range(2):
                                        t, tn = STEP_TILE[g][d], STEP_TILE[2][d]
                                        V.tensor_scalar(SH[:, 2, d, :], stmp[:, d, :], et[:, d, t:t + 1], et[:, d, tn:tn + 1],
                                                        ALU.mult, ALU.mult).then_inc(*made("SH", (c, 2, d)))
                    dve.wait_ge(*after("y_raw", 2))
                    dve.wait_ge(*after("gate", 2))
                    for c in range(HC):
                        dve.wait_ge(*after("gn_mean_mm", c))
                        V.scalar_tensor_tensor(yT[:, c, :], PS[:, c, 0:TOK], -1.0 / HD, yT[:, c, :], ALU.mult, ALU.add).then_inc(*made("gn_d", c))
                        dve.wait_ge(*after("gn_d", c))
                        V.tensor_tensor((KAP[:, 0], KAP[:, 1], RT[:, 0])[c], yT[:, c, :], yT[:, c, :], ALU.mult).then_inc(*made("gn_sq", c))
                    for c in range(HC):
                        b = (KT[:, 0, :], KT[:, 1, :], BT[:, 0, :])[c]
                        dve.wait_ge(*after("gn_sqrt", c))
                        V.reciprocal(b, b).then_inc(*made("gn", (c, 0)))
                        dve.wait_ge(*after("gn", (c, 0)))
                        V.tensor_tensor(yT[:, c, :], yT[:, c, :], b, ALU.mult).then_inc(*made("gn", (c, 1)))
                        dve.wait_ge(*after("gn", (c, 1)))
                        V.tensor_scalar(yT[:, c, :], yT[:, c, :], vec[:, VEC["lnx_g"] + c:VEC["lnx_g"] + c + 1],
                                        vec[:, VEC["lnx_b"] + c:VEC["lnx_b"] + c + 1], ALU.mult, ALU.add).then_inc(*made("gn", (c, 2)))
                        dve.wait_ge(*after("gn", (c, 2)))
                        V.tensor_tensor(yT[:, c, :], yT[:, c, :], bonus[:, c, :], ALU.add).then_inc(*made("gn", (c, 3)))
                        dve.wait_ge(*after("gn", (c, 3)))
                        V.tensor_tensor(yT[:, c, :], yT[:, c, :], gate[:, c, :], ALU.mult).then_inc(*made("y_rwkv", c))

                    for m in range(KC):
                        dve.wait_ge(*after("out_mm", m))
                        for gi, (t0, t1) in enumerate(GROUPS):
                            V.scalar_tensor_tensor(xT[:, m, t0:t1], PS[:, m % 4, t0:t1], mods[:, G1 + m, gi:gi + 1], xT[:, m, t0:t1],
                                                   ALU.mult, ALU.add).then_inc(*made("x1", (m, gi)))
                    norm_apply("n2", 1, SH2)
                    for f in range(FC):
                        dve.wait_ge(*after("ff_tanh", f))
                        V.scalar_tensor_tensor(tanh2[:, f % 2, :], tanh2[:, f % 2, :], 1.0, PS[:, 2 * (f % 2), 0:TOK], ALU.add, ALU.mult).then_inc(*made("ff_silu", f))
                        dve.wait_ge(*after("ff_silu", f))
                        V.scalar_tensor_tensor(ffT[:, f, :], tanh2[:, f % 2, :], 0.5, PS[:, 2 * (f % 2) + 1, 0:TOK], ALU.mult, ALU.mult).then_inc(*made("ff", f))
                    for half in range(2):
                        dve.wait_ge(*(after("ffo_mm", SLOTS - S_FO - 1) if half else after("ffo_half")))
                        for m in range(4):
                            for gi, (t0, t1) in enumerate(GROUPS):
                                V.scalar_tensor_tensor(xT[:, 4 * half + m, t0:t1], PS[:, 4 - 4 * half + m, t0:t1],
                                                       mods[:, G2 + 4 * half + m, gi:gi + 1], xT[:, 4 * half + m, t0:t1],
                                                       ALU.mult, ALU.add).then_inc(*made("x2", (half, m, gi)))

                @block.tensor
                def _(pe):
                    T = nc.tensor

                    def need(s):
                        pe.wait_ge(*after(f"slot{s % RING}", s))
                        return ring[:, s % RING, :].rearrange("p (k n) -> p k n", k=4 if s >= S_FO else KC)

                    pe.wait_ge(*after("vec_loaded", ("mue", 1)))
                    T.transpose(PS[:, 5, 0:P], vrow[:, :], ident).then_inc(*made("vec_tr"))
                    norm_pe(pe, "n1")
                    for s in range(S_R):
                        w = need(s)
                        for b in range(2):
                            n = 2 * s + b
                            for k in range(KC):
                                mm = T.matmul(PS[:, 7, 2 * n:2 * n + 2], w[:, k, b * P:(b + 1) * P], scond[:, k, :],
                                              start=(k == 0), stop=(k == KC - 1))
                        mm.then_inc(*made("mod_mm", s))
                    for j in range(11):
                        s = S_R + j // 2
                        m = HD if j == 10 else P
                        at = P * (j % 2)
                        w = need(s)
                        if j == 0:
                            pe.wait_ge(*after("vec"))
                            pe.wait_ge(*after("n1_h", (KC - 1, 1)))
                        if j >= 4:
                            pe.wait_ge(*after("u_own", j - 4))
                        for k in range(KC):
                            mm = T.matmul(PS[0:m, j % 4, 0:TOK], w[:, k, at:at + m], hT[:, k, :], start=(k == 0), stop=(k == KC - 1))
                        mm.then_inc(*made("in_mm", j))
                    for n in range(18):
                        at, wd, t = tok_job(n)
                        s = S_GD if n < 3 else S_T + (n - 3) // 3
                        w = need(s)
                        q = 11 + n - 4
                        if q < 11:
                            pe.wait_ge(*after("u_own", q))
                        else:
                            o = q - 11
                            pe.wait_ge(*after("tok_dve" if o % 2 else "tok_act", o if o < 14 else 14))
                        a0 = 64 if n < 3 else 0
                        for k in range(KC):
                            mm = T.matmul(PS[:, (11 + n) % 4, 0:wd], hT[:, k, t * P:(t + 1) * P], w[:, k, a0:a0 + wd],
                                          start=(k == 0), stop=(k == KC - 1))
                        mm.then_inc(*made("in_mm", 11 + n))
                    pe.wait_ge(*after("shifted", 10))
                    for c in range(HC):
                        if c == 1:
                            pe.wait_ge(*after("vec"))
                        for t in range(TILES):
                            mm = T.transpose(PS[:, 4 + c, t * P:(t + 1) * P], uT[:, 6 + c, t * P:(t + 1) * P], ident)
                        mm.then_inc(*made("v_tr", c))
                    pe.wait_ge(*after("state_loaded", 1))
                    pe.wait_ge(*after("mods"))
                    for d in range(2):
                        for c in range(HC):
                            mm = T.transpose(PS[:, 7, (3 * d + c) * HD:(3 * d + c + 1) * HD], sin_rows[:, d, c * P:(c + 1) * P], ident[0:HD, 0:HD])
                    mm.then_inc(*made("s0_tr"))
                    pe.wait_ge(*after("rope", 1))
                    pe.wait_ge(*after("tok_dve", 14))
                    pe.wait_ge(*after("tok_act", 14))
                    pe.wait_ge(*after("S0T"))
                    pe.wait_ge(*after("ctx_loaded", 1))
                    for c in range(HC):
                        cs = slice(c * P, (c + 1) * P)
                        ks = slice(DR + c * P, DR + (c + 1) * P)
                        for t in range(TILES):
                            src = tok[:, 0, cs] if t == 0 else rot[:, t - 1, cs]
                            mm = T.transpose(PS[:, 2 * c, t * P:(t + 1) * P], src, ident)
                        mm.then_inc(*made("q_tr", c))
                        for t in range(4):
                            src = (tok[:, 0, ks], ctxk[:, cs], rot[:, 0, ks], rot[:, 1, ks])[t]
                            mm = T.transpose(PS[:, 2 * c + 1, t * P:(t + 1) * P], src, ident)
                        mm.then_inc(*made("k_tr", c))

                    def scores(i):
                        t, h = divmod(i, HEADS)
                        k0, k1 = (0, P) if t == 0 else (P, 512)
                        if i < 2:
                            pe.wait_ge(*after("qT", 2))
                            pe.wait_ge(*after("kT", 2))
                        else:
                            pe.wait_ge(*after("exp", (i - 2, 1)))
                        for m in range(2):
                            c, r = divmod(2 * h + m, 4)
                            rows = slice(32 * r, 32 * r + 32)
                            mm = T.matmul(PS[:, 2 * (i % 2) + m, 0:k1 - k0], qT[rows, c, t * P:(t + 1) * P], kT[rows, c, k0:k1],
                                          start=True, stop=True)
                        mm.then_inc(*made("scores", i))

                    def p_transpose(i):
                        pe.wait_ge(*after("pdiff", i))
                        if i >= 2:
                            pe.wait_ge(*after("pdT", i - 2))
                        for kt in range(1 if i < HEADS else 3):
                            mm = T.transpose(PS[:, 4 + i % 2, kt * P:(kt + 1) * P], pdiff[:, i % 2, kt * P:(kt + 1) * P], ident)
                        mm.then_inc(*made("p_tr", i))

                    def values(i):
                        t, h = divmod(i, HEADS)
                        pe.wait_ge(*after("pdT", i))
                        if t == 2 and h == 0:
                            pe.wait_ge(*after("o", 0))
                        vs = slice(768 + h * HD, 768 + (h + 1) * HD)
                        vals = [tok[:, 0, vs]] if t == 0 else [ctxv[:, h * HD:(h + 1) * HD], tok[:, 1, vs], tok[:, 2, vs]]
                        for kt, v in enumerate(vals):
                            mm = T.matmul(PS[:, 6 + t % 2, h * HD:(h + 1) * HD], pdT[:, i % 2, kt * P:(kt + 1) * P], v,
                                          start=(kt == 0), stop=(kt == len(vals) - 1))
                        mm.then_inc(*made("pv", i))

                    for i in range(18 + 2):
                        if i < 18:
                            scores(i)
                        if 1 <= i <= 18:
                            p_transpose(i - 1)
                        if i >= 2:
                            values(i - 2)
                    pe.wait_ge(*after("gd_sig"))
                    pe.wait_ge(*after("lora_loaded", 2))
                    pe.wait_ge(*after("exp", (17, 1)))
                    for c in range(HC):
                        T.matmul(PS[:, c, 0:TOK], gup[:, c * P:(c + 1) * P], tanh2[0:64, 1, :], start=True, stop=True).then_inc(*made("gate_mm", c))
                    for c in range(HC):
                        pe.wait_ge(*after("kk_sq", c))
                        if c == 0:
                            pe.wait_ge(*after("pdT", 17))
                        T.matmul(PS[:, 3 + c, 0:TOK], bones, (LW, EI, EX)[c][:, :], start=True, stop=True).then_inc(*made("kk_ss", c))
                    for t in range(TILES):
                        pe.wait_ge(*after("o_n", t))
                        pe.wait_ge(*after("gate", t))
                        for c in range(HC):
                            mm = T.transpose(PS[:, t, c * P:(c + 1) * P], osb[:, t, c * P:(c + 1) * P], ident)
                        mm.then_inc(*made("o_tr", t))
                    pe.wait_ge(*after("kk_sqrt", 2))
                    pe.wait_ge(*after("o", 2))
                    for dc in range(2):
                        fs = slice(FNET0 + dc * P, FNET0 + (dc + 1) * P)
                        T.matmul(PS[:, 4 + 2 * dc, 0:256], tok[:, 0, fs], dft_prompt, start=True, stop=True)
                        for t in range(2):
                            mm = T.matmul(PS[:, 5 + 2 * dc, :], tok[:, 1 + t, fs], dft_sample[:, t, :], start=(t == 0), stop=(t == 1))
                        mm.then_inc(*made("fz_mm", dc))
                    for dc in range(2):
                        pe.wait_ge(*after("fz", (dc, 1)))
                        pe.wait_ge(*after("y_attn", dc))
                        for m in range(2):
                            T.matmul(PS[:, dc, 0:SEQ], dft_dim[:, m, :], fz[:, dc, m * SEQ:(m + 1) * SEQ], start=(m == 0), stop=(m == 1))
                        for m in range(2):
                            mm = T.matmul(PS[:, dc, SEQ:TOK], dft_dim[:, m, :], fz[:, dc, 256 + m * DEC:256 + (m + 1) * DEC], start=(m == 0), stop=(m == 1))
                        mm.then_inc(*made("fnet_mm", dc))

                    for c in range(HC):
                        cs = slice(c * P, (c + 1) * P)
                        for d in range(2):
                            if (c, d) == (0, 0):
                                pe.wait_ge(*after("wd_tanh"))
                                pe.wait_ge(*after("y_fnet", 1))
                            else:
                                pe.wait_ge(*after("a_tanh", (c, 0) if d else (c - 1, 1)))
                                if d == 0:
                                    pe.wait_ge(*after("V", (c - 1, 6, 2)))
                            r = slice(32 * d, 32 * d + 32)
                            T.matmul(PS[:, 0, 0:TOK], lora[r, cs], tanh2[r, 0, :], start=True, stop=True)
                            r = slice(64 + 32 * d, 96 + 32 * d)
                            T.matmul(PS[:, 1, 0:TOK], lora[r, cs], uT[r, 9, :], start=True, stop=True).then_inc(*made("lora_mm", (c, d)))
                        pe.wait_ge(*after("b_scaled", (c, 1)))
                        pe.wait_ge(*after("y_attn", 2))
                        if c >= 1:
                            pe.wait_ge(*after("XT", (c - 1, 6, 2)))
                            pe.wait_ge(*after("stmp", (c - 1, 1)))
                        for i, src in enumerate((KT, BT)):
                            for d in range(2):
                                for g in range(2):
                                    t = STEP_TILE[g][d]
                                    mm = T.transpose(PS[:, 2 + i, (2 * d + g) * P:(2 * d + g + 1) * P], src[:, d, t * P:(t + 1) * P], ident)
                        mm.then_inc(*made("kt_tr", c))
                        pe.wait_ge(*after("bonus_r", c))
                        if c == 0:
                            pe.wait_ge(*after("fz", (1, 1)))
                        else:
                            pe.wait_ge(*after("stmp", (c - 1, 1)))
                        T.matmul(PS[:, 4, 0:TOK], bones, gsum[:, :], start=True, stop=True).then_inc(*made("bonus_mm", c))
                        pe.wait_ge(*after("r", (c, 1)))
                        pe.wait_ge(*after("kap", (c, 1)))
                        for g in range(3):
                            for n, rhs in enumerate((KAP, RT)):
                                if g:
                                    pe.wait_ge(*after("A", (c, g - 1, n)))
                                elif n == 0:
                                    pe.wait_ge(*after("a_tanh", (c, 1)))
                                else:
                                    pe.wait_ge(*after("fz", (1, 1)) if c == 0 else after("y_raw", c - 1))
                                for i, lhs in enumerate((BT, KT)):
                                    for d in range(2):
                                        t = STEP_TILE[g][d]
                                        ts = slice(t * P, (t + 1) * P)
                                        for h in range(2):
                                            hs = slice(h * HD, (h + 1) * HD)
                                            mm = T.matmul(PS[:, abank(2 * g + n, h), (2 * i + d) * P:(2 * i + d + 1) * P],
                                                          lhs[hs, d, ts], rhs[hs, d, ts], start=True, stop=True)
                                mm.then_inc(*made("A_mm", (c, g, n)))
                        if c == 0:
                            pass
                        pe.wait_ge(*after("A", (c, 2, 1)))
                        pe.wait_ge(*after("btok", c))
                        pe.wait_ge(*after("bonus", c))
                        for j in range(LEVELS):
                            def join(j, g):
                                if j == 0:
                                    pe.wait_ge(*after("A1", (c, g)))
                                    pe.wait_ge(*after("V", (c, 0, g - 2)) if g == 2 else after("A", (c, 2, 1)))
                                else:
                                    pe.wait_ge(*after("V", (c, 0, g)) if j == 1 else after("X", (c, j - 1, g)))
                                    pj, pg = divmod(3 * j + g - 2, 3)
                                    pe.wait_ge(*after("V", (c, pj, pg)))
                                for u in range(4):
                                    mm = T.matmul(PS[:, vbank(j, g), u * P:(u + 1) * P], AKB[:, g, u, :], ident if j == 0 else X[:, g, u, :],
                                                  start=True, stop=True)
                                mm.then_inc(*made("V_mm", (c, j, g)))

                            def merge(j, g):
                                pe.wait_ge(*after("V", (c, j, g)))
                                if j == 1:
                                    pe.wait_ge(*after("XT0", (c, g, 1)))
                                else:
                                    pe.wait_ge(*after("XT", (c, j - 1, g)))
                                if 3 * j + g - 2 >= 3:
                                    pj, pg = divmod(3 * j + g - 2, 3)
                                    pe.wait_ge(*after("XT", (c, pj, pg)))
                                b = xbank(j, g)
                                if j < LEVELS - 1:
                                    for u in range(4):
                                        mm = T.matmul(PS[:, b, u * P:(u + 1) * P], XT[:, g, u, :], VB[:, g, u, :], start=True, stop=True)
                                    mm.then_inc(*made("X_mm", (c, j, g)))
                                for u in range(4):
                                    mm = T.matmul(PS[:, b + 1, u * P:(u + 1) * P], VB[:, g, u, :], XT[:, g, u, :], start=True, stop=True)
                                mm.then_inc(*made("XT_mm", (c, j, g)))

                            for g in range(3):
                                join(j, g)
                                if j >= 1 and g >= 1:
                                    merge(j, g - 1)
                            if j >= 1:
                                merge(j, 2)
                        pe.wait_ge(*after("XT", (c, LEVELS - 1, 2)))
                        for g in range(3):
                            if g == 0:
                                pe.wait_ge(*after("A", (c, 2, 1)))
                            else:
                                pe.wait_ge(*after("Z", (c, g - 1)))
                                pe.wait_ge(*after("SH", (c, g, 1)))
                            for d in range(2):
                                t = STEP_TILE[g][d]
                                for h in range(2):
                                    hs = slice(h * HD, (h + 1) * HD)
                                    u = 2 * d + h
                                    o = PS[:, (6, 4)[h], d * HD:(d + 1) * HD]
                                    if g:
                                        T.matmul(o, KAP[hs, d, t * P:(t + 1) * P], SH[hs, g, d, :], start=True, stop=False)
                                    mm = T.matmul(o, AKV[:, g, u, :], vtok[:, t, c * P + h * HD:c * P + (h + 1) * HD], start=(g == 0), stop=True)
                            mm.then_inc(*made("Z_mm", (c, g)))
                            pe.wait_ge(*after("Z", (c, g)))
                            if g:
                                pe.wait_ge(*after("U", (c, g - 1)))
                            for u in range(4):
                                mm = T.matmul(PS[:, 7, u * HD:(u + 1) * HD], XT[:, g, u, :], zs[:, u * HD:(u + 1) * HD], start=True, stop=True)
                            mm.then_inc(*made("U_mm", (c, g)))
                            pe.wait_ge(*after("U", (c, g)))
                            if g == 1:
                                pe.wait_ge(*after("Sfin", (c, 1)))
                            if g < 2:
                                for d in range(2):
                                    t = STEP_TILE[g][d]
                                    for h in range(2):
                                        hs = slice(h * HD, (h + 1) * HD)
                                        u = 2 * d + h
                                        o = PS[hs, 3, d * HD:(d + 1) * HD]
                                        T.matmul(o, ktok[:, d, g, hs], vtok[:, t, c * P + h * HD:c * P + (h + 1) * HD], start=True, stop=False)
                                        mm = T.matmul(o, btok[:, d, g, hs], usb[:, g, u * HD:(u + 1) * HD], start=False, stop=True)
                                mm.then_inc(*made("S_mm", (c, g)))
                        for h in range(2):
                            hs = slice(h * HD, (h + 1) * HD)
                            for t in range(TILES):
                                ts = slice(t * P, (t + 1) * P)
                                ops = []
                                for d in range(2):
                                    g = [st[d] for st in STEP_TILE].index(t)
                                    u = 2 * d + h
                                    if g:
                                        ops.append((SH[hs, g, d, :], RT[hs, d, ts]))
                                    ops.append((vtok[:, t, c * P + h * HD:c * P + (h + 1) * HD], ARV[:, g, u, :]))
                                    ops.append((usb[:, g, u * HD:(u + 1) * HD], ARB[:, g, u, :]))
                                for i, (lhs, rhs) in enumerate(ops):
                                    mm = T.matmul(PS[hs, 5 + h, ts], lhs, rhs, start=(i == 0), stop=(i == len(ops) - 1))
                        mm.then_inc(*made("Y_mm", c))
                    pe.wait_ge(*after("Sfin", (2, 1)))
                    pe.wait_ge(*after("U", (2, 2)))
                    pe.wait_ge(*after("y_raw", 2))
                    for d in range(2):
                        for c in range(HC):
                            mm = T.transpose(PS[0:HD, 6 + d, c * P:(c + 1) * P], Sfin[:, c, d, :], ident)
                        mm.then_inc(*made("st_tr", d))
                    for c in range(HC):
                        pe.wait_ge(*after("y_raw", c))
                        if c == 0:
                            pe.wait_ge(*after("V", (2, 6, 2)))
                            pe.wait_ge(*after("XT", (2, 6, 2)))
                        T.matmul(PS[:, c, 0:TOK], bones, yT[:, c, :], start=True, stop=True).then_inc(*made("gn_mean_mm", c))
                    for c in range(HC):
                        pe.wait_ge(*after("gn_sq", c))
                        T.matmul(PS[:, 3 + c, 0:TOK], bones, (KAP[:, 0, :], KAP[:, 1, :], RT[:, 0, :])[c], start=True, stop=True).then_inc(*made("gn_var_mm", c))
                    for m in range(KC):
                        s = S_OUT + m // 2
                        w = need(s)
                        if m == 0:
                            pe.wait_ge(*after("y_rwkv", 2))
                            pe.wait_ge(*after("gn_sqrt", 2))
                        if m >= 4:
                            pe.wait_ge(*after("x1", (m - 4, 1)))
                        for k in range(KC):
                            mm = T.matmul(PS[:, m % 4, 0:TOK], w[:, k, (m % 2) * P:(m % 2 + 1) * P], yT[:, k, :], start=(k == 0), stop=(k == KC - 1))
                        mm.then_inc(*made("out_mm", m))
                    pe.wait_ge(*after("state_rows", 1))
                    norm_pe(pe, "n2")
                    for f in range(FC):
                        w = need(S_FI + f)
                        if f == 0:
                            pe.wait_ge(*after("n2_h", (KC - 1, 1)))
                        if f >= 2:
                            pe.wait_ge(*after("ff", f - 2))
                        for b in range(2):
                            for k in range(KC):
                                mm = T.matmul(PS[:, 2 * (f % 2) + b, 0:TOK], w[:, k, b * P:(b + 1) * P], hT[:, k, :], start=(k == 0), stop=(k == KC - 1))
                        mm.then_inc(*made("ff_mm", f))
                    for q in range(2 * FC):
                        half, k = divmod(q, FC)
                        s, j = S_FO + q // 4, q % 4
                        w = need(s)
                        if half == 0:
                            pe.wait_ge(*after("ff", k))
                        if q == 0:
                            pe.wait_ge(*after("n2_sqrt"))
                        for m in range(4):
                            mm = T.matmul(PS[:, 4 - 4 * half + m, 0:TOK], w[:, j, m * P:(m + 1) * P], ffT[:, k, :], start=(k == 0), stop=(k == FC - 1))
                        if j == 3:
                            mm.then_inc(*made("ffo_mm", s - S_FO))
                        elif k == FC - 1:
                            mm.then_inc(*made("ffo_half"))

            reset([sems[n] for n in sems if n not in prologue_names])

        with nc.Block() as block:
            @block.scalar
            def _(act):
                norm_act(act, "n3")

            @block.tensor
            def _(pe):
                norm_pe(pe, "n3")
                for t in range(TILES):
                    for half in range(2):
                        b = (2 * t + half) % 4
                        if 2 * t + half >= 4:
                            pe.wait_ge(*after("y_rows", 2 * t + half - 4))
                        for k in range(4):
                            kk_ = 4 * half + k
                            if t == 0:
                                pe.wait_ge(*after("n3_h", kk_))
                            mm = nc.tensor.transpose(PS[:, b, k * P:(k + 1) * P], hT[:, kk_, t * P:(t + 1) * P], ident)
                        mm.then_inc(*made("y_tr", 2 * t + half))

            @block.vector
            def _(dve):
                dve.wait_ge(*after("n3_sqrt"))
                nc.vector.reciprocal(rstd[:, :], rstd[:, :]).then_inc(*made("n3_rstd"))
                dve.wait_ge(*after("n3_rstd"))
                for k in range(KC):
                    nc.vector.scalar_tensor_tensor(hT[:, k, :], xT[:, k, :], fing[:, k:k + 1], rstd[:, :], ALU.mult,
                                                   ALU.mult).then_inc(*made("n3_h", k))
                for i in range(6):
                    dve.wait_ge(*after("y_tr", i))
                    if i == 0:
                        dve.wait_ge(*after("n3_ss"))
                    nc.vector.tensor_copy(xin[:, i // 2, (i % 2) * 512:(i % 2) * 512 + 512], PS[:, i % 4, :]).then_inc(*made("y_rows", i))

            @block.sync
            def _(sp):
                sp.wait_ge(*after("y_rows", 1))
                sp.dma_start(a["out_p"][0], xin[:, 0, :]).then_inc(*loaded("y_stored"))
                for t in range(1, TILES):
                    sp.wait_ge(*after("y_rows", 2 * t + 1))
                    sp.dma_start(a["out_x"][0, (t - 1) * P:t * P, :], xin[:, t, :]).then_inc(*loaded("y_stored", t))
                sp.wait_ge(*after("y_stored", 2))


def kernel(**inputs):
    import numpy as _np
    import concourse.bacc as _bacc
    from concourse.bass_utils import run_bass_kernel_spmd as _run

    lay = {
        "x_prompt": None, "x_sample": None, "c": None, "c_ctx": None, "norm1_g": None, "norm2_g": None,
        "final_norm_g": None, "w_mod": None, "b_mod": None, "w_in": None, "w_out": None, "shift_mu": None,
        "decay_w0": None, "decay_up": None, "iclr_a0": None, "iclr_up": None, "gate_up": None, "k_k": None,
        "k_a": None, "r_k": None, "lnx_g": None, "lnx_b": None, "diff_lambda": None, "subln_g": None,
        "w_ffn_in": None, "w_ffn_out": None,
        "state": ("state_rwkv", (DEPTH, 2, HEADS, HD, HD)),
        "cache_k": ("cache_diff_k", (DEPTH, P, DR)),
        "cache_v": ("cache_diff_v", (DEPTH, P, DR)),
    }
    arrays = {}
    for name, how in lay.items():
        v = _np.ascontiguousarray(inputs[how[0] if how else name])
        arrays[name] = v.reshape(how[1]) if how else v
    arrays["tables"] = packed_tables()
    arrays["lam_init"] = lam_table()
    outs = {"out_p": (1, SEQ, D), "out_x": (1, DEC, D), "out_s": (DEPTH, 2, HEADS, HD, HD),
            "out_k": (DEPTH, SEQ, DR), "out_v": (DEPTH, SEQ, DR)}
    counts = {}
    for _ in range(2):
        nc = _bacc.Bacc("TRN2", target_bir_lowering=False, num_devices=1)
        a = {n: nc.dram_tensor("in_" + n, v.shape, F32, kind="ExternalInput").ap() for n, v in arrays.items()}
        a.update({n: nc.dram_tensor(n, s, F32, kind="ExternalOutput").ap() for n, s in outs.items()})
        build(nc, a, counts)
    r = _run(nc, [{"in_" + n: v for n, v in arrays.items()}], core_ids=[0]).results[0]
    return (r["out_p"], r["out_x"], r["out_s"].reshape(1, DEPTH, 2, HEADS, HD, HD),
            r["out_k"].reshape(1, DEPTH, SEQ, HEADS, 2, DQK), r["out_v"].reshape(1, DEPTH, SEQ, HEADS, HD))
```

```python
import math
from contextlib import ExitStack

import numpy as np

import concourse.bass as bass
from concourse import mybir

F32 = mybir.dt.float32
F32R = mybir.dt.float32r
ALU = mybir.AluOpType
ACT = mybir.ActivationFunctionType
AX = mybir.AxisListType

P = 128
D = 1024
KC = D // P
DEPTH = 2
SEQ, DEC = 128, 256
TOK = SEQ + DEC
TILES = TOK // P
HD = 64
DR = 384
HC = DR // P
HEADS = DR // HD
DQK = 32
NR = 1344
FNET0 = 1152
NTOK = 1408
DIN = NR + NTOK
DFF = 2816
FC = DFF // P
GRID_W = 64
RMS_EPS, GN_EPS, SUBLN_EPS = 1e-6, 64e-5, 1e-5
DECAY = math.exp(-0.5)
QSCALE = DQK ** -0.5
GROUPS = ((0, SEQ), (SEQ, TOK))
RING = 4
LEVELS = 7

VEC = {}
_row = 0
for _name, _n in (("norm1_g", 8), ("norm2_g", 8), ("b_mod", 48), ("decay_w0", 6), ("iclr_a0", 6), ("k_k", 3),
                  ("k_a", 3), ("r_k", 3), ("lnx_g", 3), ("lnx_b", 3), ("subln_g", 1), ("mu0", 11), ("mu1", 11)):
    VEC[_name] = _row
    _row += _n
SH1, SC1, G1, SH2, SC2, G2 = range(0, 48, 8)

S_MOD_A, S_R, S_GD, S_T, S_MOD_B, S_OUT, S_FFN = 0, 8, 13, 14, 19, 35, 39
HALF = FC // 2
FO_SLOTS = -(-2 * HALF // 4)
FFN_SLOTS = HALF + FO_SLOTS
SLOTS = S_FFN + 2 * FFN_SLOTS
SPLIT = [*range(S_R, S_MOD_B), *range(S_OUT, SLOTS)]
MOD_PAIRS_A = 4
MOD_PAIRS_SOLVE = ((4, 5, 6), (7, 8, 9), (10, 11))

STAGES = {
    "vector_setup": "vec dvec lam_dots mod_sum mods gmod lam",
    "vector_norm1": "n1_rstd n1_scaled",
    "vector_norm2": "n2_rstd n2_scaled",
    "vector_shift": "u_prev shifted",
    "vector_layouts": "gd_sig vtok S0T kT",
    "vector_attention": "max neg_max rinv rlam p1 pdiff o",
    "vector_subnorm": "o_sq o_ms o_rinv o_n",
    "vector_keys": "kk_raw kk_sq kk_den kk",
    "vector_decay": "LW sum nh EI EX kap r k_scaled b_scaled",
    "vector_bonus": "bonus_k bonus_r bonus",
    "vector_solve": "Z Sfin stmp SH",
    "vector_groupnorm": "gn_d gn_sq gn y_rwkv",
    "vector_ffn": "ff_silu ff",
    "vector_prologue": "xT cond_cols final_g cond_half cond",
    "scalar_inputs": "u_copy u_own wd_tanh gd_tanh",
    "scalar_sqrt": "o_sqrt kk_sqrt",
    "scalar_outputs": "y_attn fz y_fnet gate",
    "scalar_decay": "w_tanh a_tanh e_kap e_r e_3 e_tot",
    "scalar_keys": "ktok btok",
    "scalar_merge": "X XT",
    "scalar_solve": "U y_raw state_rows",
    "pool_rope": "rope_cos rope_sin rope",
    "pool_keys": "a b ka kd",
    "pool_merge": "A1 XT0",
    "vector_low": "n1_low n2_low y_lo ff_lo",
    "tensor_norm": "vec_tr n1_ss n2_ss",
    "tensor_layouts": "v_tr s0_tr q_tr k_tr",
    "tensor_attention": "scores p_tr pv",
    "tensor_mixed": "gate_mm kk_ss o_tr fz_mm fnet_mm",
    "tensor_decay": "lora_mm kt_tr bonus_mm",
    "tensor_merge": "V_mm X_mm XT_mm",
    "tensor_solve": "Z_mm U_mm S_mm Y_mm st_tr",
    "tensor_groupnorm": "gn_mean_mm gn_var_mm",
    "tensor_ffn_out": "ffo_mm ffo_half",
}
STAGE_OF = {step: stage for stage, steps in STAGES.items() for step in steps.split()}

STEP_TILE = ((0, 0), (1, 2), (2, 1))


def tables():
    i = np.arange(P)
    eye = np.eye(P)
    t = {"ident": eye, "ones": np.ones((P, P)), "bones": (i[:, None] // HD == i[None] // HD) * 1.0}
    s, q = i[:, None], i[None]
    t["amask"] = np.concatenate([s < q, s > q, s <= q, s >= q], 1) * 1.0
    lm = []
    for j in range(LEVELS):
        b = 1 << j
        low = (s // (2 * b) == q // (2 * b)) & (s // b % 2 == 1) & (q // b % 2 == 0)
        lm += [eye - low, eye - low.T]
    t["lmask"] = np.concatenate(lm, 1)
    t["smask"] = np.tile((np.arange(TOK) % P != 0) * 1.0, (P, 1))
    f = np.float32
    pos = np.arange(DEC)
    row, col = (pos // GRID_W).astype(f), (pos % GRID_W).astype(f)
    inv = (1.0 / (f(10000.0) ** (np.arange(8, dtype=f) / f(8)))).astype(f)
    ang = np.stack([row[:, None] * inv, col[:, None] * inv], 1)
    cs, sn = np.cos(ang), np.sin(ang)
    cos = np.stack([cs, cs], 2).reshape(2, P, 32)
    sin = np.stack([-sn, sn], 2).reshape(2, P, 32)
    t["cos"] = cos.transpose(1, 0, 2).reshape(P, 64)
    t["sin"] = sin.transpose(1, 0, 2).reshape(P, 64)

    def dft(n):
        a = 2 * np.pi * (np.outer(np.arange(n), np.arange(n)) % n) / n
        return np.cos(a) / np.sqrt(n), np.sin(a) / np.sqrt(n)

    c, s_ = dft(SEQ)
    t["dft_prompt"] = np.concatenate([c, s_], 1)
    c, s_ = dft(DEC)
    t["dft_sample"] = np.concatenate([c, s_], 1).reshape(2, P, 512).transpose(1, 0, 2).reshape(P, 1024)
    c, s_ = dft(HD)
    z = np.zeros((HD, HD))
    t["dft_dim"] = np.concatenate([np.block([[c, z], [z, c]]), -np.block([[s_, z], [z, s_]])], 1)
    return t


TABLES = tables()
TABLE_AT = {}
_at = 0
for _k, _v in TABLES.items():
    TABLE_AT[_k] = (_at, _v.shape[1])
    _at += _v.shape[1]
NTABLE = _at


def packed_tables():
    return np.concatenate(list(TABLES.values()), 1).astype(np.float32)


def lam_table():
    li = np.array([0.8 - 0.6 * math.exp(-0.3 * l) for l in range(DEPTH)])
    return np.repeat(np.stack([li, 1 - li], 1)[:, None], P, 1).astype(np.float32)


def build(nc, a, counts):
    ctx = ExitStack()
    with ctx:
        def sb(name, shape, dt=F32):
            return ctx.enter_context(nc.sbuf_tensor(name, shape, dt))

        sems = {}
        seen = {}
        counted = bool(counts)

        def sem(name):
            if name not in sems:
                sems[name] = ctx.enter_context(nc.semaphore(name))
            return sems[name]

        def made(name, key=0, by=1):
            stage = STAGE_OF.get(name, name)
            seen[stage] = seen.get(stage, 0) + by
            counts[name, key] = seen[stage]
            return sem(stage), by

        def loaded(name, key=0):
            return made(name, key, 16)

        def after(name, key=0):
            return sem(STAGE_OF.get(name, name)), counts[name, key] if counted else 1

        tab = sb("tab", [P, NTABLE])

        def table(name):
            at, n = TABLE_AT[name]
            return tab[:, at:at + n]

        ident, ones, bones = table("ident"), table("ones"), table("bones")
        amask = table("amask").rearrange("p (m t) -> p m t", m=4)
        lmask = table("lmask").rearrange("p (j d t) -> p j d t", j=LEVELS, d=2)
        smask = table("smask")
        cos = table("cos").rearrange("p (t n) -> p t n", t=2)
        sin = table("sin").rearrange("p (t x h n) -> p t x h n", t=2, x=2, h=2)
        dft_prompt = table("dft_prompt")
        dft_sample = table("dft_sample").rearrange("p (t n) -> p t n", t=2)
        dft_dim = table("dft_dim").rearrange("p (m n) -> p m n", m=2)

        def region(name, shape):
            nc.bump_sbuf((-nc.sbuf_base) % 32) if nc.sbuf_base % 32 else None
            at = nc.sbuf_base
            return sb(name, shape), at

        def split(name, shape, at, words=0):
            return nc.alloc_sbuf_tensor_at(name, shape, F32R, offset=at + 4 * words)

        xT = sb("xT", [P, KC, TOK])
        hT, hT_at = region("hT", [P, KC, TOK])
        h_hi = split("h_hi", [P, KC, TOK], hT_at)
        h_lo = sb("h_lo", [P, KC, TOK], F32R)
        yT = sb("yT", [P, KC, TOK])
        ring = sb("ring", [P, RING, 2048])
        big, big_at = region("big", [P, FC * TOK])
        y_hi = split("y_hi", [P, KC, TOK], big_at)
        y_lo = split("y_lo", [P, KC, TOK], big_at, KC * TOK)
        ff_hi = split("ff_hi", [P, HALF, TOK], big_at)
        ff_lo = split("ff_lo", [P, HALF, TOK], big_at, HALF * TOK)
        tok = big[:, 0:TILES * NTOK].rearrange("p (t n) -> p t n", t=TILES)
        uT = big[:, TILES * NTOK:].rearrange("p (c t) -> p c t", c=11)
        xsq = big[:, 0:KC * TOK].rearrange("p (k t) -> p k t", k=KC)
        xin = big[:, 0:TILES * D].rearrange("p (t n) -> p t n", t=TILES)

        share, share_at = region("share", [P, 10752])
        w_hi = split("w_hi", [P, 2, 2048], share_at)
        w_lo = split("w_lo", [P, 2, 2048], share_at, 4096)
        cut = [0]

        def part(n):
            cut[0] += n
            return share[:, cut[0] - n:cut[0]]

        rot = part(1536).rearrange("p (t n) -> p t n", t=2)
        rot2 = part(1536).rearrange("p (t n) -> p t n", t=2)
        qT = part(HC * TOK).rearrange("p (c t) -> p c t", c=HC)
        kT = part(HC * 512).rearrange("p (c t) -> p c t", c=HC)
        prob = part(1536).rearrange("p (b m t) -> p b m t", b=2, m=2)
        pdiff = part(768).rearrange("p (b t) -> p b t", b=2)
        pdT = part(768).rearrange("p (b t) -> p b t", b=2)
        osb = part(TILES * DR).rearrange("p (t n) -> p t n", t=TILES)
        ctxk = part(DR)
        ctxv = part(DR)
        cut[0] = 0
        AKB, AKV, ARB, ARV = (part(1536).rearrange("p (g u t) -> p g u t", g=3, u=4) for _ in range(4))
        X, XT, VB = (part(1536).rearrange("p (g u t) -> p g u t", g=3, u=4) for _ in range(3))

        kk = yT[:, 0:HC, :]
        vtok = sb("vtok", [P, TILES, DR])
        bonus = hT[:, 0:HC, :]
        gate = hT[:, HC:2 * HC, :]
        late = sb("late", [P, 2, 2, TOK])
        KAP, RT = late[:, 0], late[:, 1]
        fz = late[:, :, :, :].rearrange("p a d t -> p a (d t)")
        BT, KT, KD = (sb(n, [P, 2, TOK]) for n in ("BT", "KT", "KD"))
        LW, EI, EX, E3, AA = (sb(n, [P, TOK]) for n in ("LW", "EI", "EX", "E3", "AA"))
        ktok = sb("ktok", [P, 2, 2, P])
        btok = sb("btok", [P, 2, 2, P])
        upad = late[:, :, :, :].rearrange("p a d t -> p (a d t)")[:, 0:2 * (TOK + 3)].rearrange("p (b t) -> p b t", b=2)
        tanh2 = sb("tanh2", [P, 2, TOK])
        gsum = rstd = sb("gsum", [P, TOK])

        vrow = LW[:, 0:P]
        vec = sb("vec", [P, P])
        mods = sb("mods", [P, 48, 2])
        gmod = sb("gmod", [P, 2, KC, 2])
        scond = sb("scond", [P, KC, 32])
        fing = sb("fing", [P, KC])
        dvec = sb("dvec", [P, 64])
        muc, w0h, a0h, omka, subs = (dvec[:, 0:11], dvec[:, 11:17], dvec[:, 17:23], dvec[:, 23:26], dvec[:, 26:27])
        eps = sb("eps", [P, 4])
        lora = sb("lora", [P, DR])
        gup = sb("gup", [HD, DR])
        lrow = E3[:, 0:P]
        lprod = sb("lprod", [P, 2, DQK])
        lsum = sb("lsum", [P, 8])
        lamc = sb("lamc", [P, 2])
        lam = sb("lam", [P, 1])
        amax = sb("amax", [P, 2, 2])
        nmax = sb("nmax", [P, 2, 2])
        rsum = sb("rsum", [P, 2, 2])
        rinv = sb("rinv", [P, 2, 2])
        onorm = sb("onorm", [P, 18])
        zs = AA[:, 0:256]
        usb = hT[:, 6:8, :].rearrange("p k t -> p (k t)").rearrange("p (g n) -> p g n", g=3)
        nh = sb("nh", [P, 2, 3])
        et = sb("et", [P, 2, 3])
        sin_rows = BT[0:HD, :, :]
        S0T = sb("S0T", [P, 2, HC, HD])
        SH = sb("SH", [P, 3, 2, HD])
        stmp = sb("stmp", [P, 2, HD])
        Sfin = sb("Sfin", [P, HC, 2, HD])
        sout = KD[0:HD, :, :]
        PS = ctx.enter_context(nc.psum_tensor("PS", [P, 8, 512], F32))

        def layer(x, l):
            s = x[bass.ds(l, 1)]
            n = len(x.shape)
            names = " ".join("bcdefg"[:n - 1])
            first = names.split()[0]
            rest = " ".join(names.split()[1:])
            return s.rearrange(f"o {names} -> (o {first}) {rest}")

        def reset(all_sems):
            with nc.Block() as block:
                @block.sync
                def _(sp):
                    for x in all_sems:
                        sp.sem_clear(x)

        with nc.Block() as block:
            @block.sync
            def _(sp):
                sp.dma_start(tab[:, :], a["tables"]).then_inc(*loaded("tables"))
                sp.dma_start(xin[:, 0, :], a["x_prompt"][0]).then_inc(*loaded("x_loaded"))
                sp.dma_start(xin[:, 1:3, :], a["x_sample"][0].rearrange("(t p) n -> p t n", p=P)).then_inc(*loaded("x_loaded", 1))

            @block.scalar
            def _(act):
                act.wait_ge(*after("vrow_zero"))
                for i, n in enumerate(("c_ctx", "c", "final_norm_g")):
                    src = a[n][0] if n == "c" else a[n]
                    act.dma_start(vrow[8 * i:8 * i + 8, :], src.rearrange("(k p) -> k p", p=P)).then_inc(*loaded("cond_loaded", i))
                act.wait_ge(*after("cond_cols"))
                act.wait_ge(*after("pads", 0))
                nc.scalar.activation(scond[:, :, 0:2].rearrange("p k c -> p c k"),
                                     vec[:, 0:16].rearrange("p (c k) -> p c k", c=2), ACT.Tanh,
                                     scale=0.5).then_inc(*made("cond_tanh"))

            @block.gpsimd
            def _(pool):
                nc.gpsimd.memset(vrow[:, :], 0.0).then_inc(*made("vrow_zero"))
                nc.gpsimd.memset(scond[:, :, :], 0.0).then_inc(*made("pads", 0))
                nc.gpsimd.memset(eps[:, 0:1], RMS_EPS).then_inc(*made("pads", 1))
                nc.gpsimd.memset(eps[:, 1:2], GN_EPS).then_inc(*made("pads", 2))
                nc.gpsimd.memset(eps[:, 2:3], SUBLN_EPS).then_inc(*made("pads", 3))
                nc.gpsimd.memset(eps[:, 3:4], 0.0).then_inc(*made("pads", 4))

            @block.tensor
            def _(pe):
                pe.wait_ge(*after("tables"))
                pe.wait_ge(*after("x_loaded", 1))
                for k in range(KC):
                    if k >= 4:
                        pe.wait_ge(*after("xT", k - 4))
                    for t in range(TILES):
                        mm = nc.tensor.transpose(PS[:, k % 4, t * P:(t + 1) * P], xin[:, t, k * P:(k + 1) * P], ident)
                    mm.then_inc(*made("xT_mm", k))
                pe.wait_ge(*after("cond_loaded", 2))
                nc.tensor.transpose(PS[:, 4, 0:P], vrow[:, :], ident).then_inc(*made("cond_mm"))

            @block.vector
            def _(dve):
                for k in range(KC):
                    dve.wait_ge(*after("xT_mm", k))
                    nc.vector.tensor_copy(xT[:, k, :], PS[:, k % 4, 0:TOK]).then_inc(*made("xT", k))
                dve.wait_ge(*after("cond_mm"))
                nc.vector.tensor_copy(vec[:, :], PS[:, 4, 0:P]).then_inc(*made("cond_cols"))
                dve.wait_ge(*after("cond_cols"))
                nc.vector.tensor_copy(fing[:, :], vec[:, 16:24]).then_inc(*made("final_g"))
                dve.wait_ge(*after("cond_tanh"))
                for i in range(2):
                    nc.vector.tensor_scalar(lprod[:, i, 0:8], scond[:, :, i], 1.0, 0.5, ALU.add, ALU.mult).then_inc(*made("cond_half", i))
                dve.wait_ge(*after("cond_half", 1))
                for i in range(2):
                    nc.vector.tensor_tensor(scond[:, :, i], lprod[:, i, 0:8], vec[:, 8 * i:8 * i + 8], ALU.mult).then_inc(*made("cond", i))

        reset(list(sems.values()))
        prologue_names = set(sems)

        def norm_act(act, n, eps_col=0):
            for k in range(KC):
                nc.scalar.activation(xsq[:, k, :], xT[:, k, :], ACT.Square).then_inc(*made(f"{n}_sq", k))
            act.wait_ge(*after(f"{n}_ss"))
            nc.scalar.activation(rstd[:, :], PS[:, 6, 0:TOK], ACT.Sqrt, bias=eps[:, eps_col:eps_col + 1],
                                 scale=1.0 / D).then_inc(*made(f"{n}_sqrt"))

        def norm_pe(pe, n):
            for k in range(KC):
                pe.wait_ge(*after(f"{n}_sq", k))
                mm = nc.tensor.matmul(PS[:, 6, 0:TOK], ones, xsq[:, k, :], start=(k == 0), stop=(k == KC - 1))
            mm.then_inc(*made(f"{n}_ss"))

        with nc.Fori(0, DEPTH) as l:
            first_sems = set(sems)
            with nc.Block() as block:
                def layer2(x, l, p=P):
                    return x[bass.ds(l, 1)].rearrange("o (k p) -> (o k) p", p=p)

                def flat(x):
                    return x.rearrange("p u t -> p (u t)")

                def tok_job(n):
                    if n < 3:
                        return NTOK - P, P, n
                    s, t = divmod(n - 3, 3)
                    return 256 * s, 256, t

                def xbank(j, g):
                    return 2 if (3 * j + g) % 2 else 4

                def vbank(j, g):
                    return (3 * j + g) % 2

                def copy_pdT(act, i):
                    nk = 128 if i < HEADS else 384
                    act.wait_ge(*after("p_tr", i))
                    if i >= 2:
                        act.wait_ge(*after("pv", i - 2))
                    nc.scalar.activation(pdT[:, i % 2, 0:nk], PS[:, 4 + i % 2, 0:nk], ACT.Copy).then_inc(*made("pdT", i))

                prob_flat = prob.rearrange("p b m t -> p (b m t)")

                def abank(n, h):
                    return ((0, 1), (5, 6))[n % 2][h]

                def diff(dve, i):
                    V = nc.vector
                    t, h = divmod(i, HEADS)
                    nk = 128 if t == 0 else 384
                    dve.wait_ge(*after("exp", (i, 1)))
                    V.reciprocal(rinv[:, i % 2, :], rsum[:, i % 2, :]).then_inc(*made("rinv", i))
                    dve.wait_ge(*after("rinv", i))
                    V.tensor_scalar(rinv[:, i % 2, 1:2], rinv[:, i % 2, 1:2], lam[:, 0:1], None, ALU.mult).then_inc(*made("rlam", i))
                    dve.wait_ge(*after("rlam", i))
                    V.tensor_scalar(prob[:, i % 2, 1, 0:nk], prob[:, i % 2, 1, 0:nk], rinv[:, i % 2, 1:2], None, ALU.mult).then_inc(*made("p1", i))
                    dve.wait_ge(*after("p1", i))
                    if i >= 2:
                        dve.wait_ge(*after("p_tr", i - 2))
                    V.scalar_tensor_tensor(pdiff[:, i % 2, 0:nk], prob[:, i % 2, 0, 0:nk], rinv[:, i % 2, 0:1],
                                           prob[:, i % 2, 1, 0:nk], ALU.mult, ALU.subtract).then_inc(*made("pdiff", i))
                    if h == 2 and t >= 1:
                        copy_o(dve, t - 1)
                    if i == 17:
                        copy_o(dve, 2)

                def copy_o(dve, t):
                    dve.wait_ge(*after("pv", HEADS * t + HEADS - 1))
                    nc.vector.tensor_copy(osb[:, t, :], PS[:, 6 + t % 2, 0:DR]).then_inc(*made("o", t))

                def ff_bank(f):
                    return 4 * (f // HALF) + 2 * (f % 2)

                def fo_bank(half, oh):
                    return 4 * (1 - half if oh == 0 else half)

                def fo_last(half, oh):
                    return S_FFN + half * FFN_SLOTS + HALF + (HALF * (oh + 1) - 1) // 4

                def mod_row(pair):
                    b = (KT if pair % 2 else tanh2 if pair < MOD_PAIRS_A else BT)
                    return b[:, :, :].rearrange("p a t -> p (a t)")[:, 0:512]

                def mod_banks(pair):
                    return ((0, 1)[pair % 2], (2, 3)[pair % 2]) if pair < MOD_PAIRS_A else ((0, 2)[pair % 2], 1)

                def mod_slot(i):
                    return i if i < S_R else S_MOD_B + i - S_R

                def copy_mod_row(act, pair):
                    act.wait_ge(*after("mod_mm", mod_slot(2 * pair + 1)))
                    if pair >= 2:
                        act.wait_ge(*after("mod_tr", pair - 2))
                    nc.scalar.activation(mod_row(pair), PS[:, mod_banks(pair)[0], :], ACT.Copy).then_inc(*made("mod_row", pair))

                def sum_mod(dve, pair):
                    dve.wait_ge(*after("mod_tr", pair))
                    nc.vector.tensor_reduce(mods[:, 4 * pair:4 * pair + 4, :],
                                            PS[:, mod_banks(pair)[1], :].rearrange("p (b j r) -> p b r j", b=4, j=4)[:, :, 0:2, :],
                                            AX.X, ALU.add).then_inc(*made("mod_sum", pair))

                def slot_mm(s):
                    if s < S_R or S_MOD_B <= s < S_OUT:
                        return "mod_mm", s
                    if s < S_GD:
                        return "in_mm", 2 * (s - S_R) + 1
                    if s < S_OUT:
                        return "in_mm", 13 + 3 * (s - S_GD)
                    if s < S_FFN:
                        return "out_mm", 2 * (s - S_OUT) + 1
                    half, i = divmod(s - S_FFN, FFN_SLOTS)
                    return ("ff_mm", half * HALF + i) if i < HALF else ("ffo_mm", s)

                def width(s):
                    last_fo = s >= S_FFN and (s - S_FFN) % FFN_SLOTS == FFN_SLOTS - 1
                    return (192, 256) if s == S_GD else (2048 - 512 * (4 * FO_SLOTS - 2 * HALF) if last_fo else 2048, 2048)

                def used(x, s):
                    n, row = width(s)
                    return x.rearrange("p (k n) -> p k n", n=row)[:, :, 0:n]

                def weights_hi(act, s):
                    n = SPLIT.index(s)
                    act.wait_ge(*after(f"slot{s % RING}", s))
                    if n >= 2:
                        act.wait_ge(*after(*slot_mm(SPLIT[n - 2])))
                    if s == S_OUT:
                        act.wait_ge(*after("Y_mm", HC - 1))
                    nc.scalar.activation(used(w_hi[:, n % 2, :], s), used(ring[:, s % RING, :], s), ACT.Copy).then_inc(*made("w_hi", s))

                def weights_lo(dve, s):
                    n = SPLIT.index(s)
                    dve.wait_ge(*after("w_hi", s))
                    nc.vector.tensor_tensor(used(w_lo[:, n % 2, :], s), used(ring[:, s % RING, :], s),
                                            used(w_hi[:, n % 2, :], s).bitcast(F32), ALU.subtract).then_inc(*made("w_lo", s))

                def last_use(s):
                    return ("w_lo", s) if s in SPLIT else slot_mm(s)

                def slot_loads(s):
                    dst = ring[:, s % RING, :]
                    d8 = dst.rearrange("p (k n) -> p k n", k=KC)
                    if s < S_R or S_MOD_B <= s < S_OUT:
                        w = layer(a["w_mod"], l).rearrange("(k p) n -> p k n", p=P)
                        at = 256 * (s if s < S_R else s - S_MOD_B + S_R)
                        return [(d8, w[:, :, at:at + 256])]
                    if s < S_OUT:
                        w = layer(a["w_in"], l).rearrange("(k p) n -> p k n", p=P)
                        if s < S_GD:
                            at = 256 * (s - S_R)
                            return [(d8, w[:, :, at:at + 256])]
                        if s == S_GD:
                            return [(d8[:, :, 0:64], w[:, :, 1280:NR]), (d8[:, :, 64:192], w[:, :, DIN - P:DIN])]
                        at = NR + 256 * (s - S_T)
                        return [(d8, w[:, :, at:at + 256])]
                    if s < S_FFN:
                        w = layer(a["w_out"], l).rearrange("(k p) n -> p k n", p=P)
                        at = 256 * (s - S_OUT)
                        return [(d8, w[:, :, at:at + 256])]
                    half, i = divmod(s - S_FFN, FFN_SLOTS)
                    if i < HALF:
                        w = layer(a["w_ffn_in"], l).rearrange("(k p) n -> p k n", p=P)
                        f = half * HALF + i
                        return [(d8[:, :, 0:P], w[:, :, f * P:f * P + P]),
                                (d8[:, :, P:2 * P], w[:, :, DFF + f * P:DFF + f * P + P])]
                    w = layer(a["w_ffn_out"], l).rearrange("(k p) n -> p k n", p=P)
                    d4 = dst.rearrange("p (k n) -> p k n", k=4)
                    units = [divmod(u, HALF) for u in range(4 * (i - HALF), min(4 * (i - HALF) + 4, 2 * HALF))]
                    out = []
                    j = 0
                    while j < len(units):
                        oh, k0 = units[j]
                        m = 1
                        while j + m < len(units) and units[j + m][0] == oh:
                            m += 1
                        k1 = half * HALF + k0
                        out.append((d4[:, j:j + m, :], w[:, k1:k1 + m, oh * 512:oh * 512 + 512]))
                        j += m
                    return out

                @block.sync
                def _(sp):
                    for s in range(SLOTS):
                        if s >= RING:
                            sp.wait_ge(*after(*last_use(s - RING)))
                        for dst, src in slot_loads(s):
                            sp.dma_start(dst, src).then_inc(*loaded(f"slot{s % RING}", s))
                    sp.wait_ge(*after("state_stored", 1))

                @block.gpsimd
                def _(pool):
                    for i, at in enumerate((0, SEQ + 1, TOK + 2)):
                        nc.gpsimd.memset(upad[:, :, at:at + 1], 0.0).then_inc(*made("pad_cols", i))
                    for t in range(2):
                        src = tok[:, t + 1, 0:768]
                        pool.wait_ge(*after("tok_dve", 14))
                        pool.wait_ge(*after("tok_act", 14))
                        nc.gpsimd.tensor_tensor(rot[:, t, :].rearrange("p (h n) -> p h n", n=32),
                                                src.rearrange("p (h n) -> p h n", n=32),
                                                cos[:, t, :].unsqueeze(1).to_broadcast([P, 24, 32]),
                                                ALU.mult).then_inc(*made("rope_cos", t))
                        for h in range(2):
                            o = rot2[:, t, :].rearrange("p (g x h n) -> p g x h n", g=24, x=2, h=2)[:, :, :, h, :]
                            i = src.rearrange("p (g x h n) -> p g x h n", g=24, x=2, h=2)[:, :, :, 1 - h, :]
                            nc.gpsimd.tensor_tensor(o, i, sin[:, t, :, h, :].unsqueeze(1).to_broadcast([P, 24, 2, 8]),
                                                    ALU.mult).then_inc(*made("rope_sin", (t, h)))
                        pool.wait_ge(*after("rope_cos", t))
                        pool.wait_ge(*after("rope_sin", (t, 1)))
                        nc.gpsimd.tensor_tensor(rot[:, t, :], rot[:, t, :], rot2[:, t, :], ALU.add).then_inc(*made("rope", t))
                    for c in range(HC):
                        for d in range(2):
                            pool.wait_ge(*after("a_tanh", (c, d)))
                            if (c, d) == (0, 0):
                                pool.wait_ge(*after("kk", HC - 1))
                            if c >= 1:
                                pool.wait_ge(*after("A_mm", (c - 1, 2, 1)))
                                pool.wait_ge(*after("kt_tr", c - 1))
                                pool.wait_ge(*after("bonus_k", c - 1))
                            nc.gpsimd.tensor_scalar(AA[:, :], AA[:, :], 0.5, 0.5, ALU.mult, ALU.add).then_inc(*made("a", (c, d)))
                            pool.wait_ge(*after("a", (c, d)))
                            nc.gpsimd.tensor_tensor(BT[:, d, :], AA[:, :], kk[:, c, :], ALU.mult).then_inc(*made("b", (c, d)))
                            nc.gpsimd.tensor_scalar(KD[:, d, :], AA[:, :], vec[:, VEC["k_a"] + c:VEC["k_a"] + c + 1],
                                                    omka[:, c:c + 1], ALU.mult, ALU.add).then_inc(*made("ka", (c, d)))
                            pool.wait_ge(*after("ka", (c, d)))
                            nc.gpsimd.tensor_tensor(KD[:, d, :], KD[:, d, :], uT[:, 3 + c, :], ALU.mult).then_inc(*made("kd", (c, d)))
                        for g in range(3):
                            pool.wait_ge(*after("A", (c, g, 0)))
                            nc.gpsimd.tensor_tensor(AKB[:, g, :, :], AKB[:, g, :, :],
                                                    ident.unsqueeze(1).to_broadcast([P, 4, P]), ALU.add).then_inc(*made("A1", (c, g)))
                            pool.wait_ge(*after("A1", (c, g)))
                            for d in range(2):
                                nc.gpsimd.tensor_tensor(XT[:, g, 2 * d:2 * d + 2, :], AKB[:, g, 2 * d:2 * d + 2, :],
                                                        lmask[:, 0, 1 - d, :].unsqueeze(1).to_broadcast([P, 2, P]),
                                                        ALU.mult).then_inc(*made("XT0", (c, g, d)))

                @block.scalar
                def _(act):
                    def vload(name, rows, src):
                        at = VEC[name]
                        act.dma_start(vrow[at:at + rows, 0:src.shape[-1]], src).then_inc(*loaded("vec_loaded", name))

                    k_p = "(k p) -> k p"
                    vload("norm1_g", 8, layer2(a["norm1_g"], l))
                    vload("norm2_g", 8, layer2(a["norm2_g"], l))
                    vload("b_mod", 48, layer2(a["b_mod"], l))
                    for n in ("decay_w0", "iclr_a0"):
                        vload(n, 6, layer(a[n], l).rearrange("d (k p) -> (d k) p", p=P))
                    for n in ("k_k", "k_a", "lnx_g", "lnx_b"):
                        vload(n, 3, layer2(a[n], l))
                    vload("r_k", 3, layer(a["r_k"], l).rearrange("(k h) n -> k (h n)", h=2))
                    sg = layer2(a["subln_g"], l, 64)
                    r0 = VEC["subln_g"]
                    for h in range(2):
                        act.dma_start(vrow[r0:r0 + 1, 64 * h:64 * h + 64], sg).then_inc(*loaded("vec_loaded", ("subln", h)))
                    for i in range(2):
                        mu = layer(a["shift_mu"], l)[i:i + 1, :]
                        r0 = VEC[f"mu{i}"]
                        act.dma_start(vrow[r0:r0 + 10, :], mu[:, 0:1280].rearrange("o (k p) -> (o k) p", p=P)).then_inc(*loaded("vec_loaded", ("mu", i)))
                        act.dma_start(vrow[r0 + 10:r0 + 11, 0:64], mu[:, 1280:NR]).then_inc(*loaded("vec_loaded", ("mue", i)))
                    act.dma_start(lora[0:64, :], layer(a["decay_up"], l).rearrange("d r n -> (d r) n")).then_inc(*loaded("lora_loaded"))
                    act.dma_start(lora[64:128, :], layer(a["iclr_up"], l).rearrange("d r n -> (d r) n")).then_inc(*loaded("lora_loaded", 1))
                    act.dma_start(gup[:, :], layer(a["gate_up"], l)).then_inc(*loaded("lora_loaded", 2))
                    dl = layer(a["diff_lambda"], l).rearrange("a b -> (a b)").unsqueeze(0).to_broadcast([P, P])
                    act.dma_start(lrow[:, :], dl).then_inc(*loaded("lam_loaded"))
                    act.dma_start(lamc[:, :], layer(a["lam_init"], l)).then_inc(*loaded("lam_loaded", 1))
                    act.dma_start(ctxk, layer(a["cache_k"], l)).then_inc(*loaded("ctx_loaded"))
                    act.dma_start(ctxv, layer(a["cache_v"], l)).then_inc(*loaded("ctx_loaded", 1))
                    for d in range(2):
                        act.dma_start(sin_rows[:, d, :].rearrange("v (h k) -> v h k", h=HEADS),
                                      layer(a["state"], l)[d].rearrange("h v k -> v h k")).then_inc(*loaded("state_loaded", d))

                    norm_act(act, "n1")
                    for pair in range(MOD_PAIRS_A):
                        copy_mod_row(act, pair)
                    weights_hi(act, S_R)
                    def add_shift(n, base):
                        for k in range(KC):
                            for gi, (t0, t1) in enumerate(GROUPS):
                                act.wait_ge(*after(f"{n}_scaled", (k, gi)))
                                nc.scalar.activation(h_hi[:, k, t0:t1], yT[:, k, t0:t1], ACT.Identity,
                                                     bias=mods[:, base + k, gi:gi + 1]).then_inc(*made(f"{n}_h", (k, gi)))

                    add_shift("n1", SH1)
                    act.wait_ge(*after("lam_dots", 1))
                    nc.scalar.activation(lsum[:, 2:4], lsum[:, 0:2], ACT.Exp).then_inc(*made("lam_exp"))

                    for j in range(11):
                        m = HD if j == 10 else P
                        if j % 2 == 0:
                            weights_hi(act, S_R + j // 2 + 1)
                        act.wait_ge(*after("in_mm", j))
                        if j >= 2:
                            act.wait_ge(*after("shifted", j - 2))
                        u = PS[0:m, j % 4, 0:TOK]
                        nc.scalar.activation(upad[0:m, j % 2, 1:1 + SEQ], u[:, 0:SEQ], ACT.Copy).then_inc(*made("u_copy", (j, 0)))
                        nc.scalar.activation(upad[0:m, j % 2, 2 + SEQ:2 + TOK], u[:, SEQ:TOK], ACT.Copy).then_inc(*made("u_copy", (j, 1)))
                        nc.scalar.activation(uT[0:m, j, :], u, ACT.Copy, scale=muc[0:m, j:j + 1]).then_inc(*made("u_own", j))
                    for n in range(18):
                        if n % 3 == 0 and 3 <= n < 15:
                            weights_hi(act, S_T + n // 3)
                        if n % 2 == 0:
                            at, w, t = tok_job(n)
                            act.wait_ge(*after("in_mm", 11 + n))
                            nc.scalar.activation(tok[:, t, at:at + w], PS[:, (11 + n) % 4, 0:w], ACT.Copy).then_inc(*made("tok_act", n if n < 14 else 14))
                    act.wait_ge(*after("tok_dve", 14))
                    act.wait_ge(*after("tok_act", 14))
                    act.dma_start(layer(a["out_k"], l), tok[:, 0, 384:768]).then_inc(*loaded("cache_stored"))
                    act.dma_start(layer(a["out_v"], l), tok[:, 0, 768:1152]).then_inc(*loaded("cache_stored", 1))
                    act.wait_ge(*after("shifted", 10))
                    nc.scalar.activation(tanh2[0:64, 0, :], uT[0:64, 9, :], ACT.Tanh).then_inc(*made("wd_tanh"))
                    nc.scalar.activation(tanh2[0:64, 1, :], uT[0:64, 10, :], ACT.Tanh, scale=0.5).then_inc(*made("gd_tanh"))
                    for c in range(HC):
                        act.wait_ge(*after("q_tr", c))
                        nc.scalar.activation(qT[:, c, :], PS[:, (2 * c) % 8, 0:TOK], ACT.Copy).then_inc(*made("qT", c))
                    for i in range(18):
                        t, h = divmod(i, HEADS)
                        nk = 128 if t == 0 else 384
                        act.wait_ge(*after("neg_max", i))
                        if i >= 2:
                            act.wait_ge(*after("pdiff", i - 2))
                        for m in range(2):
                            nc.scalar.activation(prob[:, i % 2, m, 0:nk], PS[:, 2 * (i % 2) + m, 0:nk], ACT.Exp,
                                                 bias=nmax[:, i % 2, m:m + 1], scale=QSCALE,
                                                 accum_out=rsum[:, i % 2, m:m + 1]).then_inc(*made("exp", (i, m)))
                        if i >= 1:
                            copy_pdT(act, i - 1)
                    copy_pdT(act, 17)
                    for c in range(HC):
                        act.wait_ge(*after("gate_mm", c))
                        nc.scalar.activation(gate[:, c, :], PS[:, c, 0:TOK], ACT.Copy).then_inc(*made("gate", c))
                    act.wait_ge(*after("o_ms"))
                    nc.scalar.activation(onorm[:, :], onorm[:, :], ACT.Sqrt, bias=eps[:, 2:3], scale=1.0 / HD).then_inc(*made("o_sqrt"))
                    for c in range(HC):
                        act.wait_ge(*after("kk_ss", c))
                        nc.scalar.activation(KD[:, 0, :] if c == 0 else KD[:, 1, :] if c == 1 else E3[:, :],
                                             PS[:, 3 + c, 0:TOK], ACT.Sqrt, bias=eps[:, 3:4]).then_inc(*made("kk_sqrt", c))
                    for t in range(TILES):
                        act.wait_ge(*after("o_tr", t))
                        nc.scalar.activation(yT[:, 3:6, t * P:(t + 1) * P],
                                             PS[:, t, 0:DR].rearrange("p (c n) -> p c n", c=3), ACT.Copy,
                                             scale=subs).then_inc(*made("y_attn", t))
                    for dc in range(2):
                        act.wait_ge(*after("fz_mm", dc))
                        nc.scalar.activation(fz[:, dc, 0:256], PS[:, 4 + 2 * dc, 0:256], ACT.Copy).then_inc(*made("fz", (dc, 0)))
                        nc.scalar.activation(fz[:, dc, 256:768], PS[:, 5 + 2 * dc, :], ACT.Copy).then_inc(*made("fz", (dc, 1)))
                    for dc in range(2):
                        act.wait_ge(*after("fnet_mm", dc))
                        nc.scalar.activation(yT[:, 6 + dc, :], PS[:, dc, 0:TOK], ACT.Copy).then_inc(*made("y_fnet", dc))
                    for c in range(HC):
                        for d in range(2):
                            act.wait_ge(*after("lora_mm", (c, d)))
                            if (c, d) != (0, 0):
                                pc, pd = (c, 0) if d else (c - 1, 1)
                                act.wait_ge(*after("ka", (pc, pd)))
                                act.wait_ge(*after("b", (pc, pd)))
                                act.wait_ge(*after("EX", (pc, pd)))
                            nc.scalar.activation(LW[:, :], PS[:, 0, 0:TOK], ACT.Tanh, scale=0.5,
                                                 bias=w0h[:, 3 * d + c:3 * d + c + 1]).then_inc(*made("w_tanh", (c, d)))
                            nc.scalar.activation(AA[:, :], PS[:, 1, 0:TOK], ACT.Tanh, scale=0.5,
                                                 bias=a0h[:, 3 * d + c:3 * d + c + 1]).then_inc(*made("a_tanh", (c, d)))
                            act.wait_ge(*after("EX", (c, d)))
                            if c >= 1:
                                act.wait_ge(*after("Y_mm", c - 1))
                            if (c, d) != (0, 0):
                                act.wait_ge(*after("b_scaled", (pc, pd)))
                            kap, r, e3 = (((EX, 1.0), (EI, 1.0), (EI, -1.0)), ((EI, -1.0), (EX, -1.0), (EX, 1.0)))[d]
                            nc.scalar.activation(KAP[:, d, :], kap[0][:, :], ACT.Exp, scale=kap[1]).then_inc(*made("e_kap", (c, d)))
                            nc.scalar.activation(RT[:, d, :], r[0][:, :], ACT.Exp, scale=r[1]).then_inc(*made("e_r", (c, d)))
                            nc.scalar.activation(E3[:, :], e3[0][:, :], ACT.Exp, scale=e3[1]).then_inc(*made("e_3", (c, d)))
                            nc.scalar.activation(et[:, d, :], nh[:, d, :], ACT.Exp, scale=-1.0).then_inc(*made("e_tot", (c, d)))
                        act.wait_ge(*after("kt_tr", c))
                        if c >= 1:
                            act.wait_ge(*after("S_mm", (c - 1, 1)))
                        nc.scalar.activation(ktok[:, :, :, :].rearrange("p d t n -> p (d t n)"), PS[:, 2, :], ACT.Copy).then_inc(*made("ktok", c))
                        nc.scalar.activation(btok[:, :, :, :].rearrange("p d t n -> p (d t n)"), PS[:, 3, :], ACT.Copy).then_inc(*made("btok", c))
                        for j in range(1, LEVELS):
                            for g in range(3):
                                if j < LEVELS - 1:
                                    act.wait_ge(*after("X_mm", (c, j, g)))
                                    nc.scalar.activation(flat(X[:, g]), PS[:, xbank(j, g), :], ACT.Copy).then_inc(*made("X", (c, j, g)))
                                act.wait_ge(*after("XT_mm", (c, j, g)))
                                nc.scalar.activation(flat(XT[:, g]), PS[:, xbank(j, g) + 1, :], ACT.Copy).then_inc(*made("XT", (c, j, g)))
                        for g in range(3):
                            act.wait_ge(*after("U_mm", (c, g)))
                            if c >= 1 and g == 0:
                                act.wait_ge(*after("Y_mm", c - 1))
                            nc.scalar.activation(usb[:, g, :], PS[:, 7, 0:256], ACT.Copy, scale=-1.0).then_inc(*made("U", (c, g)))
                            if g < len(MOD_PAIRS_SOLVE[c]):
                                copy_mod_row(act, MOD_PAIRS_SOLVE[c][g])
                        act.wait_ge(*after("Y_mm", c))
                        for h in range(2):
                            hs = slice(h * HD, (h + 1) * HD)
                            nc.scalar.activation(yT[hs, c, :], PS[hs, 5 + h, 0:TOK], ACT.Copy).then_inc(*made("y_raw", c if h else (c, 0)))
                    weights_hi(act, S_OUT)
                    act.wait_ge(*after("cache_stored", 1))
                    for k in range(HC, KC):
                        nc.scalar.activation(y_hi[:, k, :], yT[:, k, :], ACT.Copy).then_inc(*made("y_hi", k))
                    for d in range(2):
                        act.wait_ge(*after("st_tr", d))
                        nc.scalar.activation(sout[:, d, :], PS[0:HD, 6 + d, 0:DR], ACT.Copy).then_inc(*made("state_rows", d))
                    act.wait_ge(*after("state_rows", 1))
                    for d in range(2):
                        act.dma_start(layer(a["out_s"], l)[d].rearrange("h v k -> v h k"),
                                      sout[:, d, :].rearrange("v (h k) -> v h k", h=HEADS)).then_inc(*loaded("state_stored", d))
                    for c in range(HC):
                        act.wait_ge(*after("gn_var_mm", c))
                        nc.scalar.activation(KT[:, 0, :] if c == 0 else KT[:, 1, :] if c == 1 else BT[:, 0, :],
                                             PS[:, 3 + c, 0:TOK], ACT.Sqrt, bias=eps[:, 1:2], scale=1.0 / HD).then_inc(*made("gn_sqrt", c))

                    for k in range(HC):
                        act.wait_ge(*after("y_rwkv", k))
                        nc.scalar.activation(y_hi[:, k, :], yT[:, k, :], ACT.Copy).then_inc(*made("y_hi", k))
                    for s in range(S_OUT + 1, S_FFN + 1):
                        weights_hi(act, s)
                    act.wait_ge(*after("x1", (KC - 1, 1)))
                    norm_act(act, "n2")
                    add_shift("n2", SH2)
                    for s in range(S_FFN, SLOTS):
                        if s + 1 < SLOTS:
                            weights_hi(act, s + 1)
                        half, i = divmod(s - S_FFN, FFN_SLOTS)
                        if i < HALF:
                            f = half * HALF + i
                            act.wait_ge(*after("ff_mm", f))
                            if f >= 2:
                                act.wait_ge(*after("ff_lo", f - 2))
                            nc.scalar.activation(tanh2[:, f % 2, :], PS[:, ff_bank(f), 0:TOK], ACT.Tanh, scale=0.5).then_inc(*made("ff_tanh", f))
                            act.wait_ge(*after("ff", f))
                            nc.scalar.activation(ff_hi[:, i, :], tanh2[:, f % 2, :], ACT.Copy).then_inc(*made("ff_hi", f))

                @block.vector
                def _(dve):
                    V = nc.vector
                    dve.wait_ge(*after("vec_tr"))
                    V.tensor_copy(vec[:, :], PS[:, 5, 0:P]).then_inc(*made("vec"))
                    dve.wait_ge(*after("vec"))
                    col = lambda n, k: vec[:, VEC[n]:VEC[n] + k]
                    dve.wait_ge(*after("lam_loaded", 1))
                    V.tensor_tensor(muc, col("mu0", 11), col("mu1", 11), ALU.add).then_inc(*made("dvec", 0))
                    V.tensor_scalar(w0h, col("decay_w0", 6), 0.5, None, ALU.mult).then_inc(*made("dvec", 1))
                    V.tensor_scalar(a0h, col("iclr_a0", 6), 0.5, None, ALU.mult).then_inc(*made("dvec", 2))
                    V.tensor_scalar(omka, col("k_a", 3), -1.0, 1.0, ALU.mult, ALU.add).then_inc(*made("dvec", 3))
                    V.tensor_tensor(subs, col("subln_g", 1), lamc[:, 1:2], ALU.mult).then_inc(*made("dvec", 4))
                    dve.wait_ge(*after("dvec", 0))
                    V.tensor_scalar(muc, muc, -1.0, 1.0, ALU.mult, ALU.add).then_inc(*made("dvec", 5))
                    lr = lrow[:, :].rearrange("p (a n) -> p a n", a=4)
                    V.tensor_tensor(lprod[:, :, :], lr[:, 0:4:2, :], lr[:, 1:4:2, :], ALU.mult).then_inc(*made("lam_dots", 0))
                    dve.wait_ge(*after("lam_dots", 0))
                    V.tensor_reduce(lsum[:, 0:2], lprod[:, :, :], AX.X, ALU.add).then_inc(*made("lam_dots", 1))

                    def norm_apply(n, g, base):
                        dve.wait_ge(*after(f"{n}_sqrt"))
                        V.reciprocal(rstd[:, :], rstd[:, :]).then_inc(*made(f"{n}_rstd"))
                        dve.wait_ge(*after(f"{n}_rstd"))
                        for k in range(KC):
                            for gi, (t0, t1) in enumerate(GROUPS):
                                V.scalar_tensor_tensor(yT[:, k, t0:t1], xT[:, k, t0:t1], gmod[:, g, k, gi:gi + 1],
                                                       rstd[:, t0:t1], ALU.mult, ALU.mult).then_inc(*made(f"{n}_scaled", (k, gi)))
                        for k in range(KC):
                            for gi, (t0, t1) in enumerate(GROUPS):
                                dve.wait_ge(*after(f"{n}_h", (k, gi)))
                                V.scalar_tensor_tensor(h_lo[:, k, t0:t1], yT[:, k, t0:t1], mods[:, base + k, gi:gi + 1],
                                                       h_hi[:, k, t0:t1].bitcast(F32), ALU.add,
                                                       ALU.subtract).then_inc(*made(f"{n}_low", (k, gi)))

                    def finish_mods(part, n0, n1, g, norm_g, sc):
                        dve.wait_ge(*after("mod_sum", n1 // 4 - 1))
                        V.tensor_tensor(mods[:, n0:n1, :], mods[:, n0:n1, :],
                                        vec[:, VEC["b_mod"] + n0:VEC["b_mod"] + n1].unsqueeze(2).to_broadcast([P, n1 - n0, 2]),
                                        ALU.add).then_inc(*made("mods", part))
                        dve.wait_ge(*after("mods", part))
                        V.tensor_scalar(gmod[:, g, :, :], mods[:, sc:sc + 8, :], 1.0, None, ALU.add).then_inc(*made("gmod", (g, 0)))
                        dve.wait_ge(*after("gmod", (g, 0)))
                        V.tensor_tensor(gmod[:, g, :, :], gmod[:, g, :, :], col(norm_g, 8).unsqueeze(2).to_broadcast([P, KC, 2]),
                                        ALU.mult).then_inc(*made("gmod", (g, 1)))
                        dve.wait_ge(*after("gmod", (g, 1)))

                    for pair in range(MOD_PAIRS_A):
                        sum_mod(dve, pair)
                    finish_mods(0, 0, 16, 0, "norm1_g", SC1)
                    weights_lo(dve, S_R)
                    norm_apply("n1", 0, SH1)
                    dve.wait_ge(*after("lam_exp"))
                    V.tensor_tensor(lsum[:, 4:5], lsum[:, 2:3], lsum[:, 3:4], ALU.subtract).then_inc(*made("lam", 0))
                    dve.wait_ge(*after("lam", 0))
                    V.tensor_tensor(lam[:, :], lsum[:, 4:5], lamc[:, 0:1], ALU.add).then_inc(*made("lam", 1))

                    for j in range(11):
                        m = HD if j == 10 else P
                        if j % 2 == 0:
                            weights_lo(dve, S_R + j // 2 + 1)
                        dve.wait_ge(*after("u_copy", (j, 1)))
                        dve.wait_ge(*after("u_own", j))
                        dve.wait_ge(*after("pad_cols", 2))
                        for side in range(2):
                            mu = vec[0:m, VEC[f"mu{side}"] + j:VEC[f"mu{side}"] + j + 1]
                            if side:
                                dve.wait_ge(*after("u_prev", (j, 1)))
                            for gi, (t0, t1) in enumerate(GROUPS):
                                at = t0 + gi + 2 * side
                                last = V.scalar_tensor_tensor(uT[0:m, j, t0:t1], upad[0:m, j % 2, at:at + t1 - t0], mu,
                                                              uT[0:m, j, t0:t1], ALU.mult, ALU.add)
                                last.then_inc(*(made("u_prev", (j, gi)) if side == 0 else made("shifted", j if gi else (j, 0))))
                    for n in range(18):
                        if n % 3 == 0 and 3 <= n < 15:
                            weights_lo(dve, S_T + n // 3)
                        if n % 2 == 1:
                            at, w, t = tok_job(n)
                            dve.wait_ge(*after("in_mm", 11 + n))
                            V.tensor_copy(tok[:, t, at:at + w], PS[:, (11 + n) % 4, 0:w]).then_inc(*made("tok_dve", n if n < 14 else 14))
                    dve.wait_ge(*after("gd_tanh"))
                    V.tensor_scalar(tanh2[0:64, 1, :], tanh2[0:64, 1, :], 0.5, 0.5, ALU.mult, ALU.add).then_inc(*made("gd_sig"))
                    for c in range(HC):
                        dve.wait_ge(*after("v_tr", c))
                        V.tensor_copy(vtok[:, :, c * P:(c + 1) * P],
                                      PS[:, 4 + c, 0:TOK].rearrange("p (t n) -> p t n", t=3)).then_inc(*made("vtok", c))
                    dve.wait_ge(*after("s0_tr"))
                    V.tensor_copy(S0T[:, :, :, :].rearrange("p d c n -> p (d c n)"), PS[:, 7, 0:DR]).then_inc(*made("S0T"))
                    for c in range(HC):
                        dve.wait_ge(*after("k_tr", c))
                        V.tensor_copy(kT[:, c, :], PS[:, 2 * c + 1, :]).then_inc(*made("kT", c))
                    for i in range(18):
                        t, h = divmod(i, HEADS)
                        nk = 128 if t == 0 else 384
                        dve.wait_ge(*after("scores", i))
                        if i >= 2:
                            dve.wait_ge(*after("exp", (i - 2, 1)))
                        V.tensor_reduce(amax[:, i % 2, :], PS[:, 2 * (i % 2):2 * (i % 2) + 2, 0:nk], AX.X, ALU.max).then_inc(*made("max", i))
                        dve.wait_ge(*after("max", i))
                        V.tensor_scalar(nmax[:, i % 2, :], amax[:, i % 2, :], -QSCALE, None, ALU.mult).then_inc(*made("neg_max", i))
                        if i >= 1:
                            diff(dve, i - 1)
                    diff(dve, 17)
                    for t in range(TILES):
                        if t == 0:
                            dve.wait_ge(*after("o", 2))
                            dve.wait_ge(*after("pdT", 17))
                        V.tensor_tensor(prob_flat[:, t * DR:(t + 1) * DR], osb[:, t, :], osb[:, t, :], ALU.mult).then_inc(*made("o_sq", t))
                    dve.wait_ge(*after("o_sq", 2))
                    V.tensor_reduce(onorm[:, :], prob_flat[:, 0:3 * DR].rearrange("p (h n) -> p h n", n=HD), AX.X, ALU.add).then_inc(*made("o_ms"))
                    for c in range(HC):
                        V.tensor_scalar(kk[:, c, :], uT[:, 3 + c, :], vec[:, VEC["k_k"] + c:VEC["k_k"] + c + 1], None, ALU.mult).then_inc(*made("kk_raw", c))
                    dve.wait_ge(*after("kk_raw", 2))
                    for c in range(HC):
                        V.tensor_tensor((LW, EI, EX)[c][:, :], kk[:, c, :], kk[:, c, :], ALU.mult).then_inc(*made("kk_sq", c))
                    dve.wait_ge(*after("o_sqrt"))
                    V.reciprocal(onorm[:, :], onorm[:, :]).then_inc(*made("o_rinv"))
                    dve.wait_ge(*after("o_rinv"))
                    for t in range(TILES):
                        V.tensor_tensor(osb[:, t, :].rearrange("p (h n) -> p h n", n=HD), osb[:, t, :].rearrange("p (h n) -> p h n", n=HD),
                                        onorm[:, 6 * t:6 * t + 6].unsqueeze(2).to_broadcast([P, 6, HD]), ALU.mult).then_inc(*made("o_n", t))
                    for c in range(HC):
                        b = (KD[:, 0, :], KD[:, 1, :], E3[:, :])[c]
                        dve.wait_ge(*after("kk_sqrt", c))
                        V.tensor_scalar(b, b, 1e-12, None, ALU.max).then_inc(*made("kk_den", (c, 0)))
                        dve.wait_ge(*after("kk_den", (c, 0)))
                        V.reciprocal(b, b).then_inc(*made("kk_den", (c, 1)))
                        dve.wait_ge(*after("kk_den", (c, 1)))
                        V.tensor_tensor(kk[:, c, :], kk[:, c, :], b, ALU.mult).then_inc(*made("kk", c))

                    for c in range(HC):
                        for d in range(2):
                            dve.wait_ge(*after("w_tanh", (c, d)))
                            if (c, d) == (0, 0):
                                dve.wait_ge(*after("kk", 2))
                            V.tensor_scalar(LW[:, :], LW[:, :], -0.5 * DECAY, -0.5 * DECAY, ALU.mult, ALU.add).then_inc(*made("LW", (c, d)))
                            dve.wait_ge(*after("LW", (c, d)))
                            if (c, d) != (0, 0):
                                pc, pd = (c, 0) if d else (c - 1, 1)
                                dve.wait_ge(*after("e_tot", (pc, pd)))
                            V.tensor_tensor_scan(EI[:, :], smask, LW[:, :], 0.0, ALU.mult, ALU.add).then_inc(*made("sum", (c, d)))
                            dve.wait_ge(*after("sum", (c, d)))
                            V.tensor_scalar(nh[:, d, :], EI[:, P - 1:TOK:P], -0.5, None, ALU.mult).then_inc(*made("nh", (c, d)))
                            dve.wait_ge(*after("nh", (c, d)))
                            V.tensor_tensor(EI[:, :].rearrange("p (t n) -> p t n", t=3), EI[:, :].rearrange("p (t n) -> p t n", t=3),
                                            nh[:, d, :].unsqueeze(2).to_broadcast([P, 3, P]), ALU.add).then_inc(*made("EI", (c, d)))
                            dve.wait_ge(*after("EI", (c, d)))
                            V.tensor_tensor(EX[:, :], EI[:, :], LW[:, :], ALU.subtract).then_inc(*made("EX", (c, d)))
                            dve.wait_ge(*after("e_kap", (c, d)))
                            V.tensor_tensor(KAP[:, d, :], KAP[:, d, :], kk[:, c, :], ALU.mult).then_inc(*made("kap", (c, d)))
                            dve.wait_ge(*after("e_r", (c, d)))
                            V.tensor_tensor(RT[:, d, :], RT[:, d, :], uT[:, c, :], ALU.mult).then_inc(*made("r", (c, d)))
                            dve.wait_ge(*after("e_3", (c, d)))
                            dve.wait_ge(*after("kd", (c, d)))
                            V.tensor_tensor(KT[:, d, :], KD[:, d, :], E3[:, :], ALU.mult).then_inc(*made("k_scaled", (c, d)))
                            V.tensor_tensor(BT[:, d, :], BT[:, d, :], E3[:, :], ALU.mult).then_inc(*made("b_scaled", (c, d)))
                        V.tensor_tensor(gsum[:, :], KD[:, 0, :], KD[:, 1, :], ALU.add).then_inc(*made("bonus_k", c))
                        dve.wait_ge(*after("bonus_k", c))
                        V.scalar_tensor_tensor(gsum[:, :], gsum[:, :], vec[:, VEC["r_k"] + c:VEC["r_k"] + c + 1], uT[:, c, :],
                                               ALU.mult, ALU.mult).then_inc(*made("bonus_r", c))
                        dve.wait_ge(*after("bonus_mm", c))
                        V.tensor_tensor(bonus[:, c, :], PS[:, 4, 0:TOK], uT[:, 6 + c, :], ALU.mult).then_inc(*made("bonus", c))
                        dve.wait_ge(*after("e_tot", (c, 1)))
                        if c >= 1:
                            dve.wait_ge(*after("Y_mm", c - 1))
                        for d in range(2):
                            t = STEP_TILE[1][d]
                            V.tensor_scalar(SH[:, 1, d, :], S0T[:, d, c, :], et[:, d, t:t + 1], None, ALU.mult).then_inc(*made("SH", (c, 1, d)))
                        for g in range(3):
                            for n in range(2):
                                dve.wait_ge(*after("A_mm", (c, g, n)))
                                if c >= 1 and g == 0 and n == 0:
                                    dve.wait_ge(*after("Y_mm", c - 1))
                                for i, dst in enumerate(((AKB, AKV), (ARB, ARV))[n]):
                                    for h in range(2):
                                        V.tensor_tensor(dst[:, g, h:4:2, :],
                                                        PS[:, abank(2 * g + n, h), 256 * i:256 * i + 256].rearrange("p (d t) -> p d t", d=2),
                                                        amask[:, 2 * n:2 * n + 2, :], ALU.mult).then_inc(*made("A", (c, g, n) if (i, h) == (1, 1) else (c, g, n, i, h)))
                        for j in range(LEVELS):
                            for g in range(3):
                                dve.wait_ge(*after("V_mm", (c, j, g)))
                                dst = X if j == 0 else VB
                                if j >= 2:
                                    dve.wait_ge(*after("XT_mm", (c, j - 1, g)))
                                for d in range(2):
                                    V.tensor_tensor(dst[:, g, 2 * d:2 * d + 2, :],
                                                    PS[:, vbank(j, g), 256 * d:256 * d + 256].rearrange("p (u t) -> p u t", u=2),
                                                    lmask[:, j, d, :].unsqueeze(1).to_broadcast([P, 2, P]),
                                                    ALU.mult).then_inc(*made("V", (c, j, g) if d else (c, j, g, 0)))
                        for g in range(3):
                            dve.wait_ge(*after("Z_mm", (c, g)))
                            if g >= 1:
                                dve.wait_ge(*after("U_mm", (c, g - 1)))
                            for h in range(2):
                                V.tensor_copy(zs.rearrange("p (d h n) -> p d h n", d=2, h=2)[:, :, h, :],
                                              PS[:, (6, 4)[h], 0:P].rearrange("p (d n) -> p d n", d=2)).then_inc(*made("Z", (c, g) if h else (c, g, 0)))
                            if g < 2:
                                dve.wait_ge(*after("S_mm", (c, g)))
                                for d in range(2):
                                    t, tn = STEP_TILE[g][d], STEP_TILE[2][d]
                                    s = PS[:, 3, d * HD:(d + 1) * HD]
                                    if g == 0:
                                        V.tensor_scalar(Sfin[:, c, d, :], s, et[:, d, t:t + 1], None, ALU.mult).then_inc(*made("Sfin", (c, d)))
                                    else:
                                        V.tensor_tensor(stmp[:, d, :], s, SH[:, 1, d, :], ALU.add).then_inc(*made("stmp", (c, d)))
                                if g == 1:
                                    dve.wait_ge(*after("stmp", (c, 1)))
                                    for d in range(2):
                                        t, tn = STEP_TILE[g][d], STEP_TILE[2][d]
                                        V.tensor_scalar(SH[:, 2, d, :], stmp[:, d, :], et[:, d, t:t + 1], et[:, d, tn:tn + 1],
                                                        ALU.mult, ALU.mult).then_inc(*made("SH", (c, 2, d)))
                            if 1 <= g <= len(MOD_PAIRS_SOLVE[c]):
                                sum_mod(dve, MOD_PAIRS_SOLVE[c][g - 1])
                        if len(MOD_PAIRS_SOLVE[c]) == 3:
                            sum_mod(dve, MOD_PAIRS_SOLVE[c][2])
                    finish_mods(1, 16, 48, 1, "norm2_g", SC2)
                    dve.wait_ge(*after("y_raw", 2))
                    dve.wait_ge(*after("gate", 2))
                    for c in range(HC):
                        dve.wait_ge(*after("gn_mean_mm", c))
                        V.scalar_tensor_tensor(yT[:, c, :], PS[:, c, 0:TOK], -1.0 / HD, yT[:, c, :], ALU.mult, ALU.add).then_inc(*made("gn_d", c))
                        dve.wait_ge(*after("gn_d", c))
                        V.tensor_tensor((KAP[:, 0], KAP[:, 1], RT[:, 0])[c], yT[:, c, :], yT[:, c, :], ALU.mult).then_inc(*made("gn_sq", c))
                    def y_low(k):
                        dve.wait_ge(*after("y_hi", k))
                        V.tensor_tensor(y_lo[:, k, :], yT[:, k, :], y_hi[:, k, :].bitcast(F32), ALU.subtract).then_inc(*made("y_lo", k))

                    weights_lo(dve, S_OUT)
                    for k in range(HC, KC):
                        y_low(k)
                    for c in range(HC):
                        b = (KT[:, 0, :], KT[:, 1, :], BT[:, 0, :])[c]
                        dve.wait_ge(*after("gn_sqrt", c))
                        V.reciprocal(b, b).then_inc(*made("gn", (c, 0)))
                        dve.wait_ge(*after("gn", (c, 0)))
                        V.tensor_tensor(yT[:, c, :], yT[:, c, :], b, ALU.mult).then_inc(*made("gn", (c, 1)))
                        dve.wait_ge(*after("gn", (c, 1)))
                        V.tensor_scalar(yT[:, c, :], yT[:, c, :], vec[:, VEC["lnx_g"] + c:VEC["lnx_g"] + c + 1],
                                        vec[:, VEC["lnx_b"] + c:VEC["lnx_b"] + c + 1], ALU.mult, ALU.add).then_inc(*made("gn", (c, 2)))
                        dve.wait_ge(*after("gn", (c, 2)))
                        V.tensor_tensor(yT[:, c, :], yT[:, c, :], bonus[:, c, :], ALU.add).then_inc(*made("gn", (c, 3)))
                        dve.wait_ge(*after("gn", (c, 3)))
                        V.tensor_tensor(yT[:, c, :], yT[:, c, :], gate[:, c, :], ALU.mult).then_inc(*made("y_rwkv", c))

                    for k in range(HC):
                        y_low(k)
                    for m in range(KC):
                        if m % 2 == 0:
                            weights_lo(dve, S_OUT + m // 2 + 1)
                        dve.wait_ge(*after("out_mm", m))
                        for gi, (t0, t1) in enumerate(GROUPS):
                            V.scalar_tensor_tensor(xT[:, m, t0:t1], PS[:, m % 4, t0:t1], mods[:, G1 + m, gi:gi + 1], xT[:, m, t0:t1],
                                                   ALU.mult, ALU.add).then_inc(*made("x1", (m, gi)))
                    norm_apply("n2", 1, SH2)
                    for s in range(S_FFN, SLOTS):
                        if s + 1 < SLOTS:
                            weights_lo(dve, s + 1)
                        half, i = divmod(s - S_FFN, FFN_SLOTS)
                        if i < HALF:
                            f = half * HALF + i
                            row = tanh2[:, f % 2, :]
                            dve.wait_ge(*after("ff_tanh", f))
                            V.scalar_tensor_tensor(row, row, 1.0, PS[:, ff_bank(f), 0:TOK], ALU.add, ALU.mult).then_inc(*made("ff_silu", f))
                            dve.wait_ge(*after("ff_silu", f))
                            V.scalar_tensor_tensor(row, row, 0.5, PS[:, ff_bank(f) + 1, 0:TOK], ALU.mult, ALU.mult).then_inc(*made("ff", f))
                            dve.wait_ge(*after("ff_hi", f))
                            V.tensor_tensor(ff_lo[:, i, :], row, ff_hi[:, i, :].bitcast(F32), ALU.subtract).then_inc(*made("ff_lo", f))
                        for oh in range(2):
                            if s == fo_last(half, oh):
                                dve.wait_ge(*(after("ffo_mm", s) if oh else after("ffo_half", half)))
                                for m in range(4):
                                    for gi, (t0, t1) in enumerate(GROUPS):
                                        V.scalar_tensor_tensor(xT[:, 4 * oh + m, t0:t1], PS[:, fo_bank(half, oh) + m, t0:t1],
                                                               mods[:, G2 + 4 * oh + m, gi:gi + 1], xT[:, 4 * oh + m, t0:t1],
                                                               ALU.mult, ALU.add).then_inc(*made("x2", (half, oh, m, gi)))

                @block.tensor
                def _(pe):
                    T = nc.tensor

                    def need(s):
                        pe.wait_ge(*after(f"slot{s % RING}", s))
                        return ring[:, s % RING, :].rearrange("p (k n) -> p k n", k=KC)

                    def need_split(s, k=KC):
                        pe.wait_ge(*after("w_lo", s))
                        n = SPLIT.index(s) % 2
                        return (w_hi[:, n, :].rearrange("p (k n) -> p k n", k=k), w_lo[:, n, :].rearrange("p (k n) -> p k n", k=k))

                    def passes(out, lhs, rhs, start, stop):
                        T.matmul(out, lhs[0], rhs[0], start=start, stop=False)
                        T.matmul(out, lhs[0], rhs[1], start=False, stop=False)
                        return T.matmul(out, lhs[1], rhs[0], start=False, stop=stop)

                    pe.wait_ge(*after("vec_loaded", ("mue", 1)))
                    T.transpose(PS[:, 5, 0:P], vrow[:, :], ident).then_inc(*made("vec_tr"))
                    norm_pe(pe, "n1")

                    def mod_products(i):
                        pair = i // 2
                        w = need(mod_slot(i))
                        bank = mod_banks(pair)[0]
                        if pair >= 2 and i % 2 == 0:
                            pe.wait_ge(*after("mod_row", pair - 2))
                        if pair >= MOD_PAIRS_A and i % 2 == 0:
                            for c in range(HC):
                                if pair in MOD_PAIRS_SOLVE[c]:
                                    pe.wait_ge(*after("V", (c, LEVELS - 1, 2)))
                        for k in range(KC):
                            q = 32 * (k % 4)
                            mm = T.matmul(PS[q:q + 32, bank, 256 * (i % 2):256 * (i % 2) + 256], scond[:, k, :], w[:, k, :],
                                          start=(k < 4), stop=(k >= 4), tile_position=(0, q))
                        mm.then_inc(*made("mod_mm", mod_slot(i)))

                    def mod_transpose(pair):
                        pe.wait_ge(*after("mod_row", pair))
                        if pair >= 2:
                            pe.wait_ge(*after("mod_sum", pair - (2 if pair < MOD_PAIRS_A else 1)))
                        for b in range(4):
                            mm = T.transpose(PS[:, mod_banks(pair)[1], b * P:(b + 1) * P], mod_row(pair)[:, b * P:(b + 1) * P], ident)
                        mm.then_inc(*made("mod_tr", pair))

                    for pair in range(MOD_PAIRS_A + 1):
                        if pair < MOD_PAIRS_A:
                            mod_products(2 * pair)
                            mod_products(2 * pair + 1)
                        if pair:
                            mod_transpose(pair - 1)
                    for j in range(11):
                        at = P * (j % 2)
                        hi, lo = need_split(S_R + j // 2)
                        if j == 0:
                            pe.wait_ge(*after("vec"))
                            pe.wait_ge(*after("n1_low", (KC - 1, 1)))
                        if j >= 4:
                            pe.wait_ge(*after("u_own", j - 4))
                        for k in range(KC):
                            mm = passes(PS[:, j % 4, 0:TOK], (hi[:, k, at:at + P], lo[:, k, at:at + P]), (h_hi[:, k, :], h_lo[:, k, :]),
                                        k == 0, k == KC - 1)
                        mm.then_inc(*made("in_mm", j))
                    for n in range(18):
                        at, wd, t = tok_job(n)
                        s = S_GD if n < 3 else S_T + (n - 3) // 3
                        hi, lo = need_split(s)
                        q = 11 + n - 4
                        if q < 11:
                            pe.wait_ge(*after("u_own", q))
                        else:
                            o = q - 11
                            pe.wait_ge(*after("tok_dve" if o % 2 else "tok_act", o if o < 14 else 14))
                        a0 = 64 if n < 3 else 0
                        ts = slice(t * P, (t + 1) * P)
                        for k in range(KC):
                            mm = passes(PS[:, (11 + n) % 4, 0:wd], (h_hi[:, k, ts], h_lo[:, k, ts]), (hi[:, k, a0:a0 + wd], lo[:, k, a0:a0 + wd]),
                                        k == 0, k == KC - 1)
                        mm.then_inc(*made("in_mm", 11 + n))
                    pe.wait_ge(*after("shifted", 10))
                    for c in range(HC):
                        if c == 1:
                            pe.wait_ge(*after("vec"))
                        for t in range(TILES):
                            mm = T.transpose(PS[:, 4 + c, t * P:(t + 1) * P], uT[:, 6 + c, t * P:(t + 1) * P], ident)
                        mm.then_inc(*made("v_tr", c))
                    pe.wait_ge(*after("state_loaded", 1))
                    for d in range(2):
                        for c in range(HC):
                            mm = T.transpose(PS[:, 7, (3 * d + c) * HD:(3 * d + c + 1) * HD], sin_rows[:, d, c * P:(c + 1) * P], ident[0:HD, 0:HD])
                    mm.then_inc(*made("s0_tr"))
                    pe.wait_ge(*after("rope", 1))
                    pe.wait_ge(*after("tok_dve", 14))
                    pe.wait_ge(*after("tok_act", 14))
                    pe.wait_ge(*after("S0T"))
                    pe.wait_ge(*after("ctx_loaded", 1))
                    for c in range(HC):
                        cs = slice(c * P, (c + 1) * P)
                        ks = slice(DR + c * P, DR + (c + 1) * P)
                        for t in range(TILES):
                            src = tok[:, 0, cs] if t == 0 else rot[:, t - 1, cs]
                            mm = T.transpose(PS[:, 2 * c, t * P:(t + 1) * P], src, ident)
                        mm.then_inc(*made("q_tr", c))
                        for t in range(4):
                            src = (tok[:, 0, ks], ctxk[:, cs], rot[:, 0, ks], rot[:, 1, ks])[t]
                            mm = T.transpose(PS[:, 2 * c + 1, t * P:(t + 1) * P], src, ident)
                        mm.then_inc(*made("k_tr", c))

                    def scores(i):
                        t, h = divmod(i, HEADS)
                        k0, k1 = (0, P) if t == 0 else (P, 512)
                        if i < 2:
                            pe.wait_ge(*after("qT", 2))
                            pe.wait_ge(*after("kT", 2))
                        else:
                            pe.wait_ge(*after("exp", (i - 2, 1)))
                        for m in range(2):
                            c, r = divmod(2 * h + m, 4)
                            rows = slice(32 * r, 32 * r + 32)
                            mm = T.matmul(PS[:, 2 * (i % 2) + m, 0:k1 - k0], qT[rows, c, t * P:(t + 1) * P], kT[rows, c, k0:k1],
                                          start=True, stop=True)
                        mm.then_inc(*made("scores", i))

                    def p_transpose(i):
                        pe.wait_ge(*after("pdiff", i))
                        if i >= 2:
                            pe.wait_ge(*after("pdT", i - 2))
                        for kt in range(1 if i < HEADS else 3):
                            mm = T.transpose(PS[:, 4 + i % 2, kt * P:(kt + 1) * P], pdiff[:, i % 2, kt * P:(kt + 1) * P], ident)
                        mm.then_inc(*made("p_tr", i))

                    def values(i):
                        t, h = divmod(i, HEADS)
                        pe.wait_ge(*after("pdT", i))
                        if t == 2 and h == 0:
                            pe.wait_ge(*after("o", 0))
                        vs = slice(768 + h * HD, 768 + (h + 1) * HD)
                        vals = [tok[:, 0, vs]] if t == 0 else [ctxv[:, h * HD:(h + 1) * HD], tok[:, 1, vs], tok[:, 2, vs]]
                        for kt, v in enumerate(vals):
                            mm = T.matmul(PS[:, 6 + t % 2, h * HD:(h + 1) * HD], pdT[:, i % 2, kt * P:(kt + 1) * P], v,
                                          start=(kt == 0), stop=(kt == len(vals) - 1))
                        mm.then_inc(*made("pv", i))

                    for i in range(18 + 2):
                        if i < 18:
                            scores(i)
                        if 1 <= i <= 18:
                            p_transpose(i - 1)
                        if i >= 2:
                            values(i - 2)
                    pe.wait_ge(*after("gd_sig"))
                    pe.wait_ge(*after("lora_loaded", 2))
                    pe.wait_ge(*after("exp", (17, 1)))
                    for c in range(HC):
                        T.matmul(PS[:, c, 0:TOK], gup[:, c * P:(c + 1) * P], tanh2[0:64, 1, :], start=True, stop=True).then_inc(*made("gate_mm", c))
                    for c in range(HC):
                        pe.wait_ge(*after("kk_sq", c))
                        if c == 0:
                            pe.wait_ge(*after("pdT", 17))
                        T.matmul(PS[:, 3 + c, 0:TOK], bones, (LW, EI, EX)[c][:, :], start=True, stop=True).then_inc(*made("kk_ss", c))
                    for t in range(TILES):
                        pe.wait_ge(*after("o_n", t))
                        pe.wait_ge(*after("gate", t))
                        for c in range(HC):
                            mm = T.transpose(PS[:, t, c * P:(c + 1) * P], osb[:, t, c * P:(c + 1) * P], ident)
                        mm.then_inc(*made("o_tr", t))
                    pe.wait_ge(*after("kk_sqrt", 2))
                    pe.wait_ge(*after("o", 2))
                    for dc in range(2):
                        fs = slice(FNET0 + dc * P, FNET0 + (dc + 1) * P)
                        T.matmul(PS[:, 4 + 2 * dc, 0:256], tok[:, 0, fs], dft_prompt, start=True, stop=True)
                        for t in range(2):
                            mm = T.matmul(PS[:, 5 + 2 * dc, :], tok[:, 1 + t, fs], dft_sample[:, t, :], start=(t == 0), stop=(t == 1))
                        mm.then_inc(*made("fz_mm", dc))
                    for dc in range(2):
                        pe.wait_ge(*after("fz", (dc, 1)))
                        pe.wait_ge(*after("y_attn", dc))
                        for m in range(2):
                            T.matmul(PS[:, dc, 0:SEQ], dft_dim[:, m, :], fz[:, dc, m * SEQ:(m + 1) * SEQ], start=(m == 0), stop=(m == 1))
                        for m in range(2):
                            mm = T.matmul(PS[:, dc, SEQ:TOK], dft_dim[:, m, :], fz[:, dc, 256 + m * DEC:256 + (m + 1) * DEC], start=(m == 0), stop=(m == 1))
                        mm.then_inc(*made("fnet_mm", dc))

                    for c in range(HC):
                        cs = slice(c * P, (c + 1) * P)
                        for d in range(2):
                            if (c, d) == (0, 0):
                                pe.wait_ge(*after("wd_tanh"))
                                pe.wait_ge(*after("y_fnet", 1))
                            else:
                                pe.wait_ge(*after("a_tanh", (c, 0) if d else (c - 1, 1)))
                                if d == 0:
                                    pe.wait_ge(*after("V", (c - 1, 6, 2)))
                                    pe.wait_ge(*after("mod_sum", MOD_PAIRS_SOLVE[c - 1][-1]))
                            r = slice(32 * d, 32 * d + 32)
                            T.matmul(PS[:, 0, 0:TOK], lora[r, cs], tanh2[r, 0, :], start=True, stop=True)
                            r = slice(64 + 32 * d, 96 + 32 * d)
                            T.matmul(PS[:, 1, 0:TOK], lora[r, cs], uT[r, 9, :], start=True, stop=True).then_inc(*made("lora_mm", (c, d)))
                        pe.wait_ge(*after("b_scaled", (c, 1)))
                        pe.wait_ge(*after("y_attn", 2))
                        if c >= 1:
                            pe.wait_ge(*after("XT", (c - 1, 6, 2)))
                            pe.wait_ge(*after("stmp", (c - 1, 1)))
                        for i, src in enumerate((KT, BT)):
                            for d in range(2):
                                for g in range(2):
                                    t = STEP_TILE[g][d]
                                    mm = T.transpose(PS[:, 2 + i, (2 * d + g) * P:(2 * d + g + 1) * P], src[:, d, t * P:(t + 1) * P], ident)
                        mm.then_inc(*made("kt_tr", c))
                        pe.wait_ge(*after("bonus_r", c))
                        if c == 0:
                            pe.wait_ge(*after("fz", (1, 1)))
                        else:
                            pe.wait_ge(*after("stmp", (c - 1, 1)))
                        T.matmul(PS[:, 4, 0:TOK], bones, gsum[:, :], start=True, stop=True).then_inc(*made("bonus_mm", c))
                        pe.wait_ge(*after("r", (c, 1)))
                        pe.wait_ge(*after("kap", (c, 1)))
                        for g in range(3):
                            for n, rhs in enumerate((KAP, RT)):
                                if g:
                                    pe.wait_ge(*after("A", (c, g - 1, n)))
                                elif n == 0:
                                    pe.wait_ge(*after("a_tanh", (c, 1)))
                                else:
                                    pe.wait_ge(*after("fz", (1, 1)) if c == 0 else after("y_raw", c - 1))
                                for i, lhs in enumerate((BT, KT)):
                                    for d in range(2):
                                        t = STEP_TILE[g][d]
                                        ts = slice(t * P, (t + 1) * P)
                                        for h in range(2):
                                            hs = slice(h * HD, (h + 1) * HD)
                                            mm = T.matmul(PS[:, abank(2 * g + n, h), (2 * i + d) * P:(2 * i + d + 1) * P],
                                                          lhs[hs, d, ts], rhs[hs, d, ts], start=True, stop=True)
                                mm.then_inc(*made("A_mm", (c, g, n)))
                        if c == 0:
                            pass
                        pe.wait_ge(*after("A", (c, 2, 1)))
                        pe.wait_ge(*after("btok", c))
                        pe.wait_ge(*after("bonus", c))
                        for j in range(LEVELS):
                            def join(j, g):
                                if j == 0:
                                    pe.wait_ge(*after("A1", (c, g)))
                                    pe.wait_ge(*after("V", (c, 0, g - 2)) if g == 2 else after("A", (c, 2, 1)))
                                else:
                                    pe.wait_ge(*after("V", (c, 0, g)) if j == 1 else after("X", (c, j - 1, g)))
                                    pj, pg = divmod(3 * j + g - 2, 3)
                                    pe.wait_ge(*after("V", (c, pj, pg)))
                                for u in range(4):
                                    mm = T.matmul(PS[:, vbank(j, g), u * P:(u + 1) * P], AKB[:, g, u, :], ident if j == 0 else X[:, g, u, :],
                                                  start=True, stop=True)
                                mm.then_inc(*made("V_mm", (c, j, g)))

                            def merge(j, g):
                                pe.wait_ge(*after("V", (c, j, g)))
                                if j == 1:
                                    pe.wait_ge(*after("XT0", (c, g, 1)))
                                else:
                                    pe.wait_ge(*after("XT", (c, j - 1, g)))
                                if 3 * j + g - 2 >= 3:
                                    pj, pg = divmod(3 * j + g - 2, 3)
                                    pe.wait_ge(*after("XT", (c, pj, pg)))
                                b = xbank(j, g)
                                if j < LEVELS - 1:
                                    for u in range(4):
                                        mm = T.matmul(PS[:, b, u * P:(u + 1) * P], XT[:, g, u, :], VB[:, g, u, :], start=True, stop=True)
                                    mm.then_inc(*made("X_mm", (c, j, g)))
                                for u in range(4):
                                    mm = T.matmul(PS[:, b + 1, u * P:(u + 1) * P], VB[:, g, u, :], XT[:, g, u, :], start=True, stop=True)
                                mm.then_inc(*made("XT_mm", (c, j, g)))

                            for g in range(3):
                                join(j, g)
                                if j >= 1 and g >= 1:
                                    merge(j, g - 1)
                            if j >= 1:
                                merge(j, 2)
                        pe.wait_ge(*after("XT", (c, LEVELS - 1, 2)))
                        for g in range(3):
                            if g == 0:
                                pe.wait_ge(*after("A", (c, 2, 1)))
                            else:
                                pe.wait_ge(*after("Z", (c, g - 1)))
                                pe.wait_ge(*after("SH", (c, g, 1)))
                            for d in range(2):
                                t = STEP_TILE[g][d]
                                for h in range(2):
                                    hs = slice(h * HD, (h + 1) * HD)
                                    u = 2 * d + h
                                    o = PS[:, (6, 4)[h], d * HD:(d + 1) * HD]
                                    if g:
                                        T.matmul(o, KAP[hs, d, t * P:(t + 1) * P], SH[hs, g, d, :], start=True, stop=False)
                                    mm = T.matmul(o, AKV[:, g, u, :], vtok[:, t, c * P + h * HD:c * P + (h + 1) * HD], start=(g == 0), stop=True)
                            mm.then_inc(*made("Z_mm", (c, g)))
                            pairs = MOD_PAIRS_SOLVE[c]
                            if g < len(pairs):
                                mod_products(2 * pairs[g])
                            if 1 <= g <= len(pairs):
                                mod_transpose(pairs[g - 1])
                            pe.wait_ge(*after("Z", (c, g)))
                            if g:
                                pe.wait_ge(*after("U", (c, g - 1)))
                            for u in range(4):
                                mm = T.matmul(PS[:, 7, u * HD:(u + 1) * HD], XT[:, g, u, :], zs[:, u * HD:(u + 1) * HD], start=True, stop=True)
                            mm.then_inc(*made("U_mm", (c, g)))
                            if g < len(pairs):
                                mod_products(2 * pairs[g] + 1)
                            pe.wait_ge(*after("U", (c, g)))
                            if g == 1:
                                pe.wait_ge(*after("Sfin", (c, 1)))
                            if g < 2:
                                for d in range(2):
                                    t = STEP_TILE[g][d]
                                    for h in range(2):
                                        hs = slice(h * HD, (h + 1) * HD)
                                        u = 2 * d + h
                                        o = PS[hs, 3, d * HD:(d + 1) * HD]
                                        T.matmul(o, ktok[:, d, g, hs], vtok[:, t, c * P + h * HD:c * P + (h + 1) * HD], start=True, stop=False)
                                        mm = T.matmul(o, btok[:, d, g, hs], usb[:, g, u * HD:(u + 1) * HD], start=False, stop=True)
                                mm.then_inc(*made("S_mm", (c, g)))
                        for h in range(2):
                            hs = slice(h * HD, (h + 1) * HD)
                            for t in range(TILES):
                                ts = slice(t * P, (t + 1) * P)
                                ops = []
                                for d in range(2):
                                    g = [st[d] for st in STEP_TILE].index(t)
                                    u = 2 * d + h
                                    if g:
                                        ops.append((SH[hs, g, d, :], RT[hs, d, ts]))
                                    ops.append((vtok[:, t, c * P + h * HD:c * P + (h + 1) * HD], ARV[:, g, u, :]))
                                    ops.append((usb[:, g, u * HD:(u + 1) * HD], ARB[:, g, u, :]))
                                for i, (lhs, rhs) in enumerate(ops):
                                    mm = T.matmul(PS[hs, 5 + h, ts], lhs, rhs, start=(i == 0), stop=(i == len(ops) - 1))
                        mm.then_inc(*made("Y_mm", c))
                        if len(pairs) == 3:
                            mod_transpose(pairs[2])
                    pe.wait_ge(*after("Sfin", (2, 1)))
                    pe.wait_ge(*after("U", (2, 2)))
                    pe.wait_ge(*after("y_raw", 2))
                    for d in range(2):
                        for c in range(HC):
                            mm = T.transpose(PS[0:HD, 6 + d, c * P:(c + 1) * P], Sfin[:, c, d, :], ident)
                        mm.then_inc(*made("st_tr", d))
                    for c in range(HC):
                        pe.wait_ge(*after("y_raw", c))
                        if c == 0:
                            pe.wait_ge(*after("V", (2, 6, 2)))
                            pe.wait_ge(*after("XT", (2, 6, 2)))
                            pe.wait_ge(*after("mod_sum", MOD_PAIRS_SOLVE[2][-1]))
                        T.matmul(PS[:, c, 0:TOK], bones, yT[:, c, :], start=True, stop=True).then_inc(*made("gn_mean_mm", c))
                    for c in range(HC):
                        pe.wait_ge(*after("gn_sq", c))
                        T.matmul(PS[:, 3 + c, 0:TOK], bones, (KAP[:, 0, :], KAP[:, 1, :], RT[:, 0, :])[c], start=True, stop=True).then_inc(*made("gn_var_mm", c))
                    for m in range(KC):
                        hi, lo = need_split(S_OUT + m // 2)
                        if m == 0:
                            pe.wait_ge(*after("gn_sqrt", 2))
                        if m >= 4:
                            pe.wait_ge(*after("x1", (m - 4, 1)))
                        ms = slice((m % 2) * P, (m % 2 + 1) * P)
                        order = [*range(HC, KC), *range(HC)]
                        for k in order:
                            if m == 0:
                                pe.wait_ge(*after("y_lo", k))
                            mm = passes(PS[:, m % 4, 0:TOK], (hi[:, k, ms], lo[:, k, ms]), (y_hi[:, k, :], y_lo[:, k, :]),
                                        k == order[0], k == order[-1])
                        mm.then_inc(*made("out_mm", m))
                    pe.wait_ge(*after("state_rows", 1))
                    norm_pe(pe, "n2")
                    for s in range(S_FFN, SLOTS):
                        half, i = divmod(s - S_FFN, FFN_SLOTS)
                        if i < HALF:
                            f = half * HALF + i
                            hi, lo = need_split(s)
                            if f == 0:
                                pe.wait_ge(*after("n2_low", (KC - 1, 1)))
                            if f >= 2:
                                pe.wait_ge(*after("ff", f - 2))
                            if f == HALF:
                                pe.wait_ge(*after("x2", (0, 0, 3, 1)))
                            for b in range(2):
                                bs = slice(b * P, (b + 1) * P)
                                for k in range(KC):
                                    mm = passes(PS[:, ff_bank(f) + b, 0:TOK], (hi[:, k, bs], lo[:, k, bs]), (h_hi[:, k, :], h_lo[:, k, :]),
                                                k == 0, k == KC - 1)
                            mm.then_inc(*made("ff_mm", f))
                            continue
                        hi, lo = need_split(s, 4)
                        for u in range(4 * (i - HALF), min(4 * (i - HALF) + 4, 2 * HALF)):
                            oh, k = divmod(u, HALF)
                            if oh == 0:
                                pe.wait_ge(*after("ff_lo", half * HALF + k))
                            if half == 1 and u == 0:
                                pe.wait_ge(*after("x2", (0, 1, 3, 1)))
                            for m in range(4):
                                ms = slice(m * P, (m + 1) * P)
                                mm = passes(PS[:, fo_bank(half, oh) + m, 0:TOK], (hi[:, u % 4, ms], lo[:, u % 4, ms]), (ff_hi[:, k, :], ff_lo[:, k, :]),
                                            k == 0, k == HALF - 1)
                            if u == HALF - 1:
                                mm.then_inc(*made("ffo_half", half))
                        mm.then_inc(*made("ffo_mm", s))

            reset([sems[n] for n in sems if n not in prologue_names])

        with nc.Block() as block:
            @block.scalar
            def _(act):
                norm_act(act, "n3")

            @block.tensor
            def _(pe):
                norm_pe(pe, "n3")
                for t in range(TILES):
                    for half in range(2):
                        b = (2 * t + half) % 4
                        if 2 * t + half >= 4:
                            pe.wait_ge(*after("y_rows", 2 * t + half - 4))
                        for k in range(4):
                            kk_ = 4 * half + k
                            if t == 0:
                                pe.wait_ge(*after("n3_h", kk_))
                            mm = nc.tensor.transpose(PS[:, b, k * P:(k + 1) * P], yT[:, kk_, t * P:(t + 1) * P], ident)
                        mm.then_inc(*made("y_tr", 2 * t + half))

            @block.vector
            def _(dve):
                dve.wait_ge(*after("n3_sqrt"))
                nc.vector.reciprocal(rstd[:, :], rstd[:, :]).then_inc(*made("n3_rstd"))
                dve.wait_ge(*after("n3_rstd"))
                for k in range(KC):
                    nc.vector.scalar_tensor_tensor(yT[:, k, :], xT[:, k, :], fing[:, k:k + 1], rstd[:, :], ALU.mult,
                                                   ALU.mult).then_inc(*made("n3_h", k))
                for i in range(6):
                    dve.wait_ge(*after("y_tr", i))
                    if i == 0:
                        dve.wait_ge(*after("n3_ss"))
                    nc.vector.tensor_copy(xin[:, i // 2, (i % 2) * 512:(i % 2) * 512 + 512], PS[:, i % 4, :]).then_inc(*made("y_rows", i))

            @block.sync
            def _(sp):
                sp.wait_ge(*after("y_rows", 1))
                sp.dma_start(a["out_p"][0], xin[:, 0, :]).then_inc(*loaded("y_stored"))
                for t in range(1, TILES):
                    sp.wait_ge(*after("y_rows", 2 * t + 1))
                    sp.dma_start(a["out_x"][0, (t - 1) * P:t * P, :], xin[:, t, :]).then_inc(*loaded("y_stored", t))
                sp.wait_ge(*after("y_stored", 2))


def kernel(**inputs):
    import numpy as _np
    import concourse.bacc as _bacc
    from concourse.bass_utils import run_bass_kernel_spmd as _run

    lay = {
        "x_prompt": None, "x_sample": None, "c": None, "c_ctx": None, "norm1_g": None, "norm2_g": None,
        "final_norm_g": None, "w_mod": None, "b_mod": None, "w_in": None, "w_out": None, "shift_mu": None,
        "decay_w0": None, "decay_up": None, "iclr_a0": None, "iclr_up": None, "gate_up": None, "k_k": None,
        "k_a": None, "r_k": None, "lnx_g": None, "lnx_b": None, "diff_lambda": None, "subln_g": None,
        "w_ffn_in": None, "w_ffn_out": None,
        "state": ("state_rwkv", (DEPTH, 2, HEADS, HD, HD)),
        "cache_k": ("cache_diff_k", (DEPTH, P, DR)),
        "cache_v": ("cache_diff_v", (DEPTH, P, DR)),
    }
    arrays = {}
    for name, how in lay.items():
        v = _np.ascontiguousarray(inputs[how[0] if how else name])
        arrays[name] = v.reshape(how[1]) if how else v
    arrays["tables"] = packed_tables()
    arrays["lam_init"] = lam_table()
    outs = {"out_p": (1, SEQ, D), "out_x": (1, DEC, D), "out_s": (DEPTH, 2, HEADS, HD, HD),
            "out_k": (DEPTH, SEQ, DR), "out_v": (DEPTH, SEQ, DR)}
    counts = {}
    for _ in range(2):
        nc = _bacc.Bacc("TRN2", target_bir_lowering=False, num_devices=1, dynamic_dma_scratch_size=1024)
        a = {n: nc.dram_tensor("in_" + n, v.shape, F32, kind="ExternalInput").ap() for n, v in arrays.items()}
        a.update({n: nc.dram_tensor(n, s, F32, kind="ExternalOutput").ap() for n, s in outs.items()})
        build(nc, a, counts)
    r = _run(nc, [{"in_" + n: v for n, v in arrays.items()}], core_ids=[0]).results[0]
    return (r["out_p"], r["out_x"], r["out_s"].reshape(1, DEPTH, 2, HEADS, HD, HD),
            r["out_k"].reshape(1, DEPTH, SEQ, HEADS, 2, DQK), r["out_v"].reshape(1, DEPTH, SEQ, HEADS, HD))
```

```python
import math
from contextlib import ExitStack

import numpy as np

import concourse.bass as bass
from concourse import mybir

F32 = mybir.dt.float32
F32R = mybir.dt.float32r
ALU = mybir.AluOpType
ACT = mybir.ActivationFunctionType
AX = mybir.AxisListType

P = 128
D = 1024
KC = D // P
DEPTH = 2
SEQ, DEC = 128, 256
TOK = SEQ + DEC
TILES = TOK // P
HD = 64
DR = 384
HC = DR // P
HEADS = DR // HD
DQK = 32
NR = 1344
FNET0 = 1152
NTOK = 1408
DIN = NR + NTOK
DFF = 2816
FC = DFF // P
GRID_W = 64
RMS_EPS, GN_EPS, SUBLN_EPS = 1e-6, 64e-5, 1e-5
DECAY = math.exp(-0.5)
QSCALE = DQK ** -0.5
GROUPS = ((0, SEQ), (SEQ, TOK))
RING = 4
LEVELS = 7

VEC = {}
_row = 0
for _name, _n in (("norm1_g", 8), ("norm2_g", 8), ("b_mod", 48), ("decay_w0", 6), ("iclr_a0", 6), ("k_k", 3),
                  ("k_a", 3), ("r_k", 3), ("lnx_g", 3), ("lnx_b", 3), ("subln_g", 1), ("mu0", 11), ("mu1", 11)):
    VEC[_name] = _row
    _row += _n
SH1, SC1, G1, SH2, SC2, G2 = range(0, 48, 8)

R_AT = [4, 5, 10, 11, 12]
S_GD, S_T, S_MOD_B, S_OUT, S_FFN = 13, 14, 19, 35, 39
HALF = FC // 2
FO_SLOTS = -(-2 * HALF // 4)
FFN_SLOTS = HALF + FO_SLOTS
SLOTS = S_FFN + 2 * FFN_SLOTS
SPLIT = [*R_AT, *range(S_GD, S_MOD_B), *range(S_OUT, SLOTS)]
MOD_AT = [0, 1, 2, 3, 6, 7, 8, 9, *range(S_MOD_B, S_OUT)]
MOD_PAIRS_A = 4
AHEAD = 4
MOD_PAIRS_SOLVE = ((4, 5, 6), (7, 8, 9), (10, 11))

FIRST_BLOCKS = [(k, b) for k in range(4) for b in range(4)] + [(k, b) for k in range(4, KC) for b in (0, 1)] + \
    [(k, b) for k in range(4, KC) for b in (2, 3)]

STAGES = {
    "vector_setup": "vec dvec lam_dots mod_sum mods gmod lam",
    "vector_norm1": "n1_rstd n1_scaled",
    "vector_norm2": "n2_rstd n2_scaled",
    "vector_shift": "u_prev shifted",
    "vector_layouts": "gd_sig vtok S0T kT",
    "vector_attention": "max neg_max rinv rlam p1 pdiff o",
    "vector_subnorm": "o_sq o_ms o_rinv o_n",
    "vector_keys": "kk_raw kk_sq kk_den kk",
    "vector_decay": "LW sum nh EI EX kap r k_scaled b_scaled",
    "vector_bonus": "bonus_k bonus_r bonus",
    "vector_solve": "Z Sfin stmp SH",
    "vector_groupnorm": "gn_d gn_sq gn y_rwkv",
    "vector_ffn": "ff_silu ff",
    "vector_prologue": "xT cond_cols final_g cond_half cond",
    "scalar_inputs": "u_copy u_own wd_tanh gd_tanh",
    "scalar_sqrt": "o_sqrt kk_sqrt",
    "scalar_outputs": "y_attn fz y_fnet gate",
    "scalar_decay": "w_tanh a_tanh e_kap e_r e_3 e_tot",
    "scalar_keys": "ktok btok",
    "scalar_merge": "X XT",
    "scalar_solve": "U y_raw state_rows",
    "pool_rope": "rope_cos rope_sin rope",
    "pool_keys": "a b ka kd",
    "pool_merge": "A1 XT0",
    "vector_low": "n1_low n2_low y_lo ff_lo",
    "tensor_norm": "vec_tr n1_ss n2_ss",
    "tensor_layouts": "v_tr s0_tr q_tr k_tr",
    "tensor_attention": "scores p_tr pv",
    "tensor_mixed": "gate_mm kk_ss o_tr fz_mm fnet_mm",
    "tensor_decay": "lora_mm kt_tr bonus_mm",
    "tensor_merge": "V_mm X_mm XT_mm",
    "tensor_solve": "Z_mm U_mm S_mm Y_mm st_tr",
    "tensor_groupnorm": "gn_mean_mm gn_var_mm",
    "tensor_ffn_out": "ffo_mm ffo_half",
}
STAGE_OF = {step: stage for stage, steps in STAGES.items() for step in steps.split()}

STEP_TILE = ((0, 0), (1, 2), (2, 1))


def tables():
    i = np.arange(P)
    eye = np.eye(P)
    t = {"ident": eye, "ones": np.ones((P, P)), "bones": (i[:, None] // HD == i[None] // HD) * 1.0}
    s, q = i[:, None], i[None]
    t["amask"] = np.concatenate([s < q, s > q, s <= q, s >= q], 1) * 1.0
    lm = []
    for j in range(LEVELS):
        b = 1 << j
        low = (s // (2 * b) == q // (2 * b)) & (s // b % 2 == 1) & (q // b % 2 == 0)
        lm += [eye - low, eye - low.T]
    t["lmask"] = np.concatenate(lm, 1)
    t["smask"] = np.tile((np.arange(TOK) % P != 0) * 1.0, (P, 1))
    f = np.float32
    pos = np.arange(DEC)
    row, col = (pos // GRID_W).astype(f), (pos % GRID_W).astype(f)
    inv = (1.0 / (f(10000.0) ** (np.arange(8, dtype=f) / f(8)))).astype(f)
    ang = np.stack([row[:, None] * inv, col[:, None] * inv], 1)
    cs, sn = np.cos(ang), np.sin(ang)
    cos = np.stack([cs, cs], 2).reshape(2, P, 32)
    sin = np.stack([-sn, sn], 2).reshape(2, P, 32)
    t["cos"] = cos.transpose(1, 0, 2).reshape(P, 64)
    t["sin"] = sin.transpose(1, 0, 2).reshape(P, 64)

    def dft(n):
        a = 2 * np.pi * (np.outer(np.arange(n), np.arange(n)) % n) / n
        return np.cos(a) / np.sqrt(n), np.sin(a) / np.sqrt(n)

    c, s_ = dft(SEQ)
    t["dft_prompt"] = np.concatenate([c, s_], 1)
    c, s_ = dft(DEC)
    t["dft_sample"] = np.concatenate([c, s_], 1).reshape(2, P, 512).transpose(1, 0, 2).reshape(P, 1024)
    c, s_ = dft(HD)
    z = np.zeros((HD, HD))
    t["dft_dim"] = np.concatenate([np.block([[c, z], [z, c]]), -np.block([[s_, z], [z, s_]])], 1)
    return t


TABLES = tables()
TABLE_AT = {}
_at = 0
for _k, _v in TABLES.items():
    TABLE_AT[_k] = (_at, _v.shape[1])
    _at += _v.shape[1]
NTABLE = _at


def packed_tables():
    return np.concatenate(list(TABLES.values()), 1).astype(np.float32)


def lam_table():
    li = np.array([0.8 - 0.6 * math.exp(-0.3 * l) for l in range(DEPTH)])
    return np.repeat(np.stack([li, 1 - li], 1)[:, None], P, 1).astype(np.float32)


def build(nc, a, counts):
    ctx = ExitStack()
    with ctx:
        def sb(name, shape, dt=F32):
            return ctx.enter_context(nc.sbuf_tensor(name, shape, dt))

        sems = {}
        seen = {}
        counted = bool(counts)

        def sem(name):
            if name not in sems:
                sems[name] = ctx.enter_context(nc.semaphore(name))
            return sems[name]

        def made(name, key=0, by=1):
            stage = STAGE_OF.get(name, name)
            seen[stage] = seen.get(stage, 0) + by
            counts[name, key] = seen[stage]
            return sem(stage), by

        def loaded(name, key=0):
            return made(name, key, 16)

        def after(name, key=0):
            return sem(STAGE_OF.get(name, name)), counts[name, key] if counted else 1

        tab = sb("tab", [P, NTABLE])

        def table(name):
            at, n = TABLE_AT[name]
            return tab[:, at:at + n]

        ident, ones, bones = table("ident"), table("ones"), table("bones")
        amask = table("amask").rearrange("p (m t) -> p m t", m=4)
        lmask = table("lmask").rearrange("p (j d t) -> p j d t", j=LEVELS, d=2)
        smask = table("smask")
        cos = table("cos").rearrange("p (t n) -> p t n", t=2)
        sin = table("sin").rearrange("p (t x h n) -> p t x h n", t=2, x=2, h=2)
        dft_prompt = table("dft_prompt")
        dft_sample = table("dft_sample").rearrange("p (t n) -> p t n", t=2)
        dft_dim = table("dft_dim").rearrange("p (m n) -> p m n", m=2)

        def region(name, shape):
            if nc.sbuf_base % 32:
                nc.bump_sbuf(32 - nc.sbuf_base % 32)
            at = nc.sbuf_base
            return sb(name, shape), at

        def split(name, shape, at, words=0):
            return nc.alloc_sbuf_tensor_at(name, shape, F32R, offset=at + 4 * words)

        xT = sb("xT", [P, KC, TOK])
        hT, hT_at = region("hT", [P, KC, TOK])
        h_hi = split("h_hi", [P, KC, TOK], hT_at)
        h_lo = sb("h_lo", [P, KC, TOK], F32R)
        yT = sb("yT", [P, KC, TOK])
        ring = sb("ring", [P, RING, 2048])
        big, big_at = region("big", [P, FC * TOK])
        y_hi = split("y_hi", [P, KC, TOK], big_at)
        y_lo = split("y_lo", [P, KC, TOK], big_at, KC * TOK)
        ff_hi = split("ff_hi", [P, HALF, TOK], big_at)
        ff_lo = split("ff_lo", [P, HALF, TOK], big_at, HALF * TOK)
        tok = big[:, 0:TILES * NTOK].rearrange("p (t n) -> p t n", t=TILES)
        uT = big[:, TILES * NTOK:].rearrange("p (c t) -> p c t", c=11)
        xsq = big[:, 0:KC * TOK].rearrange("p (k t) -> p k t", k=KC)
        xin = big[:, 0:TILES * D].rearrange("p (t n) -> p t n", t=TILES)

        share, share_at = region("share", [P, 10752])
        w_hi = split("w_hi", [P, 2, 2048], share_at)
        w_lo = split("w_lo", [P, 2, 2048], share_at, 4096)
        cut = [0]

        def part(n):
            cut[0] += n
            return share[:, cut[0] - n:cut[0]]

        swapped = share[:, 8192:8192 + 1536].rearrange("p (t n) -> p t n", t=2)
        qT = part(HC * TOK).rearrange("p (c t) -> p c t", c=HC)
        kT = part(HC * 512).rearrange("p (c t) -> p c t", c=HC)
        prob = part(1536).rearrange("p (b m t) -> p b m t", b=2, m=2)
        pdiff = part(768).rearrange("p (b t) -> p b t", b=2)
        pdT = part(768).rearrange("p (b t) -> p b t", b=2)
        osb = part(TILES * DR).rearrange("p (t n) -> p t n", t=TILES)
        assert cut[0] <= 10752 - 2 * DR
        ctxk = share[:, 10752 - 2 * DR:10752 - DR]
        ctxv = share[:, 10752 - DR:10752]
        cut[0] = 0
        AKB, AKV, ARB, ARV = (part(1536).rearrange("p (g u t) -> p g u t", g=3, u=4) for _ in range(4))
        X, XT, VB = (part(1536).rearrange("p (g u t) -> p g u t", g=3, u=4) for _ in range(3))

        kk = yT[:, 0:HC, :]
        vtok = sb("vtok", [P, TILES, DR])
        bonus = hT[:, 0:HC, :]
        gate = hT[:, HC:2 * HC, :]
        late = sb("late", [P, 2, 2, TOK])
        late_odd = big[:, 0:1536].rearrange("p (a d t) -> p a d t", a=2, d=2)
        KAP, RT = (late[:, 0], late_odd[:, 0]), (late[:, 1], late_odd[:, 1])
        fz = share[:, 0:1536].rearrange("p (a n) -> p a n", a=2)
        BT, KT, KD = (sb(n, [P, 2, TOK]) for n in ("BT", "KT", "KD"))
        E3 = sb("E3", [P, TOK])
        LW, EI, EX, AA = ((sb(n, [P, TOK]), big[:, 2560 + i * TOK:2560 + (i + 1) * TOK], share[:, 8192 + i * TOK:8192 + (i + 1) * TOK])
                          for i, n in enumerate(("LW", "EI", "EX", "AA")))
        mod_rows = big[:, 3072:4096].rearrange("p (b n) -> p b n", b=2)
        ktok = sb("ktok", [P, 2, 2, P])
        btok = sb("btok", [P, 2, 2, P])
        upad = late[:, :, :, :].rearrange("p a d t -> p (a d t)")[:, 0:2 * (TOK + 3)].rearrange("p (b t) -> p b t", b=2)
        tanh2 = sb("tanh2", [P, 2, TOK])
        gsum = rstd = sb("gsum", [P, TOK])

        vrow = LW[0][:, 0:P]
        vec = sb("vec", [P, P])
        mods = sb("mods", [P, 48, 2])
        gmod = sb("gmod", [P, 2, KC, 2])
        scond = sb("scond", [P, KC, 32])
        fing = sb("fing", [P, KC])
        dvec = sb("dvec", [P, 64])
        muc, w0h, a0h, omka, subs = (dvec[:, 0:11], dvec[:, 11:17], dvec[:, 17:23], dvec[:, 23:26], dvec[:, 26:27])
        eps = sb("eps", [P, 4])
        lora = sb("lora", [P, DR])
        gup = sb("gup", [HD, DR])
        lrow = E3[:, 0:P]
        lprod = sb("lprod", [P, 2, DQK])
        lsum = sb("lsum", [P, 8])
        lamc = sb("lamc", [P, 2])
        lam = sb("lam", [P, 1])
        amax = sb("amax", [P, 2, 2])
        nmax = sb("nmax", [P, 2, 2])
        rsum = sb("rsum", [P, 2, 2])
        rinv = sb("rinv", [P, 2, 2])
        onorm = sb("onorm", [P, 18])
        zs = AA[0][:, 0:256]
        usb = hT[:, 6:8, :].rearrange("p k t -> p (k t)").rearrange("p (g n) -> p g n", g=3)
        nh = sb("nh", [P, 2, 3])
        et = sb("et", [P, 2, 2, 3])
        sin_rows = BT[0:HD, :, :]
        S0T = sb("S0T", [P, 2, HC, HD])
        SH = sb("SH", [P, 3, 2, HD])
        stmp = sb("stmp", [P, 2, HD])
        Sfin = sb("Sfin", [P, HC, 2, HD])
        sout = KD[0:HD, :, :]
        PS = ctx.enter_context(nc.psum_tensor("PS", [P, 8, 512], F32))

        def layer(x, l):
            s = x[bass.ds(l, 1)]
            n = len(x.shape)
            names = " ".join("bcdefg"[:n - 1])
            first = names.split()[0]
            rest = " ".join(names.split()[1:])
            return s.rearrange(f"o {names} -> (o {first}) {rest}")

        def reset(all_sems):
            with nc.Block() as block:
                @block.sync
                def _(sp):
                    for x in all_sems:
                        sp.sem_clear(x)

        def load_ahead(sp, w_mod, name):
            for s in range(AHEAD):
                if name == "ahead":
                    sp.wait_ge(*after("w_lo", max(u for u in range(SLOTS) if u % RING == s)))
                sp.dma_start(ring[:, s, :].rearrange("p (k n) -> p k n", k=KC),
                             w_mod.rearrange("o (k p) n -> p (o k) n", p=P)[:, :, 256 * s:256 * s + 256]).then_inc(*loaded(name, s))

        with nc.Block() as block:
            @block.sync
            def _(sp):
                sp.dma_start(tab[:, :], a["tables"]).then_inc(*loaded("tables"))
                sp.dma_start(xin[:, 0, :], a["x_prompt"][0]).then_inc(*loaded("x_loaded"))
                sp.dma_start(xin[:, 1:3, :], a["x_sample"][0].rearrange("(t p) n -> p t n", p=P)).then_inc(*loaded("x_loaded", 1))
                load_ahead(sp, a["w_mod"][0:1], "first_ahead")
                sp.wait_ge(*after("first_ahead", AHEAD - 1))

            @block.scalar
            def _(act):
                act.wait_ge(*after("vrow_zero"))
                for i, n in enumerate(("c_ctx", "c", "final_norm_g")):
                    src = a[n][0] if n == "c" else a[n]
                    act.dma_start(vrow[8 * i:8 * i + 8, :], src.rearrange("(k p) -> k p", p=P)).then_inc(*loaded("cond_loaded", i))
                act.wait_ge(*after("cond_cols"))
                act.wait_ge(*after("pads", 0))
                nc.scalar.activation(scond[:, :, 0:2].rearrange("p k c -> p c k"),
                                     vec[:, 0:16].rearrange("p (c k) -> p c k", c=2), ACT.Tanh,
                                     scale=0.5).then_inc(*made("cond_tanh"))

            @block.gpsimd
            def _(pool):
                nc.gpsimd.memset(vrow[:, :], 0.0).then_inc(*made("vrow_zero"))
                nc.gpsimd.memset(scond[:, :, :], 0.0).then_inc(*made("pads", 0))
                nc.gpsimd.memset(eps[:, 0:1], RMS_EPS).then_inc(*made("pads", 1))
                nc.gpsimd.memset(eps[:, 1:2], GN_EPS).then_inc(*made("pads", 2))
                nc.gpsimd.memset(eps[:, 2:3], SUBLN_EPS).then_inc(*made("pads", 3))
                nc.gpsimd.memset(eps[:, 3:4], 0.0).then_inc(*made("pads", 4))

            @block.tensor
            def _(pe):
                pe.wait_ge(*after("tables"))
                pe.wait_ge(*after("x_loaded", 1))
                for k in range(KC):
                    if k >= 4:
                        pe.wait_ge(*after("xT", k - 4))
                    for t in range(TILES):
                        mm = nc.tensor.transpose(PS[:, k % 4, t * P:(t + 1) * P], xin[:, t, k * P:(k + 1) * P], ident)
                    mm.then_inc(*made("xT_mm", k))
                pe.wait_ge(*after("cond_loaded", 2))
                nc.tensor.transpose(PS[:, 4, 0:P], vrow[:, :], ident).then_inc(*made("cond_mm"))

            @block.vector
            def _(dve):
                for k in range(KC):
                    dve.wait_ge(*after("xT_mm", k))
                    nc.vector.tensor_copy(xT[:, k, :], PS[:, k % 4, 0:TOK]).then_inc(*made("xT", k))
                dve.wait_ge(*after("cond_mm"))
                nc.vector.tensor_copy(vec[:, :], PS[:, 4, 0:P]).then_inc(*made("cond_cols"))
                dve.wait_ge(*after("cond_cols"))
                nc.vector.tensor_copy(fing[:, :], vec[:, 16:24]).then_inc(*made("final_g"))
                dve.wait_ge(*after("cond_tanh"))
                for i in range(2):
                    nc.vector.tensor_scalar(lprod[:, i, 0:8], scond[:, :, i], 1.0, 0.5, ALU.add, ALU.mult).then_inc(*made("cond_half", i))
                dve.wait_ge(*after("cond_half", 1))
                for i in range(2):
                    nc.vector.tensor_tensor(scond[:, :, i], lprod[:, i, 0:8], vec[:, 8 * i:8 * i + 8], ALU.mult).then_inc(*made("cond", i))

        reset(list(sems.values()))
        prologue_names = set(sems)

        def norm_squares(act, n, x=None):
            for k in range(KC):
                if x:
                    act.wait_ge(*after(x, (k, 1)))
                nc.scalar.activation(xsq[:, k, :], xT[:, k, :], ACT.Square).then_inc(*made(f"{n}_sq", k))

        def norm_root(act, n):
            act.wait_ge(*after(f"{n}_ss"))
            nc.scalar.activation(rstd[:, :], PS[:, 6, 0:TOK], ACT.Sqrt, bias=eps[:, 0:1], scale=1.0 / D).then_inc(*made(f"{n}_sqrt"))

        def norm_pe(pe, n):
            for k in range(KC):
                pe.wait_ge(*after(f"{n}_sq", k))
                mm = nc.tensor.matmul(PS[:, 6, 0:TOK], ones, xsq[:, k, :], start=(k == 0), stop=(k == KC - 1))
            mm.then_inc(*made(f"{n}_ss"))

        with nc.Fori(0, DEPTH) as l:
            with nc.Block() as block:
                def layer2(x, l, p=P):
                    return x[bass.ds(l, 1)].rearrange("o (k p) -> (o k) p", p=p)

                def flat(x):
                    return x.rearrange("p u t -> p (u t)")

                def tok_job(n):
                    if n < 3:
                        return NTOK - P, P, n
                    s, t = divmod(n - 3, 3)
                    return 256 * s, 256, t

                def xbank(j, g):
                    return 2 if (3 * j + g) % 2 else 4

                def vbank(j, g):
                    return (3 * j + g) % 2

                def copy_pdT(act, i):
                    nk = 128 if i < HEADS else 384
                    act.wait_ge(*after("p_tr", i))
                    if i >= 2:
                        act.wait_ge(*after("pv", i - 2))
                    nc.scalar.activation(pdT[:, i % 2, 0:nk], PS[:, 4 + i % 2, 0:nk], ACT.Copy).then_inc(*made("pdT", i))

                prob_flat = prob.rearrange("p b m t -> p (b m t)")

                def abank(n, h):
                    return ((0, 1), (5, 6))[n % 2][h]

                def diff(dve, i):
                    V = nc.vector
                    t, h = divmod(i, HEADS)
                    nk = 128 if t == 0 else 384
                    dve.wait_ge(*after("exp", (i, 1)))
                    V.reciprocal(rinv[:, i % 2, :], rsum[:, i % 2, :]).then_inc(*made("rinv", i))
                    dve.wait_ge(*after("rinv", i))
                    V.tensor_scalar(rinv[:, i % 2, 1:2], rinv[:, i % 2, 1:2], lam[:, 0:1], None, ALU.mult).then_inc(*made("rlam", i))
                    dve.wait_ge(*after("rlam", i))
                    V.tensor_scalar(prob[:, i % 2, 1, 0:nk], prob[:, i % 2, 1, 0:nk], rinv[:, i % 2, 1:2], None, ALU.mult).then_inc(*made("p1", i))
                    dve.wait_ge(*after("p1", i))
                    if i >= 2:
                        dve.wait_ge(*after("p_tr", i - 2))
                    V.scalar_tensor_tensor(pdiff[:, i % 2, 0:nk], prob[:, i % 2, 0, 0:nk], rinv[:, i % 2, 0:1],
                                           prob[:, i % 2, 1, 0:nk], ALU.mult, ALU.subtract).then_inc(*made("pdiff", i))
                    if h == 2 and t >= 1:
                        copy_o(dve, t - 1)
                    if i == 17:
                        copy_o(dve, 2)

                def copy_o(dve, t):
                    dve.wait_ge(*after("pv", HEADS * t + HEADS - 1))
                    nc.vector.tensor_copy(osb[:, t, :], PS[:, 6 + t % 2, 0:DR]).then_inc(*made("o", t))

                def ff_bank(f):
                    return 4 * (f // HALF) + 2 * (f % 2)

                def fo_bank(half, oh):
                    return 4 * (1 - half if oh == 0 else half)

                def fo_last(half, oh):
                    return S_FFN + half * FFN_SLOTS + HALF + (HALF * (oh + 1) - 1) // 4

                def gn_places(c):
                    return ((6, 6, E3[:, :], tanh2[:, 1, :]), (7, 7, KAP[1][:, 0, :], tanh2[:, 0, :]),
                            (0, 4, KAP[0][:, 0, :], BT[:, 0, :]))[c]

                def rows_of(c, d):
                    return 2 if (c, d) == (0, 1) else d

                def mod_row(pair):
                    if pair >= MOD_PAIRS_A:
                        return mod_rows[:, pair % 2, :]
                    return (KT if pair % 2 else tanh2)[:, :, :].rearrange("p a t -> p (a t)")[:, 0:512]

                def mod_banks(pair):
                    return ((0, 1)[pair % 2], (2, 3)[pair % 2]) if pair < MOD_PAIRS_A else ((0, 2)[pair % 2], 1)

                def copy_mod_row(act, pair):
                    act.wait_ge(*after("mod_mm", MOD_AT[2 * pair + 1]))
                    if pair >= 2:
                        act.wait_ge(*after("mod_tr", pair - 2))
                    nc.scalar.activation(mod_row(pair), PS[:, mod_banks(pair)[0], :], ACT.Copy).then_inc(*made("mod_row", pair))

                def sum_mod(dve, pair):
                    dve.wait_ge(*after("mod_tr", pair))
                    nc.vector.tensor_reduce(mods[:, 4 * pair:4 * pair + 4, :],
                                            PS[:, mod_banks(pair)[1], :].rearrange("p (b j r) -> p b r j", b=4, j=4)[:, :, 0:2, :],
                                            AX.X, ALU.add).then_inc(*made("mod_sum", pair))

                def slot_mm(s):
                    if s in MOD_AT:
                        return "mod_mm", s
                    if s < S_GD:
                        return "in_mm", 2 * R_AT.index(s) + 1
                    if s < S_OUT:
                        return "in_mm", 13 + 3 * (s - S_GD)
                    if s < S_FFN:
                        return "out_mm", 2 * (s - S_OUT) + 1
                    half, i = divmod(s - S_FFN, FFN_SLOTS)
                    return ("ff_mm", half * HALF + i) if i < HALF else ("ffo_mm", s)

                def width(s):
                    last_fo = s >= S_FFN and (s - S_FFN) % FFN_SLOTS == FFN_SLOTS - 1
                    return (192, 256) if s == S_GD else (2048 - 512 * (4 * FO_SLOTS - 2 * HALF) if last_fo else 2048, 2048)

                def used(x, s):
                    n, row = width(s)
                    return x.rearrange("p (k n) -> p k n", n=row)[:, :, 0:n]

                def weights_hi(act, s):
                    n = SPLIT.index(s)
                    act.wait_ge(*after(f"slot{s % RING}", s))
                    if n >= 2:
                        act.wait_ge(*after(*slot_mm(SPLIT[n - 2])))
                    if s == S_OUT:
                        act.wait_ge(*after("Y_mm", HC - 1))
                    nc.scalar.activation(used(w_hi[:, n % 2, :], s), used(ring[:, s % RING, :], s), ACT.Copy).then_inc(*made("w_hi", s))

                def weights_lo(dve, s):
                    n = SPLIT.index(s)
                    dve.wait_ge(*after("w_hi", s))
                    nc.vector.tensor_tensor(used(w_lo[:, n % 2, :], s), used(ring[:, s % RING, :], s),
                                            used(w_hi[:, n % 2, :], s).bitcast(F32), ALU.subtract).then_inc(*made("w_lo", s))

                def y_round(act, k):
                    nc.scalar.activation(y_hi[:, k, :], yT[:, k, :], ACT.Copy).then_inc(*made("y_hi", k))

                def y_low(dve, k):
                    dve.wait_ge(*after("y_hi", k))
                    nc.vector.tensor_tensor(y_lo[:, k, :], yT[:, k, :], y_hi[:, k, :].bitcast(F32), ALU.subtract).then_inc(*made("y_lo", k))

                def last_use(s):
                    return ("w_lo", s) if s in SPLIT else slot_mm(s)

                def slot_loads(s):
                    dst = ring[:, s % RING, :]
                    d8 = dst.rearrange("p (k n) -> p k n", k=KC)
                    if s in MOD_AT:
                        w = layer(a["w_mod"], l).rearrange("(k p) n -> p k n", p=P)
                        at = 256 * MOD_AT.index(s)
                        return [(d8, w[:, :, at:at + 256])]
                    if s < S_OUT:
                        w = layer(a["w_in"], l).rearrange("(k p) n -> p k n", p=P)
                        if s < S_GD:
                            at = 256 * R_AT.index(s)
                            return [(d8, w[:, :, at:at + 256])]
                        if s == S_GD:
                            return [(d8[:, :, 0:64], w[:, :, 1280:NR]), (d8[:, :, 64:192], w[:, :, DIN - P:DIN])]
                        at = NR + 256 * (s - S_T)
                        return [(d8, w[:, :, at:at + 256])]
                    if s < S_FFN:
                        w = layer(a["w_out"], l).rearrange("(k p) n -> p k n", p=P)
                        at = 256 * (s - S_OUT)
                        return [(d8, w[:, :, at:at + 256])]
                    half, i = divmod(s - S_FFN, FFN_SLOTS)
                    if i < HALF:
                        w = layer(a["w_ffn_in"], l).rearrange("(k p) n -> p k n", p=P)
                        f = half * HALF + i
                        return [(d8[:, :, 0:P], w[:, :, f * P:f * P + P]),
                                (d8[:, :, P:2 * P], w[:, :, DFF + f * P:DFF + f * P + P])]
                    w = layer(a["w_ffn_out"], l).rearrange("(k p) n -> p k n", p=P)
                    d4 = dst.rearrange("p (k n) -> p k n", k=4)
                    units = [divmod(u, HALF) for u in range(4 * (i - HALF), min(4 * (i - HALF) + 4, 2 * HALF))]
                    out = []
                    j = 0
                    while j < len(units):
                        oh, k0 = units[j]
                        m = 1
                        while j + m < len(units) and units[j + m][0] == oh:
                            m += 1
                        k1 = half * HALF + k0
                        out.append((d4[:, j:j + m, :], w[:, k1:k1 + m, oh * 512:oh * 512 + 512]))
                        j += m
                    return out

                def vec_loads(sp):
                    def vload(name, rows, src):
                        at = VEC[name]
                        sp.dma_start(vrow[at:at + rows, 0:src.shape[-1]], src).then_inc(*loaded("vec_loaded", name))

                    vload("norm1_g", 8, layer2(a["norm1_g"], l))
                    vload("norm2_g", 8, layer2(a["norm2_g"], l))
                    vload("b_mod", 48, layer2(a["b_mod"], l))
                    for n in ("decay_w0", "iclr_a0"):
                        vload(n, 6, layer(a[n], l).rearrange("d (k p) -> (d k) p", p=P))
                    for n in ("k_k", "k_a", "lnx_g", "lnx_b"):
                        vload(n, 3, layer2(a[n], l))
                    vload("r_k", 3, layer(a["r_k"], l).rearrange("(k h) n -> k (h n)", h=2))
                    sg = layer2(a["subln_g"], l, 64)
                    r0 = VEC["subln_g"]
                    for h in range(2):
                        sp.dma_start(vrow[r0:r0 + 1, 64 * h:64 * h + 64], sg).then_inc(*loaded("vec_loaded", ("subln", h)))
                    for i in range(2):
                        mu = layer(a["shift_mu"], l)[i:i + 1, :]
                        r0 = VEC[f"mu{i}"]
                        sp.dma_start(vrow[r0:r0 + 10, :], mu[:, 0:1280].rearrange("o (k p) -> (o k) p", p=P)).then_inc(*loaded("vec_loaded", ("mu", i)))
                        sp.dma_start(vrow[r0 + 10:r0 + 11, 0:64], mu[:, 1280:NR]).then_inc(*loaded("vec_loaded", ("mue", i)))

                @block.sync
                def _(sp):
                    for s in range(AHEAD, SLOTS):
                        if s == AHEAD + RING:
                            vec_loads(sp)
                        if s >= RING:
                            sp.wait_ge(*after(*last_use(s - RING)))
                        for dst, src in slot_loads(s):
                            sp.dma_start(dst, src).then_inc(*loaded(f"slot{s % RING}", s))
                    assert DEPTH == 2
                    load_ahead(sp, a["w_mod"][bass.ds(1 - l, 1)], "ahead")
                    sp.wait_ge(*after("ahead", AHEAD - 1))
                    sp.wait_ge(*after("state_stored", 1))

                @block.gpsimd
                def _(pool):
                    for i, at in enumerate((0, SEQ + 1, TOK + 2)):
                        nc.gpsimd.memset(upad[:, :, at:at + 1], 0.0).then_inc(*made("pad_cols", i))
                    for t in range(2):
                        src = tok[:, t + 1, 0:768]
                        pool.wait_ge(*after("tok_dve", 11))
                        pool.wait_ge(*after("tok_act", 10))
                        for h in range(2):
                            o = swapped[:, t, :].rearrange("p (g x h n) -> p g x h n", g=24, x=2, h=2)[:, :, :, h, :]
                            i = src.rearrange("p (g x h n) -> p g x h n", g=24, x=2, h=2)[:, :, :, 1 - h, :]
                            nc.gpsimd.tensor_tensor(o, i, sin[:, t, :, h, :].unsqueeze(1).to_broadcast([P, 24, 2, 8]),
                                                    ALU.mult).then_inc(*made("rope_sin", (t, h)))
                        pool.wait_ge(*after("rope_sin", (t, 1)))
                        nc.gpsimd.tensor_tensor(src.rearrange("p (h n) -> p h n", n=32),
                                                src.rearrange("p (h n) -> p h n", n=32),
                                                cos[:, t, :].unsqueeze(1).to_broadcast([P, 24, 32]),
                                                ALU.mult).then_inc(*made("rope_cos", t))
                        pool.wait_ge(*after("rope_cos", t))
                        nc.gpsimd.tensor_tensor(src, src, swapped[:, t, :], ALU.add).then_inc(*made("rope", t))
                    def keys(c):
                        for d in range(2):
                            aa = AA[rows_of(c, d)][:, :]
                            pool.wait_ge(*after("a_tanh", (c, d)))
                            if (c, d) == (0, 0):
                                pool.wait_ge(*after("kk", HC - 1))
                            if c >= 1:
                                pool.wait_ge(*after("A_mm", (c - 1, 2, 1)))
                                pool.wait_ge(*after("kt_tr", c - 1))
                                pool.wait_ge(*after("bonus_k", c - 1))
                            nc.gpsimd.tensor_scalar(aa, aa, 0.5, 0.5, ALU.mult, ALU.add).then_inc(*made("a", (c, d)))
                            pool.wait_ge(*after("a", (c, d)))
                            nc.gpsimd.tensor_tensor(BT[:, d, :], aa, kk[:, c, :], ALU.mult).then_inc(*made("b", (c, d)))
                            nc.gpsimd.tensor_scalar(KD[:, d, :], aa, vec[:, VEC["k_a"] + c:VEC["k_a"] + c + 1],
                                                    omka[:, c:c + 1], ALU.mult, ALU.add).then_inc(*made("ka", (c, d)))
                            pool.wait_ge(*after("ka", (c, d)))
                            nc.gpsimd.tensor_tensor(KD[:, d, :], KD[:, d, :], uT[:, 3 + c, :], ALU.mult).then_inc(*made("kd", (c, d)))

                    keys(0)
                    for c in range(HC):
                        for g in range(3):
                            pool.wait_ge(*after("A", (c, g, 0)))
                            nc.gpsimd.tensor_tensor(AKB[:, g, :, :], AKB[:, g, :, :],
                                                    ident.unsqueeze(1).to_broadcast([P, 4, P]), ALU.add).then_inc(*made("A1", (c, g)))
                            pool.wait_ge(*after("A1", (c, g)))
                            for d in range(2):
                                nc.gpsimd.tensor_tensor(XT[:, g, 2 * d:2 * d + 2, :], AKB[:, g, 2 * d:2 * d + 2, :],
                                                        lmask[:, 0, 1 - d, :].unsqueeze(1).to_broadcast([P, 2, P]),
                                                        ALU.mult).then_inc(*made("XT0", (c, g, d)))
                        if c + 1 < HC:
                            keys(c + 1)

                @block.scalar
                def _(act):
                    dl = layer(a["diff_lambda"], l).rearrange("a b -> (a b)").unsqueeze(0).to_broadcast([P, P])
                    act.dma_start(lrow[:, :], dl).then_inc(*loaded("lam_loaded"))
                    act.dma_start(lamc[:, :], layer(a["lam_init"], l)).then_inc(*loaded("lam_loaded", 1))
                    norm_squares(act, "n1")
                    copy_mod_row(act, 0)
                    weights_hi(act, R_AT[0])
                    copy_mod_row(act, 1)
                    weights_hi(act, R_AT[1])
                    for pair in range(2, MOD_PAIRS_A):
                        if pair == MOD_PAIRS_A - 1:
                            norm_root(act, "n1")
                        copy_mod_row(act, pair)
                    def add_shift(n, base):
                        for k in range(KC):
                            for gi, (t0, t1) in enumerate(GROUPS):
                                act.wait_ge(*after(f"{n}_scaled", (k, gi)))
                                nc.scalar.activation(h_hi[:, k, t0:t1], yT[:, k, t0:t1], ACT.Identity,
                                                     bias=mods[:, base + k, gi:gi + 1]).then_inc(*made(f"{n}_h", (k, gi)))

                    add_shift("n1", SH1)
                    act.wait_ge(*after("lam_dots", 1))
                    nc.scalar.activation(lsum[:, 2:4], lsum[:, 0:2], ACT.Exp).then_inc(*made("lam_exp"))

                    def rates(c, d):
                        act.wait_ge(*after("lora_mm", (c, d)))
                        i = rows_of(c, d)
                        nc.scalar.activation(LW[i][:, :], PS[:, 6, 0:TOK], ACT.Tanh, scale=0.5,
                                             bias=w0h[:, 3 * d + c:3 * d + c + 1]).then_inc(*made("w_tanh", (c, d)))
                        nc.scalar.activation(AA[i][:, :], PS[:, 7, 0:TOK], ACT.Tanh, scale=0.5,
                                             bias=a0h[:, 3 * d + c:3 * d + c + 1]).then_inc(*made("a_tanh", (c, d)))

                    def exponentials(c, d, part):
                        i = rows_of(c, d)
                        kap, r, e3 = (((EX, 1.0), (EI, 1.0), (EI, -1.0)), ((EI, -1.0), (EX, -1.0), (EX, 1.0)))[d]
                        if part == 0:
                            act.wait_ge(*after("EX", (c, d)))
                            nc.scalar.activation(KAP[c % 2][:, d, :], kap[0][i][:, :], ACT.Exp, scale=kap[1]).then_inc(*made("e_kap", (c, d)))
                            nc.scalar.activation(RT[c % 2][:, d, :], r[0][i][:, :], ACT.Exp, scale=r[1]).then_inc(*made("e_r", (c, d)))
                        else:
                            nc.scalar.activation(KT[:, d, :], e3[0][i][:, :], ACT.Exp, scale=e3[1]).then_inc(*made("e_3", (c, d)))
                            nc.scalar.activation(et[:, c % 2, d, :], nh[:, d, :], ACT.Exp, scale=-1.0).then_inc(*made("e_tot", (c, d)))

                    act.dma_start(lora[0:64, :], layer(a["decay_up"], l).rearrange("d r n -> (d r) n")).then_inc(*loaded("lora_loaded"))
                    act.dma_start(lora[64:128, :], layer(a["iclr_up"], l).rearrange("d r n -> (d r) n")).then_inc(*loaded("lora_loaded", 1))
                    act.dma_start(gup[:, :], layer(a["gate_up"], l)).then_inc(*loaded("lora_loaded", 2))
                    act.dma_start(ctxk, layer(a["cache_k"], l)).then_inc(*loaded("ctx_loaded"))
                    act.dma_start(ctxv, layer(a["cache_v"], l)).then_inc(*loaded("ctx_loaded", 1))
                    for d in range(2):
                        act.dma_start(sin_rows[:, d, :].rearrange("v (h k) -> v h k", h=HEADS),
                                      layer(a["state"], l)[d].rearrange("h v k -> v h k")).then_inc(*loaded("state_loaded", d))

                    for j in range(11):
                        m = HD if j == 10 else P
                        if j % 2 == 0 and j:
                            weights_hi(act, SPLIT[j // 2 + 1])
                        act.wait_ge(*after("in_mm", j))
                        if j >= 2:
                            act.wait_ge(*after("shifted", j - 2))
                        u = PS[0:m, j % 4, 0:TOK]
                        nc.scalar.activation(upad[0:m, j % 2, 1:1 + SEQ], u[:, 0:SEQ], ACT.Copy).then_inc(*made("u_copy", (j, 0)))
                        nc.scalar.activation(upad[0:m, j % 2, 2 + SEQ:2 + TOK], u[:, SEQ:TOK], ACT.Copy).then_inc(*made("u_copy", (j, 1)))
                        nc.scalar.activation(uT[0:m, j, :], u, ACT.Copy, scale=muc[0:m, j:j + 1]).then_inc(*made("u_own", j))
                    for n in range(18):
                        if n % 3 == 0 and 3 <= n < 15:
                            weights_hi(act, S_T + n // 3)
                        if n % 2 == 0:
                            at, w, t = tok_job(n)
                            act.wait_ge(*after("in_mm", 11 + n))
                            nc.scalar.activation(tok[:, t, at:at + w], PS[:, (11 + n) % 4, 0:w], ACT.Copy).then_inc(*made("tok_act", n if n < 14 else 14))
                        if n == 2:
                            act.wait_ge(*after("shifted", 10))
                            nc.scalar.activation(tanh2[0:64, 0, :], uT[0:64, 9, :], ACT.Tanh).then_inc(*made("wd_tanh"))
                            nc.scalar.activation(tanh2[0:64, 1, :], uT[0:64, 10, :], ACT.Tanh, scale=0.5).then_inc(*made("gd_tanh"))
                        if n == 6:
                            for c in range(HC):
                                act.wait_ge(*after("kk_ss", c))
                                nc.scalar.activation(KD[:, 0, :] if c == 0 else KD[:, 1, :] if c == 1 else E3[:, :],
                                                     PS[:, 4 + c, 0:TOK], ACT.Sqrt, bias=eps[:, 3:4]).then_inc(*made("kk_sqrt", c))
                    rates(0, 0)
                    for c in range(HC):
                        act.wait_ge(*after("q_tr", c))
                        nc.scalar.activation(qT[:, c, :], PS[:, (2 * c) % 8, 0:TOK], ACT.Copy).then_inc(*made("qT", c))
                    rates(0, 1)
                    act.wait_ge(*after("tok_dve", 14))
                    act.wait_ge(*after("tok_act", 14))
                    act.dma_start(layer(a["out_k"], l), tok[:, 0, 384:768]).then_inc(*loaded("cache_stored"))
                    act.dma_start(layer(a["out_v"], l), tok[:, 0, 768:1152]).then_inc(*loaded("cache_stored", 1))
                    for i in range(18):
                        t, h = divmod(i, HEADS)
                        nk = 128 if t == 0 else 384
                        act.wait_ge(*after("neg_max", i))
                        if i >= 2:
                            act.wait_ge(*after("pdiff", i - 2))
                        for m in range(2):
                            nc.scalar.activation(prob[:, i % 2, m, 0:nk], PS[:, 2 * (i % 2) + m, 0:nk], ACT.Exp,
                                                 bias=nmax[:, i % 2, m:m + 1], scale=QSCALE,
                                                 accum_out=rsum[:, i % 2, m:m + 1]).then_inc(*made("exp", (i, m)))
                        if i >= 2:
                            copy_pdT(act, i - 2)
                        if 6 <= i < 10:
                            exponentials(0, (i - 6) // 2, i % 2)
                    copy_pdT(act, 16)
                    copy_pdT(act, 17)
                    for c in range(HC):
                        act.wait_ge(*after("gate_mm", c))
                        nc.scalar.activation(gate[:, c, :], PS[:, c, 0:TOK], ACT.Copy).then_inc(*made("gate", c))
                    act.wait_ge(*after("o_ms"))
                    nc.scalar.activation(onorm[:, :], onorm[:, :], ACT.Sqrt, bias=eps[:, 2:3], scale=1.0 / HD).then_inc(*made("o_sqrt"))
                    for dc in range(2):
                        act.wait_ge(*after("fz_mm", dc))
                        nc.scalar.activation(fz[:, dc, 0:256], PS[:, 4 + 2 * dc, 0:256], ACT.Copy).then_inc(*made("fz", (dc, 0)))
                        nc.scalar.activation(fz[:, dc, 256:768], PS[:, 5 + 2 * dc, :], ACT.Copy).then_inc(*made("fz", (dc, 1)))
                    for dc in range(2):
                        act.wait_ge(*after("fnet_mm", dc))
                        nc.scalar.activation(yT[:, 6 + dc, :], PS[:, (3, 0)[dc], 0:TOK], ACT.Copy).then_inc(*made("y_fnet", dc))
                    for t in range(TILES):
                        act.wait_ge(*after("o_tr", t))
                        nc.scalar.activation(yT[:, 3:6, t * P:(t + 1) * P],
                                             PS[:, (1, 2, 4)[t], 0:DR].rearrange("p (c n) -> p c n", c=3), ACT.Copy,
                                             scale=subs).then_inc(*made("y_attn", t))
                    def gn_root(c):
                        _, bank, _, root = gn_places(c)
                        act.wait_ge(*after("gn_var_mm", c))
                        nc.scalar.activation(root, PS[:, bank, 0:TOK], ACT.Sqrt, bias=eps[:, 1:2],
                                             scale=1.0 / HD).then_inc(*made("gn_sqrt", c))

                    for c in range(HC):
                        act.wait_ge(*after("kt_tr", c))
                        if c >= 1:
                            act.wait_ge(*after("S_mm", (c - 1, 1)))
                        nc.scalar.activation(ktok[:, :, :, :].rearrange("p d t n -> p (d t n)"), PS[:, 2, :], ACT.Copy).then_inc(*made("ktok", c))
                        nc.scalar.activation(btok[:, :, :, :].rearrange("p d t n -> p (d t n)"), PS[:, 3, :], ACT.Copy).then_inc(*made("btok", c))
                        for j in range(1, LEVELS):
                            for g in range(3):
                                if j < LEVELS - 1:
                                    act.wait_ge(*after("X_mm", (c, j, g)))
                                    nc.scalar.activation(flat(X[:, g]), PS[:, xbank(j, g), :], ACT.Copy).then_inc(*made("X", (c, j, g)))
                                act.wait_ge(*after("XT_mm", (c, j, g)))
                                nc.scalar.activation(flat(XT[:, g]), PS[:, xbank(j, g) + 1, :], ACT.Copy).then_inc(*made("XT", (c, j, g)))
                                q = 3 * j + g
                                if c == HC - 1 and q in (9, 11):
                                    gn_root((q - 9) // 2)
                                if c + 1 < HC:
                                    if q == 3:
                                        act.wait_ge(*after("cache_stored", 1))
                                    if q in (3, 6):
                                        rates(c + 1, (q - 3) // 3)
                                    if q in (10, 12, 14, 16):
                                        exponentials(c + 1, (q - 10) // 4, (q - 10) // 2 % 2)
                            if c == HC - 1 and HC <= j + 2 < KC:
                                if j + 2 == HC:
                                    act.wait_ge(*after("cache_stored", 1))
                                y_round(act, j + 2)
                        for g in range(3):
                            act.wait_ge(*after("U_mm", (c, g)))
                            if c >= 1 and g == 0:
                                act.wait_ge(*after("Y_mm", c - 1))
                            nc.scalar.activation(usb[:, g, :], PS[:, 7, 0:256], ACT.Copy, scale=-1.0).then_inc(*made("U", (c, g)))
                            if g < len(MOD_PAIRS_SOLVE[c]):
                                copy_mod_row(act, MOD_PAIRS_SOLVE[c][g])
                        act.wait_ge(*after("Y_mm", c))
                        for h in range(2):
                            hs = slice(h * HD, (h + 1) * HD)
                            nc.scalar.activation(yT[hs, c, :], PS[hs, 5 + h, 0:TOK], ACT.Copy).then_inc(*made("y_raw", c if h else (c, 0)))
                    weights_hi(act, S_OUT)
                    weights_hi(act, S_OUT + 1)
                    for d in range(2):
                        act.wait_ge(*after("st_tr", d))
                        nc.scalar.activation(sout[:, d, :], PS[0:HD, 6 + d, 0:DR], ACT.Copy).then_inc(*made("state_rows", d))
                    act.wait_ge(*after("state_rows", 1))
                    for d in range(2):
                        act.dma_start(layer(a["out_s"], l)[d].rearrange("h v k -> v h k"),
                                      sout[:, d, :].rearrange("v (h k) -> v h k", h=HEADS)).then_inc(*loaded("state_stored", d))
                    y_round(act, 0)
                    y_round(act, 1)
                    gn_root(HC - 1)
                    act.wait_ge(*after("y_rwkv", HC - 1))
                    y_round(act, HC - 1)
                    for s in range(S_OUT + 2, S_FFN + 1):
                        weights_hi(act, s)
                    act.wait_ge(*after("out_mm", KC - 1))
                    norm_squares(act, "n2", "x1")
                    weights_hi(act, S_FFN + 1)
                    norm_root(act, "n2")
                    add_shift("n2", SH2)
                    for s in range(S_FFN, SLOTS):
                        if S_FFN < s < SLOTS - 1:
                            weights_hi(act, s + 1)
                        half, i = divmod(s - S_FFN, FFN_SLOTS)
                        if i < HALF:
                            f = half * HALF + i
                            act.wait_ge(*after("ff_mm", f))
                            if f >= 2:
                                act.wait_ge(*after("ff_lo", f - 2))
                            nc.scalar.activation(tanh2[:, f % 2, :], PS[:, ff_bank(f), 0:TOK], ACT.Tanh, scale=0.5).then_inc(*made("ff_tanh", f))
                            act.wait_ge(*after("ff", f))
                            nc.scalar.activation(ff_hi[:, i, :], tanh2[:, f % 2, :], ACT.Copy).then_inc(*made("ff_hi", f))

                @block.vector
                def _(dve):
                    V = nc.vector
                    def norm_scale(n):
                        dve.wait_ge(*after(f"{n}_sqrt"))
                        V.reciprocal(rstd[:, :], rstd[:, :]).then_inc(*made(f"{n}_rstd"))

                    sum_mod(dve, 0)
                    weights_lo(dve, R_AT[0])
                    sum_mod(dve, 1)
                    weights_lo(dve, R_AT[1])
                    sum_mod(dve, 2)
                    norm_scale("n1")
                    dve.wait_ge(*after("vec_tr"))
                    V.tensor_copy(vec[:, :], PS[:, 5, 0:P]).then_inc(*made("vec"))
                    dve.wait_ge(*after("vec"))
                    col = lambda n, k: vec[:, VEC[n]:VEC[n] + k]
                    dve.wait_ge(*after("lam_loaded", 1))
                    V.tensor_tensor(muc, col("mu0", 11), col("mu1", 11), ALU.add).then_inc(*made("dvec", 0))
                    V.tensor_scalar(w0h, col("decay_w0", 6), 0.5, None, ALU.mult).then_inc(*made("dvec", 1))
                    V.tensor_scalar(a0h, col("iclr_a0", 6), 0.5, None, ALU.mult).then_inc(*made("dvec", 2))
                    V.tensor_scalar(omka, col("k_a", 3), -1.0, 1.0, ALU.mult, ALU.add).then_inc(*made("dvec", 3))
                    V.tensor_tensor(subs, col("subln_g", 1), lamc[:, 1:2], ALU.mult).then_inc(*made("dvec", 4))
                    dve.wait_ge(*after("dvec", 0))
                    V.tensor_scalar(muc, muc, -1.0, 1.0, ALU.mult, ALU.add).then_inc(*made("dvec", 5))
                    lr = lrow[:, :].rearrange("p (a n) -> p a n", a=4)
                    V.tensor_tensor(lprod[:, :, :], lr[:, 0:4:2, :], lr[:, 1:4:2, :], ALU.mult).then_inc(*made("lam_dots", 0))
                    dve.wait_ge(*after("lam_dots", 0))
                    V.tensor_reduce(lsum[:, 0:2], lprod[:, :, :], AX.X, ALU.add).then_inc(*made("lam_dots", 1))

                    def norm_apply(n, g, base):
                        dve.wait_ge(*after(f"{n}_rstd"))
                        for step in range(KC + 1):
                            for gi, (t0, t1) in enumerate(GROUPS):
                                if step < KC:
                                    V.scalar_tensor_tensor(yT[:, step, t0:t1], xT[:, step, t0:t1], gmod[:, g, step, gi:gi + 1],
                                                           rstd[:, t0:t1], ALU.mult, ALU.mult).then_inc(*made(f"{n}_scaled", (step, gi)))
                            for gi, (t0, t1) in enumerate(GROUPS if step else ()):
                                k = step - 1
                                dve.wait_ge(*after(f"{n}_h", (k, gi)))
                                V.scalar_tensor_tensor(h_lo[:, k, t0:t1], yT[:, k, t0:t1], mods[:, base + k, gi:gi + 1],
                                                       h_hi[:, k, t0:t1].bitcast(F32), ALU.add,
                                                       ALU.subtract).then_inc(*made(f"{n}_low", (k, gi)))

                    def finish_mods(part, n0, n1, g, norm_g, sc):
                        dve.wait_ge(*after("mod_sum", n1 // 4 - 1))
                        V.tensor_tensor(mods[:, n0:n1, :], mods[:, n0:n1, :],
                                        vec[:, VEC["b_mod"] + n0:VEC["b_mod"] + n1].unsqueeze(2).to_broadcast([P, n1 - n0, 2]),
                                        ALU.add).then_inc(*made("mods", part))
                        dve.wait_ge(*after("mods", part))
                        V.tensor_scalar(gmod[:, g, :, :], mods[:, sc:sc + 8, :], 1.0, None, ALU.add).then_inc(*made("gmod", (g, 0)))
                        dve.wait_ge(*after("gmod", (g, 0)))
                        V.tensor_tensor(gmod[:, g, :, :], gmod[:, g, :, :], col(norm_g, 8).unsqueeze(2).to_broadcast([P, KC, 2]),
                                        ALU.mult).then_inc(*made("gmod", (g, 1)))
                        dve.wait_ge(*after("gmod", (g, 1)))

                    sum_mod(dve, MOD_PAIRS_A - 1)
                    finish_mods(0, 0, 16, 0, "norm1_g", SC1)
                    norm_apply("n1", 0, SH1)
                    dve.wait_ge(*after("lam_exp"))
                    V.tensor_tensor(lsum[:, 4:5], lsum[:, 2:3], lsum[:, 3:4], ALU.subtract).then_inc(*made("lam", 0))
                    dve.wait_ge(*after("lam", 0))
                    V.tensor_tensor(lam[:, :], lsum[:, 4:5], lamc[:, 0:1], ALU.add).then_inc(*made("lam", 1))

                    for j in range(11):
                        m = HD if j == 10 else P
                        if j % 2 == 0 and j:
                            weights_lo(dve, SPLIT[j // 2 + 1])
                        dve.wait_ge(*after("u_copy", (j, 1)))
                        dve.wait_ge(*after("u_own", j))
                        dve.wait_ge(*after("pad_cols", 2))
                        for side in range(2):
                            mu = vec[0:m, VEC[f"mu{side}"] + j:VEC[f"mu{side}"] + j + 1]
                            if side:
                                dve.wait_ge(*after("u_prev", (j, 1)))
                            for gi, (t0, t1) in enumerate(GROUPS):
                                at = t0 + gi + 2 * side
                                last = V.scalar_tensor_tensor(uT[0:m, j, t0:t1], upad[0:m, j % 2, at:at + t1 - t0], mu,
                                                              uT[0:m, j, t0:t1], ALU.mult, ALU.add)
                                last.then_inc(*(made("u_prev", (j, gi)) if side == 0 else made("shifted", j if gi else (j, 0))))
                    for n in range(18):
                        if n % 3 == 0 and 3 <= n < 15:
                            weights_lo(dve, S_T + n // 3)
                        if n % 2 == 1:
                            at, w, t = tok_job(n)
                            dve.wait_ge(*after("in_mm", 11 + n))
                            V.tensor_copy(tok[:, t, at:at + w], PS[:, (11 + n) % 4, 0:w]).then_inc(*made("tok_dve", n if n < 14 else 14))
                        if n == 2:
                            for c in range(HC):
                                V.tensor_scalar(kk[:, c, :], uT[:, 3 + c, :], vec[:, VEC["k_k"] + c:VEC["k_k"] + c + 1], None, ALU.mult).then_inc(*made("kk_raw", c))
                            dve.wait_ge(*after("kk_raw", 2))
                            for c in range(HC):
                                V.tensor_tensor((LW, EI, EX)[c][0][:, :], kk[:, c, :], kk[:, c, :], ALU.mult).then_inc(*made("kk_sq", c))
                        if n == 9:
                            for c in range(HC):
                                b = (KD[:, 0, :], KD[:, 1, :], E3[:, :])[c]
                                dve.wait_ge(*after("kk_sqrt", c))
                                V.tensor_scalar(b, b, 1e-12, None, ALU.max).then_inc(*made("kk_den", (c, 0)))
                                dve.wait_ge(*after("kk_den", (c, 0)))
                                V.reciprocal(b, b).then_inc(*made("kk_den", (c, 1)))
                                dve.wait_ge(*after("kk_den", (c, 1)))
                                V.tensor_tensor(kk[:, c, :], kk[:, c, :], b, ALU.mult).then_inc(*made("kk", c))
                    for c in range(HC):
                        dve.wait_ge(*after("v_tr", c))
                        V.tensor_copy(vtok[:, :, c * P:(c + 1) * P],
                                      PS[:, 4 + c, 0:TOK].rearrange("p (t n) -> p t n", t=3)).then_inc(*made("vtok", c))
                    dve.wait_ge(*after("s0_tr"))
                    V.tensor_copy(S0T[:, :, :, :].rearrange("p d c n -> p (d c n)"), PS[:, 7, 0:DR]).then_inc(*made("S0T"))
                    dve.wait_ge(*after("gd_tanh"))
                    V.tensor_scalar(tanh2[0:64, 1, :], tanh2[0:64, 1, :], 0.5, 0.5, ALU.mult, ALU.add).then_inc(*made("gd_sig"))
                    for c in range(HC):
                        dve.wait_ge(*after("k_tr", c))
                        V.tensor_copy(kT[:, c, :], PS[:, 2 * c + 1, :]).then_inc(*made("kT", c))
                    def prepare(c, part):
                        d = part // 2 % 2
                        lw, ei, ex = (x[rows_of(c, d)][:, :] for x in (LW, EI, EX))
                        if part in (0, 2):
                            dve.wait_ge(*after("w_tanh", (c, d)))
                            V.tensor_scalar(lw, lw, -0.5 * DECAY, -0.5 * DECAY, ALU.mult, ALU.add).then_inc(*made("LW", (c, d)))
                            dve.wait_ge(*after("LW", (c, d)))
                            V.tensor_tensor_scan(ei, smask, lw, 0.0, ALU.mult, ALU.add).then_inc(*made("sum", (c, d)))
                        if part in (1, 3):
                            dve.wait_ge(*after("sum", (c, d)))
                            V.tensor_scalar(nh[:, d, :], ei[:, P - 1:TOK:P], -0.5, None, ALU.mult).then_inc(*made("nh", (c, d)))
                            dve.wait_ge(*after("nh", (c, d)))
                            V.tensor_tensor(ei.rearrange("p (t n) -> p t n", t=3), ei.rearrange("p (t n) -> p t n", t=3),
                                            nh[:, d, :].unsqueeze(2).to_broadcast([P, 3, P]), ALU.add).then_inc(*made("EI", (c, d)))
                            dve.wait_ge(*after("EI", (c, d)))
                            V.tensor_tensor(ex, ei, lw, ALU.subtract).then_inc(*made("EX", (c, d)))
                        if part in (4, 6):
                            kap, r = KAP[c % 2][:, d, :], RT[c % 2][:, d, :]
                            dve.wait_ge(*after("e_kap", (c, d)))
                            V.tensor_tensor(kap, kap, kk[:, c, :], ALU.mult).then_inc(*made("kap", (c, d)))
                            dve.wait_ge(*after("e_r", (c, d)))
                            V.tensor_tensor(r, r, uT[:, c, :], ALU.mult).then_inc(*made("r", (c, d)))
                        if part in (5, 7):
                            dve.wait_ge(*after("e_3", (c, d)))
                            dve.wait_ge(*after("kd", (c, d)))
                            V.tensor_tensor(BT[:, d, :], BT[:, d, :], KT[:, d, :], ALU.mult).then_inc(*made("b_scaled", (c, d)))
                            dve.wait_ge(*after("b_scaled", (c, d)))
                            V.tensor_tensor(KT[:, d, :], KT[:, d, :], KD[:, d, :], ALU.mult).then_inc(*made("k_scaled", (c, d)))
                        if part == 8:
                            V.tensor_tensor(gsum[:, :], KD[:, 0, :], KD[:, 1, :], ALU.add).then_inc(*made("bonus_k", c))
                            dve.wait_ge(*after("bonus_k", c))
                            V.scalar_tensor_tensor(gsum[:, :], gsum[:, :], vec[:, VEC["r_k"] + c:VEC["r_k"] + c + 1], uT[:, c, :],
                                                   ALU.mult, ALU.mult).then_inc(*made("bonus_r", c))

                    for i in range(18):
                        t, h = divmod(i, HEADS)
                        nk = 128 if t == 0 else 384
                        dve.wait_ge(*after("scores", i))
                        if i >= 2:
                            dve.wait_ge(*after("exp", (i - 2, 1)))
                        V.tensor_reduce(amax[:, i % 2, :], PS[:, 2 * (i % 2):2 * (i % 2) + 2, 0:nk], AX.X, ALU.max).then_inc(*made("max", i))
                        dve.wait_ge(*after("max", i))
                        V.tensor_scalar(nmax[:, i % 2, :], amax[:, i % 2, :], -QSCALE, None, ALU.mult).then_inc(*made("neg_max", i))
                        if i >= 1:
                            diff(dve, i - 1)
                        if 1 <= i < 5:
                            prepare(0, i - 1)
                        if 10 <= i < 15:
                            prepare(0, i - 6)
                    diff(dve, 17)
                    for t in range(TILES):
                        if t == 0:
                            dve.wait_ge(*after("o", 2))
                            dve.wait_ge(*after("pdT", 17))
                        V.tensor_tensor(prob_flat[:, t * DR:(t + 1) * DR], osb[:, t, :], osb[:, t, :], ALU.mult).then_inc(*made("o_sq", t))
                    dve.wait_ge(*after("o_sq", 2))
                    V.tensor_reduce(onorm[:, :], prob_flat[:, 0:3 * DR].rearrange("p (h n) -> p h n", n=HD), AX.X, ALU.add).then_inc(*made("o_ms"))
                    dve.wait_ge(*after("o_sqrt"))
                    V.reciprocal(onorm[:, :], onorm[:, :]).then_inc(*made("o_rinv"))
                    dve.wait_ge(*after("o_rinv"))
                    for t in range(TILES):
                        V.tensor_tensor(osb[:, t, :].rearrange("p (h n) -> p h n", n=HD), osb[:, t, :].rearrange("p (h n) -> p h n", n=HD),
                                        onorm[:, 6 * t:6 * t + 6].unsqueeze(2).to_broadcast([P, 6, HD]), ALU.mult).then_inc(*made("o_n", t))
                    def gn_center(c):
                        bank, _, squares, _ = gn_places(c)
                        dve.wait_ge(*after("gn_mean_mm", c))
                        V.scalar_tensor_tensor(yT[:, c, :], PS[:, bank, 0:TOK], -1.0 / HD, yT[:, c, :], ALU.mult, ALU.add).then_inc(*made("gn_d", c))
                        dve.wait_ge(*after("gn_d", c))
                        V.tensor_tensor(squares, yT[:, c, :], yT[:, c, :], ALU.mult).then_inc(*made("gn_sq", c))

                    def gn_finish(c, part):
                        y, root = yT[:, c, :], gn_places(c)[3]
                        if part == 0:
                            dve.wait_ge(*after("gn_sqrt", c))
                            V.reciprocal(root, root).then_inc(*made("gn", (c, 0)))
                            dve.wait_ge(*after("gn", (c, 0)))
                            V.tensor_tensor(y, y, root, ALU.mult).then_inc(*made("gn", (c, 1)))
                            return
                        dve.wait_ge(*after("gn", (c, 1)))
                        V.tensor_scalar(y, y, vec[:, VEC["lnx_g"] + c:VEC["lnx_g"] + c + 1],
                                        vec[:, VEC["lnx_b"] + c:VEC["lnx_b"] + c + 1], ALU.mult, ALU.add).then_inc(*made("gn", (c, 2)))
                        dve.wait_ge(*after("gn", (c, 2)))
                        V.tensor_tensor(y, y, bonus[:, c, :], ALU.add).then_inc(*made("gn", (c, 3)))
                        dve.wait_ge(*after("gn", (c, 3)))
                        V.tensor_tensor(y, y, gate[:, c, :], ALU.mult).then_inc(*made("y_rwkv", c))

                    for c in range(HC):
                        dve.wait_ge(*after("bonus_mm", c))
                        V.tensor_tensor(bonus[:, c, :], PS[:, 4, 0:TOK], uT[:, 6 + c, :], ALU.mult).then_inc(*made("bonus", c))
                        dve.wait_ge(*after("e_tot", (c, 1)))
                        if c >= 1:
                            dve.wait_ge(*after("Y_mm", c - 1))
                        for d in range(2):
                            t = STEP_TILE[1][d]
                            V.tensor_scalar(SH[:, 1, d, :], S0T[:, d, c, :], et[:, c % 2, d, t:t + 1], None, ALU.mult).then_inc(*made("SH", (c, 1, d)))
                        for g in range(3):
                            for n in range(2):
                                dve.wait_ge(*after("A_mm", (c, g, n)))
                                if c >= 1 and g == 0 and n == 0:
                                    dve.wait_ge(*after("Y_mm", c - 1))
                                for i, dst in enumerate(((AKB, AKV), (ARB, ARV))[n]):
                                    for h in range(2):
                                        V.tensor_tensor(dst[:, g, h:4:2, :],
                                                        PS[:, abank(2 * g + n, h), 256 * i:256 * i + 256].rearrange("p (d t) -> p d t", d=2),
                                                        amask[:, 2 * n:2 * n + 2, :], ALU.mult).then_inc(*made("A", (c, g, n) if (i, h) == (1, 1) else (c, g, n, i, h)))
                        for j in range(LEVELS):
                            for g in range(3):
                                dve.wait_ge(*after("V_mm", (c, j, g)))
                                dst = X if j == 0 else VB
                                if j >= 2:
                                    dve.wait_ge(*after("XT_mm", (c, j - 1, g)))
                                for d in range(2):
                                    V.tensor_tensor(dst[:, g, 2 * d:2 * d + 2, :],
                                                    PS[:, vbank(j, g), 256 * d:256 * d + 256].rearrange("p (u t) -> p u t", u=2),
                                                    lmask[:, j, d, :].unsqueeze(1).to_broadcast([P, 2, P]),
                                                    ALU.mult).then_inc(*made("V", (c, j, g) if d else (c, j, g, 0)))
                                q = 3 * j + g
                                if c + 1 < HC and q >= 5 and q % 2:
                                    prepare(c + 1, (q - 5) // 2)
                                if c == HC - 1 and q in (4, 6):
                                    gn_center((q - 4) // 2)
                                if c == HC - 1 and q in (12, 13, 15, 16):
                                    gn_finish((q - 12) // 3, q % 3)
                            if c == HC - 1 and HC <= j + 1 < KC:
                                y_low(dve, j + 1)
                        if c + 1 < HC:
                            prepare(c + 1, 8)
                        for g in range(3):
                            dve.wait_ge(*after("Z_mm", (c, g)))
                            if g >= 1:
                                dve.wait_ge(*after("U_mm", (c, g - 1)))
                            for h in range(2):
                                V.tensor_copy(zs.rearrange("p (d h n) -> p d h n", d=2, h=2)[:, :, h, :],
                                              PS[:, (6, 4)[h], 0:P].rearrange("p (d n) -> p d n", d=2)).then_inc(*made("Z", (c, g) if h else (c, g, 0)))
                            if g < 2:
                                dve.wait_ge(*after("S_mm", (c, g)))
                                for d in range(2):
                                    t, tn = STEP_TILE[g][d], STEP_TILE[2][d]
                                    s = PS[:, 3, d * HD:(d + 1) * HD]
                                    if g == 0:
                                        V.tensor_scalar(Sfin[:, c, d, :], s, et[:, c % 2, d, t:t + 1], None, ALU.mult).then_inc(*made("Sfin", (c, d)))
                                    else:
                                        V.tensor_tensor(stmp[:, d, :], s, SH[:, 1, d, :], ALU.add).then_inc(*made("stmp", (c, d)))
                                if g == 1:
                                    dve.wait_ge(*after("stmp", (c, 1)))
                                    for d in range(2):
                                        t, tn = STEP_TILE[g][d], STEP_TILE[2][d]
                                        V.tensor_scalar(SH[:, 2, d, :], stmp[:, d, :], et[:, c % 2, d, t:t + 1], et[:, c % 2, d, tn:tn + 1],
                                                        ALU.mult, ALU.mult).then_inc(*made("SH", (c, 2, d)))
                            if 1 <= g <= len(MOD_PAIRS_SOLVE[c]):
                                sum_mod(dve, MOD_PAIRS_SOLVE[c][g - 1])
                        if len(MOD_PAIRS_SOLVE[c]) == 3:
                            sum_mod(dve, MOD_PAIRS_SOLVE[c][2])
                    finish_mods(1, 16, 48, 1, "norm2_g", SC2)
                    gn_center(HC - 1)
                    weights_lo(dve, S_OUT)
                    weights_lo(dve, S_OUT + 1)
                    y_low(dve, 0)
                    y_low(dve, 1)
                    gn_finish(HC - 1, 0)
                    gn_finish(HC - 1, 1)
                    y_low(dve, HC - 1)

                    for m in range(KC):
                        if m in (2, 4, 6):
                            weights_lo(dve, S_OUT + m // 2 + 1)
                        dve.wait_ge(*after("out_mm", m))
                        for gi, (t0, t1) in enumerate(GROUPS):
                            V.scalar_tensor_tensor(xT[:, m, t0:t1], PS[:, m % 4, t0:t1], mods[:, G1 + m, gi:gi + 1], xT[:, m, t0:t1],
                                                   ALU.mult, ALU.add).then_inc(*made("x1", (m, gi)))
                    weights_lo(dve, S_FFN + 1)
                    norm_scale("n2")
                    norm_apply("n2", 1, SH2)
                    for s in range(S_FFN, SLOTS):
                        if S_FFN < s < SLOTS - 1:
                            weights_lo(dve, s + 1)
                        half, i = divmod(s - S_FFN, FFN_SLOTS)
                        if i < HALF:
                            f = half * HALF + i
                            row = tanh2[:, f % 2, :]
                            dve.wait_ge(*after("ff_tanh", f))
                            V.scalar_tensor_tensor(row, row, 1.0, PS[:, ff_bank(f), 0:TOK], ALU.add, ALU.mult).then_inc(*made("ff_silu", f))
                            dve.wait_ge(*after("ff_silu", f))
                            V.scalar_tensor_tensor(row, row, 0.5, PS[:, ff_bank(f) + 1, 0:TOK], ALU.mult, ALU.mult).then_inc(*made("ff", f))
                            dve.wait_ge(*after("ff_hi", f))
                            V.tensor_tensor(ff_lo[:, i, :], row, ff_hi[:, i, :].bitcast(F32), ALU.subtract).then_inc(*made("ff_lo", f))
                        for oh in range(2):
                            if s == fo_last(half, oh):
                                dve.wait_ge(*(after("ffo_mm", s) if oh else after("ffo_half", half)))
                                for m in range(4):
                                    for gi, (t0, t1) in enumerate(GROUPS):
                                        V.scalar_tensor_tensor(xT[:, 4 * oh + m, t0:t1], PS[:, fo_bank(half, oh) + m, t0:t1],
                                                               mods[:, G2 + 4 * oh + m, gi:gi + 1], xT[:, 4 * oh + m, t0:t1],
                                                               ALU.mult, ALU.add).then_inc(*made("x2", (half, oh, m, gi)))

                @block.tensor
                def _(pe):
                    T = nc.tensor

                    def need(s):
                        if s >= AHEAD:
                            pe.wait_ge(*after(f"slot{s % RING}", s))
                        return ring[:, s % RING, :].rearrange("p (k n) -> p k n", k=KC)

                    def need_split(s, k=KC):
                        pe.wait_ge(*after("w_lo", s))
                        n = SPLIT.index(s) % 2
                        return (w_hi[:, n, :].rearrange("p (k n) -> p k n", k=k), w_lo[:, n, :].rearrange("p (k n) -> p k n", k=k))

                    def passes(out, lhs, rhs, start, stop):
                        T.matmul(out, lhs[0], rhs[0], start=start, stop=False)
                        T.matmul(out, lhs[0], rhs[1], start=False, stop=False)
                        return T.matmul(out, lhs[1], rhs[0], start=False, stop=stop)

                    def mod_products(i):
                        pair = i // 2
                        w = need(MOD_AT[i])
                        bank = mod_banks(pair)[0]
                        if pair >= 2 and i % 2 == 0:
                            pe.wait_ge(*after("mod_row", pair - 2))
                        if pair >= MOD_PAIRS_A and i % 2 == 0:
                            for c in range(HC):
                                if pair in MOD_PAIRS_SOLVE[c]:
                                    pe.wait_ge(*after("V", (c, LEVELS - 1, 2)))
                        for k in range(KC):
                            q = 32 * (k % 4)
                            mm = T.matmul(PS[q:q + 32, bank, 256 * (i % 2):256 * (i % 2) + 256], scond[:, k, :], w[:, k, :],
                                          start=(k < 4), stop=(k >= 4), tile_position=(0, q))
                        mm.then_inc(*made("mod_mm", MOD_AT[i]))

                    def mod_transpose(pair):
                        pe.wait_ge(*after("mod_row", pair))
                        if pair >= 2:
                            pe.wait_ge(*after("mod_sum", pair - (2 if pair < MOD_PAIRS_A else 1)))
                        for b in range(4):
                            mm = T.transpose(PS[:, mod_banks(pair)[1], b * P:(b + 1) * P], mod_row(pair)[:, b * P:(b + 1) * P], ident)
                        mm.then_inc(*made("mod_tr", pair))

                    def first_block(s, n, k, b):
                        hi, lo = need_split(s + b // 2)
                        pe.wait_ge(*after(f"{n}_low", (k, 1)))
                        bs = slice(P * (b % 2), P * (b % 2) + P)
                        return passes(PS[:, b, 0:TOK], (hi[:, k, bs], lo[:, k, bs]), (h_hi[:, k, :], h_lo[:, k, :]),
                                      k == 0, k == KC - 1)

                    for pair in range(MOD_PAIRS_A + 1):
                        if pair == 2:
                            norm_pe(pe, "n1")
                        if pair == MOD_PAIRS_A:
                            pe.wait_ge(*after("vec_loaded", ("mue", 1)))
                            T.transpose(PS[:, 5, 0:P], vrow[:, :], ident).then_inc(*made("vec_tr"))
                        if pair < MOD_PAIRS_A:
                            mod_products(2 * pair)
                            mod_products(2 * pair + 1)
                        if pair:
                            mod_transpose(pair - 1)
                    for j in range(11):
                        at = P * (j % 2)
                        hi, lo = need_split(SPLIT[j // 2])
                        if j >= 4:
                            pe.wait_ge(*after("u_own", j - 4))
                        if j < 4:
                            if j == 0:
                                pe.wait_ge(*after("vec"))
                                for k, b in FIRST_BLOCKS:
                                    mm = first_block(R_AT[0], "n1", k, b)
                                    if k == KC - 1:
                                        mm.then_inc(*made("in_mm", b))
                            continue
                        for k in range(KC):
                            mm = passes(PS[:, j % 4, 0:TOK], (hi[:, k, at:at + P], lo[:, k, at:at + P]), (h_hi[:, k, :], h_lo[:, k, :]),
                                        k == 0, k == KC - 1)
                        mm.then_inc(*made("in_mm", j))
                    for n in range(18):
                        at, wd, t = tok_job(n)
                        s = S_GD if n < 3 else S_T + (n - 3) // 3
                        hi, lo = need_split(s)
                        q = 11 + n - 4
                        if q < 11:
                            pe.wait_ge(*after("u_own", q))
                        else:
                            o = q - 11
                            pe.wait_ge(*after("tok_dve" if o % 2 else "tok_act", o if o < 14 else 14))
                        a0 = 64 if n < 3 else 0
                        ts = slice(t * P, (t + 1) * P)
                        for k in range(KC):
                            mm = passes(PS[:, (11 + n) % 4, 0:wd], (h_hi[:, k, ts], h_lo[:, k, ts]), (hi[:, k, a0:a0 + wd], lo[:, k, a0:a0 + wd]),
                                        k == 0, k == KC - 1)
                        mm.then_inc(*made("in_mm", 11 + n))
                        if n == 5:
                            for c in range(HC):
                                pe.wait_ge(*after("kk_sq", c))
                                T.matmul(PS[:, 4 + c, 0:TOK], bones, (LW, EI, EX)[c][0][:, :], start=True, stop=True).then_inc(*made("kk_ss", c))
                    def low_rank(c, d):
                        cs = slice(c * P, (c + 1) * P)
                        r = slice(32 * d, 32 * d + 32)
                        T.matmul(PS[:, 6, 0:TOK], lora[r, cs], tanh2[r, 0, :], start=True, stop=True)
                        r = slice(64 + 32 * d, 96 + 32 * d)
                        T.matmul(PS[:, 7, 0:TOK], lora[r, cs], uT[r, 9, :], start=True, stop=True).then_inc(*made("lora_mm", (c, d)))

                    pe.wait_ge(*after("shifted", 10))
                    pe.wait_ge(*after("kk_sqrt", 2))
                    for c in range(HC):
                        if c == 1:
                            pe.wait_ge(*after("vec"))
                        for t in range(TILES):
                            mm = T.transpose(PS[:, 4 + c, t * P:(t + 1) * P], uT[:, 6 + c, t * P:(t + 1) * P], ident)
                        mm.then_inc(*made("v_tr", c))
                    pe.wait_ge(*after("state_loaded", 1))
                    for d in range(2):
                        for c in range(HC):
                            mm = T.transpose(PS[:, 7, (3 * d + c) * HD:(3 * d + c + 1) * HD], sin_rows[:, d, c * P:(c + 1) * P], ident[0:HD, 0:HD])
                    mm.then_inc(*made("s0_tr"))
                    pe.wait_ge(*after("lora_loaded", 2))
                    pe.wait_ge(*after("wd_tanh"))
                    pe.wait_ge(*after("S0T"))
                    low_rank(0, 0)
                    pe.wait_ge(*after("rope", 1))
                    pe.wait_ge(*after("tok_dve", 14))
                    pe.wait_ge(*after("tok_act", 14))
                    pe.wait_ge(*after("S0T"))
                    pe.wait_ge(*after("ctx_loaded", 1))
                    for c in range(HC):
                        cs = slice(c * P, (c + 1) * P)
                        ks = slice(DR + c * P, DR + (c + 1) * P)
                        for t in range(TILES):
                            src = tok[:, t, cs]
                            mm = T.transpose(PS[:, 2 * c, t * P:(t + 1) * P], src, ident)
                        mm.then_inc(*made("q_tr", c))
                        for t in range(4):
                            src = (tok[:, 0, ks], ctxk[:, cs], tok[:, 1, ks], tok[:, 2, ks])[t]
                            mm = T.transpose(PS[:, 2 * c + 1, t * P:(t + 1) * P], src, ident)
                        mm.then_inc(*made("k_tr", c))
                    pe.wait_ge(*after("a_tanh", (0, 0)))
                    low_rank(0, 1)

                    def scores(i):
                        t, h = divmod(i, HEADS)
                        k0, k1 = (0, P) if t == 0 else (P, 512)
                        if i < 2:
                            pe.wait_ge(*after("qT", 2))
                            pe.wait_ge(*after("kT", 2))
                        else:
                            pe.wait_ge(*after("exp", (i - 2, 1)))
                        for m in range(2):
                            c, r = divmod(2 * h + m, 4)
                            rows = slice(32 * r, 32 * r + 32)
                            mm = T.matmul(PS[:, 2 * (i % 2) + m, 0:k1 - k0], qT[rows, c, t * P:(t + 1) * P], kT[rows, c, k0:k1],
                                          start=True, stop=True)
                        mm.then_inc(*made("scores", i))

                    def p_transpose(i):
                        pe.wait_ge(*after("pdiff", i))
                        if i >= 2:
                            pe.wait_ge(*after("pdT", i - 2))
                        for kt in range(1 if i < HEADS else 3):
                            mm = T.transpose(PS[:, 4 + i % 2, kt * P:(kt + 1) * P], pdiff[:, i % 2, kt * P:(kt + 1) * P], ident)
                        mm.then_inc(*made("p_tr", i))

                    def values(i):
                        t, h = divmod(i, HEADS)
                        pe.wait_ge(*after("pdT", i))
                        if i == 0:
                            pe.wait_ge(*after("a_tanh", (0, 1)))
                        if t == 2 and h == 0:
                            pe.wait_ge(*after("o", 0))
                        vs = slice(768 + h * HD, 768 + (h + 1) * HD)
                        vals = [tok[:, 0, vs]] if t == 0 else [ctxv[:, h * HD:(h + 1) * HD], tok[:, 1, vs], tok[:, 2, vs]]
                        for kt, v in enumerate(vals):
                            mm = T.matmul(PS[:, 6 + t % 2, h * HD:(h + 1) * HD], pdT[:, i % 2, kt * P:(kt + 1) * P], v,
                                          start=(kt == 0), stop=(kt == len(vals) - 1))
                        mm.then_inc(*made("pv", i))

                    for i in range(18 + 3):
                        if i < 18:
                            scores(i)
                        if 2 <= i < 18 + 2:
                            p_transpose(i - 2)
                        if i >= 3:
                            values(i - 3)
                    pe.wait_ge(*after("gd_sig"))
                    pe.wait_ge(*after("exp", (17, 1)))
                    for c in range(HC):
                        T.matmul(PS[:, c, 0:TOK], gup[:, c * P:(c + 1) * P], tanh2[0:64, 1, :], start=True, stop=True).then_inc(*made("gate_mm", c))
                    pe.wait_ge(*after("o", 2))
                    pe.wait_ge(*after("pdT", 17))
                    for dc in range(2):
                        fs = slice(FNET0 + dc * P, FNET0 + (dc + 1) * P)
                        T.matmul(PS[:, 4 + 2 * dc, 0:256], tok[:, 0, fs], dft_prompt, start=True, stop=True)
                        for t in range(2):
                            mm = T.matmul(PS[:, 5 + 2 * dc, :], tok[:, 1 + t, fs], dft_sample[:, t, :], start=(t == 0), stop=(t == 1))
                        mm.then_inc(*made("fz_mm", dc))
                    for dc in range(2):
                        pe.wait_ge(*after("fz", (dc, 1)))
                        if dc:
                            pe.wait_ge(*after("gate", 0))
                        for m in range(2):
                            T.matmul(PS[:, (3, 0)[dc], 0:SEQ], dft_dim[:, m, :], fz[:, dc, m * SEQ:(m + 1) * SEQ], start=(m == 0), stop=(m == 1))
                        for m in range(2):
                            mm = T.matmul(PS[:, (3, 0)[dc], SEQ:TOK], dft_dim[:, m, :], fz[:, dc, 256 + m * DEC:256 + (m + 1) * DEC], start=(m == 0), stop=(m == 1))
                        mm.then_inc(*made("fnet_mm", dc))
                    for t in range(TILES):
                        pe.wait_ge(*after("o_n", t))
                        pe.wait_ge(*(after("fz", (0, 1)) if t == 2 else after("gate", t + 1)))
                        for c in range(HC):
                            mm = T.transpose(PS[:, (1, 2, 4)[t], c * P:(c + 1) * P], osb[:, t, c * P:(c + 1) * P], ident)
                        mm.then_inc(*made("o_tr", t))
                    def gn_mean(c):
                        pe.wait_ge(*after("y_raw", c))
                        T.matmul(PS[:, gn_places(c)[0], 0:TOK], bones, yT[:, c, :], start=True, stop=True).then_inc(*made("gn_mean_mm", c))

                    def gn_var(c):
                        _, bank, squares, _ = gn_places(c)
                        pe.wait_ge(*after("gn_sq", c))
                        T.matmul(PS[:, bank, 0:TOK], bones, squares, start=True, stop=True).then_inc(*made("gn_var_mm", c))

                    for c in range(HC):
                        cs = slice(c * P, (c + 1) * P)
                        pe.wait_ge(*after("k_scaled", (c, 1)))
                        if c == 0:
                            pe.wait_ge(*after("y_attn", 2))
                        if c >= 1:
                            pe.wait_ge(*after("XT", (c - 1, 6, 2)))
                            pe.wait_ge(*after("stmp", (c - 1, 1)))
                        for i, src in enumerate((KT, BT)):
                            for d in range(2):
                                for g in range(2):
                                    t = STEP_TILE[g][d]
                                    mm = T.transpose(PS[:, 2 + i, (2 * d + g) * P:(2 * d + g + 1) * P], src[:, d, t * P:(t + 1) * P], ident)
                        mm.then_inc(*made("kt_tr", c))
                        pe.wait_ge(*after("bonus_r", c))
                        if c == 0:
                            pe.wait_ge(*after("fz", (1, 1)))
                        else:
                            pe.wait_ge(*after("stmp", (c - 1, 1)))
                        T.matmul(PS[:, 4, 0:TOK], bones, gsum[:, :], start=True, stop=True).then_inc(*made("bonus_mm", c))
                        pe.wait_ge(*after("r", (c, 1)))
                        pe.wait_ge(*after("kap", (c, 1)))
                        for g in range(3):
                            for n, rhs in enumerate((KAP[c % 2], RT[c % 2])):
                                if g:
                                    pe.wait_ge(*after("A", (c, g - 1, n)))
                                elif n == 0:
                                    pe.wait_ge(*(after("mod_sum", MOD_PAIRS_SOLVE[c - 1][-1]) if c else after("y_fnet", 1)))
                                else:
                                    pe.wait_ge(*after("fz", (1, 1)) if c == 0 else after("y_raw", c - 1))
                                for i, lhs in enumerate((BT, KT)):
                                    for d in range(2):
                                        t = STEP_TILE[g][d]
                                        ts = slice(t * P, (t + 1) * P)
                                        for h in range(2):
                                            hs = slice(h * HD, (h + 1) * HD)
                                            mm = T.matmul(PS[:, abank(2 * g + n, h), (2 * i + d) * P:(2 * i + d + 1) * P],
                                                          lhs[hs, d, ts], rhs[hs, d, ts], start=True, stop=True)
                                mm.then_inc(*made("A_mm", (c, g, n)))
                        pe.wait_ge(*after("A", (c, 2, 1)))
                        pe.wait_ge(*after("btok", c))
                        pe.wait_ge(*after("bonus", c))
                        for j in range(LEVELS):
                            def join(j, g):
                                if j == 0:
                                    pe.wait_ge(*after("A1", (c, g)))
                                    pe.wait_ge(*after("V", (c, 0, g - 2)) if g == 2 else after("A", (c, 2, 1)))
                                else:
                                    pe.wait_ge(*after("V", (c, 0, g)) if j == 1 else after("X", (c, j - 1, g)))
                                    pj, pg = divmod(3 * j + g - 2, 3)
                                    pe.wait_ge(*after("V", (c, pj, pg)))
                                for u in range(4):
                                    mm = T.matmul(PS[:, vbank(j, g), u * P:(u + 1) * P], AKB[:, g, u, :], ident if j == 0 else X[:, g, u, :],
                                                  start=True, stop=True)
                                mm.then_inc(*made("V_mm", (c, j, g)))

                            def merge(j, g):
                                pe.wait_ge(*after("V", (c, j, g)))
                                if j == 1:
                                    pe.wait_ge(*after("XT0", (c, g, 1)))
                                else:
                                    pe.wait_ge(*after("XT", (c, j - 1, g)))
                                if 3 * j + g - 2 >= 3:
                                    pj, pg = divmod(3 * j + g - 2, 3)
                                    pe.wait_ge(*after("XT", (c, pj, pg)))
                                b = xbank(j, g)
                                if j < LEVELS - 1:
                                    for u in range(4):
                                        mm = T.matmul(PS[:, b, u * P:(u + 1) * P], XT[:, g, u, :], VB[:, g, u, :], start=True, stop=True)
                                    mm.then_inc(*made("X_mm", (c, j, g)))
                                for u in range(4):
                                    mm = T.matmul(PS[:, b + 1, u * P:(u + 1) * P], VB[:, g, u, :], XT[:, g, u, :], start=True, stop=True)
                                mm.then_inc(*made("XT_mm", (c, j, g)))

                            if c + 1 < HC and j in (1, 2):
                                if j == 2:
                                    pe.wait_ge(*after("a_tanh", (c + 1, 0)))
                                low_rank(c + 1, j - 1)
                            if c == HC - 1 and j == 1:
                                gn_mean(0)
                                gn_mean(1)
                            if c == HC - 1 and j == 3:
                                gn_var(0)
                                gn_var(1)
                            for g in range(3):
                                join(j, g)
                                if j >= 1 and g >= 1:
                                    merge(j, g - 1)
                            if j >= 1:
                                merge(j, 2)
                        pe.wait_ge(*after("XT", (c, LEVELS - 1, 2)))
                        for g in range(3):
                            if g == 0:
                                pe.wait_ge(*after("A", (c, 2, 1)))
                                if c == HC - 1:
                                    pe.wait_ge(*after("gn_sqrt", 1))
                            else:
                                pe.wait_ge(*after("Z", (c, g - 1)))
                                pe.wait_ge(*after("SH", (c, g, 1)))
                            for d in range(2):
                                t = STEP_TILE[g][d]
                                for h in range(2):
                                    hs = slice(h * HD, (h + 1) * HD)
                                    u = 2 * d + h
                                    o = PS[:, (6, 4)[h], d * HD:(d + 1) * HD]
                                    if g:
                                        T.matmul(o, KAP[c % 2][hs, d, t * P:(t + 1) * P], SH[hs, g, d, :], start=True, stop=False)
                                    mm = T.matmul(o, AKV[:, g, u, :], vtok[:, t, c * P + h * HD:c * P + (h + 1) * HD], start=(g == 0), stop=True)
                            mm.then_inc(*made("Z_mm", (c, g)))
                            pairs = MOD_PAIRS_SOLVE[c]
                            if g < len(pairs):
                                mod_products(2 * pairs[g])
                            if 1 <= g <= len(pairs):
                                mod_transpose(pairs[g - 1])
                            pe.wait_ge(*after("Z", (c, g)))
                            if g:
                                pe.wait_ge(*after("U", (c, g - 1)))
                            for u in range(4):
                                mm = T.matmul(PS[:, 7, u * HD:(u + 1) * HD], XT[:, g, u, :], zs[:, u * HD:(u + 1) * HD], start=True, stop=True)
                            mm.then_inc(*made("U_mm", (c, g)))
                            if g < len(pairs):
                                mod_products(2 * pairs[g] + 1)
                            pe.wait_ge(*after("U", (c, g)))
                            if g == 1:
                                pe.wait_ge(*after("Sfin", (c, 1)))
                            if g < 2:
                                for d in range(2):
                                    t = STEP_TILE[g][d]
                                    for h in range(2):
                                        hs = slice(h * HD, (h + 1) * HD)
                                        u = 2 * d + h
                                        o = PS[hs, 3, d * HD:(d + 1) * HD]
                                        T.matmul(o, ktok[:, d, g, hs], vtok[:, t, c * P + h * HD:c * P + (h + 1) * HD], start=True, stop=False)
                                        mm = T.matmul(o, btok[:, d, g, hs], usb[:, g, u * HD:(u + 1) * HD], start=False, stop=True)
                                mm.then_inc(*made("S_mm", (c, g)))
                        for h in range(2):
                            hs = slice(h * HD, (h + 1) * HD)
                            for t in range(TILES):
                                ts = slice(t * P, (t + 1) * P)
                                ops = []
                                for d in range(2):
                                    g = [st[d] for st in STEP_TILE].index(t)
                                    u = 2 * d + h
                                    if g:
                                        ops.append((SH[hs, g, d, :], RT[c % 2][hs, d, ts]))
                                    ops.append((vtok[:, t, c * P + h * HD:c * P + (h + 1) * HD], ARV[:, g, u, :]))
                                    ops.append((usb[:, g, u * HD:(u + 1) * HD], ARB[:, g, u, :]))
                                for i, (lhs, rhs) in enumerate(ops):
                                    mm = T.matmul(PS[hs, 5 + h, ts], lhs, rhs, start=(i == 0), stop=(i == len(ops) - 1))
                        mm.then_inc(*made("Y_mm", c))
                        if len(pairs) == 3:
                            mod_transpose(pairs[2])
                    pe.wait_ge(*after("Sfin", (2, 1)))
                    pe.wait_ge(*after("U", (2, 2)))
                    pe.wait_ge(*after("y_raw", 2))
                    for d in range(2):
                        for c in range(HC):
                            mm = T.transpose(PS[0:HD, 6 + d, c * P:(c + 1) * P], Sfin[:, c, d, :], ident)
                        mm.then_inc(*made("st_tr", d))
                    pe.wait_ge(*after("V", (2, 6, 2)))
                    pe.wait_ge(*after("mod_sum", MOD_PAIRS_SOLVE[2][-1]))
                    gn_mean(HC - 1)
                    gn_var(HC - 1)
                    def out_products(m, ks, first, last):
                        hi, lo = need_split(S_OUT + m // 2)
                        ms = slice((m % 2) * P, (m % 2 + 1) * P)
                        for k in ks:
                            if m == 0:
                                pe.wait_ge(*after("y_lo", k))
                            mm = passes(PS[:, m % 4, 0:TOK], (hi[:, k, ms], lo[:, k, ms]), (y_hi[:, k, :], y_lo[:, k, :]),
                                        k == first, k == last)
                        return mm

                    pe.wait_ge(*after("gn_d", HC - 1))
                    for m in range(4):
                        out_products(m, range(HC, KC), HC, None)
                    for m in range(4):
                        out_products(m, range(HC), None, HC - 1).then_inc(*made("out_mm", m))
                    for m in range(4, KC):
                        pe.wait_ge(*after("x1", (m - 4, 1)))
                        out_products(m, range(KC), 0, KC - 1).then_inc(*made("out_mm", m))
                    pe.wait_ge(*after("state_rows", 1))
                    norm_pe(pe, "n2")
                    for s in range(S_FFN, SLOTS):
                        half, i = divmod(s - S_FFN, FFN_SLOTS)
                        if i < HALF:
                            f = half * HALF + i
                            hi, lo = need_split(s)
                            if f < 2:
                                if f == 0:
                                    for k, b in FIRST_BLOCKS:
                                        mm = first_block(s, "n2", k, b)
                                        if k == KC - 1 and b % 2:
                                            mm.then_inc(*made("ff_mm", b // 2))
                                continue
                            if f >= 2:
                                pe.wait_ge(*after("ff", f - 2))
                            if f == HALF:
                                pe.wait_ge(*after("x2", (0, 0, 3, 1)))
                            for b in range(2):
                                bs = slice(b * P, (b + 1) * P)
                                for k in range(KC):
                                    mm = passes(PS[:, ff_bank(f) + b, 0:TOK], (hi[:, k, bs], lo[:, k, bs]), (h_hi[:, k, :], h_lo[:, k, :]),
                                                k == 0, k == KC - 1)
                            mm.then_inc(*made("ff_mm", f))
                            continue
                        hi, lo = need_split(s, 4)
                        for u in range(4 * (i - HALF), min(4 * (i - HALF) + 4, 2 * HALF)):
                            oh, k = divmod(u, HALF)
                            if oh == 0:
                                pe.wait_ge(*after("ff_lo", half * HALF + k))
                            if half == 1 and u == 0:
                                pe.wait_ge(*after("x2", (0, 1, 3, 1)))
                            for m in range(4):
                                ms = slice(m * P, (m + 1) * P)
                                mm = passes(PS[:, fo_bank(half, oh) + m, 0:TOK], (hi[:, u % 4, ms], lo[:, u % 4, ms]), (ff_hi[:, k, :], ff_lo[:, k, :]),
                                            k == 0, k == HALF - 1)
                            if u == HALF - 1:
                                mm.then_inc(*made("ffo_half", half))
                        mm.then_inc(*made("ffo_mm", s))

            reset([sems[n] for n in sems if n not in prologue_names])

        with nc.Block() as block:
            @block.scalar
            def _(act):
                norm_squares(act, "n3")
                norm_root(act, "n3")

            @block.tensor
            def _(pe):
                norm_pe(pe, "n3")
                for t in range(TILES):
                    for half in range(2):
                        b = (2 * t + half) % 4
                        if 2 * t + half >= 4:
                            pe.wait_ge(*after("y_rows", 2 * t + half - 4))
                        for k in range(4):
                            kk_ = 4 * half + k
                            if t == 0:
                                pe.wait_ge(*after("n3_h", kk_))
                            mm = nc.tensor.transpose(PS[:, b, k * P:(k + 1) * P], yT[:, kk_, t * P:(t + 1) * P], ident)
                        mm.then_inc(*made("y_tr", 2 * t + half))

            @block.vector
            def _(dve):
                dve.wait_ge(*after("n3_sqrt"))
                nc.vector.reciprocal(rstd[:, :], rstd[:, :]).then_inc(*made("n3_rstd"))
                dve.wait_ge(*after("n3_rstd"))
                for k in range(KC):
                    nc.vector.scalar_tensor_tensor(yT[:, k, :], xT[:, k, :], fing[:, k:k + 1], rstd[:, :], ALU.mult,
                                                   ALU.mult).then_inc(*made("n3_h", k))
                for i in range(6):
                    dve.wait_ge(*after("y_tr", i))
                    if i == 0:
                        dve.wait_ge(*after("n3_ss"))
                    nc.vector.tensor_copy(xin[:, i // 2, (i % 2) * 512:(i % 2) * 512 + 512], PS[:, i % 4, :]).then_inc(*made("y_rows", i))

            @block.sync
            def _(sp):
                sp.wait_ge(*after("y_rows", 1))
                sp.dma_start(a["out_p"][0], xin[:, 0, :]).then_inc(*loaded("y_stored"))
                for t in range(1, TILES):
                    sp.wait_ge(*after("y_rows", 2 * t + 1))
                    sp.dma_start(a["out_x"][0, (t - 1) * P:t * P, :], xin[:, t, :]).then_inc(*loaded("y_stored", t))
                sp.wait_ge(*after("y_stored", 2))


def kernel(**inputs):
    import numpy as _np
    import concourse.bacc as _bacc
    from concourse.bass_utils import run_bass_kernel_spmd as _run

    lay = {
        "x_prompt": None, "x_sample": None, "c": None, "c_ctx": None, "norm1_g": None, "norm2_g": None,
        "final_norm_g": None, "w_mod": None, "b_mod": None, "w_in": None, "w_out": None, "shift_mu": None,
        "decay_w0": None, "decay_up": None, "iclr_a0": None, "iclr_up": None, "gate_up": None, "k_k": None,
        "k_a": None, "r_k": None, "lnx_g": None, "lnx_b": None, "diff_lambda": None, "subln_g": None,
        "w_ffn_in": None, "w_ffn_out": None,
        "state": ("state_rwkv", (DEPTH, 2, HEADS, HD, HD)),
        "cache_k": ("cache_diff_k", (DEPTH, P, DR)),
        "cache_v": ("cache_diff_v", (DEPTH, P, DR)),
    }
    arrays = {}
    for name, how in lay.items():
        v = _np.ascontiguousarray(inputs[how[0] if how else name])
        arrays[name] = v.reshape(how[1]) if how else v
    arrays["tables"] = packed_tables()
    arrays["lam_init"] = lam_table()
    outs = {"out_p": (1, SEQ, D), "out_x": (1, DEC, D), "out_s": (DEPTH, 2, HEADS, HD, HD),
            "out_k": (DEPTH, SEQ, DR), "out_v": (DEPTH, SEQ, DR)}
    counts = {}
    for _ in range(2):
        nc = _bacc.Bacc("TRN2", target_bir_lowering=False, num_devices=1, dynamic_dma_scratch_size=1024)
        a = {n: nc.dram_tensor("in_" + n, v.shape, F32, kind="ExternalInput").ap() for n, v in arrays.items()}
        a.update({n: nc.dram_tensor(n, s, F32, kind="ExternalOutput").ap() for n, s in outs.items()})
        build(nc, a, counts)
    r = _run(nc, [{"in_" + n: v for n, v in arrays.items()}], core_ids=[0]).results[0]
    return (r["out_p"], r["out_x"], r["out_s"].reshape(1, DEPTH, 2, HEADS, HD, HD),
            r["out_k"].reshape(1, DEPTH, SEQ, HEADS, 2, DQK), r["out_v"].reshape(1, DEPTH, SEQ, HEADS, HD))
```
